# Optimizing a Trainium2 kernel written in Bass

```python
import math
import jax, jax.numpy as jnp
from jax import lax
import numpy as np

D_MODEL = 1024
BATCH = 1
SEQ = 1024
DEPTH = 2

D_MIX = D_MODEL
DN_HEADS = 4
DN_DK = 128
DN_DV = 128
DN_CONV = 4
DN_CHUNK = 64
DN_WIDTH = DN_HEADS * DN_DV
DN_KEY_WIDTH = DN_HEADS * DN_DK
GLA_HEADS = 4
GLA_DK = 64
GLA_DV = 128
GLA_GATE_RANK = 16
GLA_TAU = 16.0
GLA_CHUNK = 16
GLA_WIDTH = GLA_HEADS * GLA_DV
GLA_KEY_WIDTH = GLA_HEADS * GLA_DK
IN_SIZES = (DN_KEY_WIDTH, DN_KEY_WIDTH, DN_WIDTH,
            DN_WIDTH,
            DN_HEADS, DN_HEADS,
            GLA_KEY_WIDTH, GLA_KEY_WIDTH, GLA_WIDTH,
            GLA_WIDTH,
            GLA_GATE_RANK)
D_IN_PROJ = 3 * 512 + 512 + 4 + 4 + 256 + 256 + 512 + 512 + 16
DEEPNORM_ALPHA = (2.0 * DEPTH) ** 0.25
DEEPNORM_BETA = (8.0 * DEPTH) ** -0.25
NORM_EPS = 1e-6


def _split(a, sizes):
    out, off = [], 0
    for s in sizes:
        out.append(a[..., off:off + s])
        off += s
    return out

def _to_chunks(a, chunk):
    b, t = a.shape[:2]
    a = a.reshape((b, t // chunk, chunk) + a.shape[2:])
    return jnp.moveaxis(a, 3, 1)

def _from_scan(o):
    n, b, h, c, d = o.shape
    return jnp.transpose(o, (1, 0, 3, 2, 4)).reshape(b, n * c, h, d)

def causal_short_conv(x, w):
    k, c = w.shape
    return lax.conv_general_dilated(
        x, w[:, None, :].astype(x.dtype), window_strides=(1,),
        padding=[(k - 1, 0)], dimension_numbers=("NWC", "WIO", "NWC"),
        feature_group_count=c)

def l2norm(x):
    xf = x.astype(jnp.float32)
    return xf * lax.rsqrt(jnp.sum(xf * xf, axis=-1, keepdims=True) + NORM_EPS)

def head_rms_norm(o, g):
    of = o.astype(jnp.float32)
    of = of * lax.rsqrt(jnp.mean(of * of, axis=-1, keepdims=True) + NORM_EPS)
    return of * g.astype(jnp.float32)

def layer_norm(x, g, b):
    xf = x.astype(jnp.float32)
    mu = jnp.mean(xf, axis=-1, keepdims=True)
    var = jnp.mean(jnp.square(xf - mu), axis=-1, keepdims=True)
    y = (xf - mu) * lax.rsqrt(var + NORM_EPS) * g.astype(jnp.float32) + b.astype(jnp.float32)
    return y.astype(x.dtype)

def gated_delta_rule_chunked(q, k, v, g, beta):
    f32 = jnp.float32
    q, k, v, g, beta = (a.astype(f32) for a in (q, k, v, g, beta))
    b_, t, h, dk = q.shape
    dv = v.shape[-1]
    c = DN_CHUNK
    qc, kc, vc = (_to_chunks(a, c) for a in (q, k, v))
    gc, bc = _to_chunks(g, c), _to_chunks(beta, c)
    G = jnp.cumsum(gc, axis=-1)
    pos = jnp.arange(c)
    causal = pos[:, None] >= pos[None, :]
    strict = pos[:, None] > pos[None, :]
    diff = G[..., :, None] - G[..., None, :]
    decay = jnp.where(causal, jnp.exp(jnp.where(causal, diff, 0.0)), 0.0)
    k_beta = kc * bc[..., None]
    kk = jnp.einsum("bhnid,bhnjd->bhnij", k_beta, kc)
    lower = jnp.eye(c, dtype=f32) + jnp.where(strict, kk * decay, 0.0)
    rhs = jnp.concatenate([vc * bc[..., None], k_beta * jnp.exp(G)[..., None]], axis=-1)
    uw = lax.linalg.triangular_solve(lower, rhs, left_side=True, lower=True)
    u, w = uw[..., :dv], uw[..., dv:]
    attn = jnp.einsum("bhnid,bhnjd->bhnij", qc, kc) * decay
    xs = tuple(jnp.moveaxis(a, 2, 0) for a in (qc, kc, u, w, G, attn))
    s0 = jnp.zeros((b_, h, dk, dv), f32)

    def step(S, inp):
        q_n, k_n, u_n, w_n, g_n, a_n = inp
        v_new = u_n - jnp.einsum("bhid,bhde->bhie", w_n, S)
        o_n = (jnp.einsum("bhid,bhde->bhie", q_n * jnp.exp(g_n)[..., None], S)
               + jnp.einsum("bhij,bhje->bhie", a_n, v_new))
        g_last = g_n[..., -1]
        k_dec = k_n * jnp.exp(g_last[..., None] - g_n)[..., None]
        S = S * jnp.exp(g_last)[..., None, None] + jnp.einsum("bhid,bhie->bhde", k_dec, v_new)
        return S, o_n

    _, o = lax.scan(step, s0, xs)
    return _from_scan(o)

def gla_chunked(q, k, v, gk):
    f32 = jnp.float32
    q, k, v, gk = (a.astype(f32) for a in (q, k, v, gk))
    b_, t, h, dk = q.shape
    dv = v.shape[-1]
    c = GLA_CHUNK
    qc, kc, vc, gc = (_to_chunks(a, c) for a in (q, k, v, gk))
    Bc = jnp.cumsum(gc, axis=-2)
    pos = jnp.arange(c)
    causal = (pos[:, None] >= pos[None, :])[..., None]
    diff = Bc[..., :, None, :] - Bc[..., None, :, :]
    dec = jnp.where(causal, jnp.exp(jnp.where(causal, diff, 0.0)), 0.0)
    attn = jnp.einsum("bhnid,bhnjd,bhnijd->bhnij", qc, kc, dec)
    xs = tuple(jnp.moveaxis(a, 2, 0) for a in (qc, kc, vc, Bc, attn))
    s0 = jnp.zeros((b_, h, dk, dv), f32)

    def step(S, inp):
        q_n, k_n, v_n, b_n, a_n = inp
        o_n = (jnp.einsum("bhid,bhde->bhie", q_n * jnp.exp(b_n), S)
               + jnp.einsum("bhij,bhje->bhie", a_n, v_n))
        b_last = b_n[..., -1:, :]
        k_dec = k_n * jnp.exp(b_last - b_n)
        S = S * jnp.exp(b_last[..., 0, :])[..., None] + jnp.einsum("bhid,bhie->bhde", k_dec, v_n)
        return S, o_n

    _, o = lax.scan(step, s0, xs)
    return _from_scan(o)

def hybrid_layer(x, w_in, conv_w, dn_a_log, dn_dt_bias, gla_gate_w2, gla_gate_b,
                 dn_norm_g, gla_norm_g, w_out, ln_g, ln_b):
    bsz, t, _ = x.shape
    proj = jnp.einsum("btd,de->bte", x, w_in)
    (dn_q, dn_k, dn_v, dn_z, dn_b, dn_a,
     g_q, g_k, g_v, g_z, g_r) = _split(proj, IN_SIZES)

    dn_qkv = jax.nn.silu(causal_short_conv(jnp.concatenate([dn_q, dn_k, dn_v], axis=-1), conv_w))
    cq, ck, cv = _split(dn_qkv, (DN_KEY_WIDTH, DN_KEY_WIDTH, DN_WIDTH))
    q = l2norm(cq.reshape(bsz, t, DN_HEADS, DN_DK)) * (DN_DK ** -0.5)
    k = l2norm(ck.reshape(bsz, t, DN_HEADS, DN_DK))
    v = cv.reshape(bsz, t, DN_HEADS, DN_DV)
    beta = jax.nn.sigmoid(dn_b.astype(jnp.float32))
    g = -jnp.exp(dn_a_log.astype(jnp.float32)) * jax.nn.softplus(
        dn_a.astype(jnp.float32) + dn_dt_bias.astype(jnp.float32))
    o_dn = gated_delta_rule_chunked(q, k, v, g, beta)
    o_dn = head_rms_norm(o_dn, dn_norm_g) * jax.nn.silu(
        dn_z.reshape(bsz, t, DN_HEADS, DN_DV).astype(jnp.float32))

    gq = g_q.reshape(bsz, t, GLA_HEADS, GLA_DK) * (GLA_DK ** -0.5)
    gk = g_k.reshape(bsz, t, GLA_HEADS, GLA_DK)
    gv = g_v.reshape(bsz, t, GLA_HEADS, GLA_DV)
    gate_logits = jnp.einsum("btr,re->bte", g_r, gla_gate_w2) + gla_gate_b
    log_f = (jax.nn.log_sigmoid(gate_logits.astype(jnp.float32)) / GLA_TAU).reshape(
        bsz, t, GLA_HEADS, GLA_DK)
    o_gla = gla_chunked(gq, gk, gv, log_f)
    o_gla = head_rms_norm(o_gla, gla_norm_g) * jax.nn.silu(
        g_z.reshape(bsz, t, GLA_HEADS, GLA_DV).astype(jnp.float32))

    o = jnp.concatenate([o_dn.reshape(bsz, t, DN_WIDTH),
                         o_gla.reshape(bsz, t, GLA_WIDTH)], axis=-1).astype(x.dtype)
    y = jnp.einsum("bte,ed->btd", o, w_out)
    return layer_norm(DEEPNORM_ALPHA * x + y, ln_g, ln_b)

def first_inputs(seed: int = 0) -> dict:
    key = jax.random.key(seed)
    ks = jax.random.split(key, 12)
    f32 = jnp.float32
    x = jax.random.normal(ks[0], (BATCH, SEQ, D_MODEL), f32)
    col_scale = jnp.concatenate([
        jnp.ones((2 * DN_KEY_WIDTH,), f32),
        jnp.full((DN_WIDTH,), DEEPNORM_BETA, f32),
        jnp.ones((DN_WIDTH + 2 * DN_HEADS + 2 * GLA_KEY_WIDTH,), f32),
        jnp.full((GLA_WIDTH,), DEEPNORM_BETA, f32),
        jnp.ones((GLA_WIDTH + GLA_GATE_RANK,), f32)])
    w_in = jax.random.normal(ks[1], (DEPTH, D_MODEL, D_IN_PROJ), f32) * (D_MODEL ** -0.5) * col_scale
    conv_w = jax.random.normal(ks[2], (DEPTH, DN_CONV, DN_KEY_WIDTH * 2 + DN_WIDTH), f32) * (DN_CONV ** -0.5)
    dn_a_log = jnp.log(jax.random.uniform(ks[3], (DEPTH, DN_HEADS), f32, 1.0, 16.0))
    dt = jnp.exp(jax.random.uniform(ks[4], (DEPTH, DN_HEADS), f32, math.log(1e-3), math.log(1e-1)))
    dn_dt_bias = dt + jnp.log(-jnp.expm1(-dt))
    gla_gate_w2 = jax.random.normal(ks[5], (DEPTH, GLA_GATE_RANK, GLA_KEY_WIDTH), f32) * (GLA_GATE_RANK ** -0.5)
    gla_gate_b = 0.1 * jax.random.normal(ks[6], (DEPTH, GLA_KEY_WIDTH), f32)
    dn_norm_g = 1.0 + 0.02 * jax.random.normal(ks[7], (DEPTH, DN_DV), f32)
    gla_norm_g = 1.0 + 0.02 * jax.random.normal(ks[8], (DEPTH, GLA_DV), f32)
    w_out = jax.random.normal(ks[9], (DEPTH, D_MIX, D_MODEL), f32) * (D_MIX ** -0.5) * DEEPNORM_BETA
    ln_g = 1.0 + 0.02 * jax.random.normal(ks[10], (DEPTH, D_MODEL), f32)
    ln_b = 0.02 * jax.random.normal(ks[11], (DEPTH, D_MODEL), f32)
    return {"x": x, "w_in": w_in, "conv_w": conv_w, "dn_a_log": dn_a_log,
            "dn_dt_bias": dn_dt_bias, "gla_gate_w2": gla_gate_w2, "gla_gate_b": gla_gate_b,
            "dn_norm_g": dn_norm_g, "gla_norm_g": gla_norm_g, "w_out": w_out,
            "ln_g": ln_g, "ln_b": ln_b}

def first_block(x, w_in, conv_w, dn_a_log, dn_dt_bias, gla_gate_w2, gla_gate_b,
              dn_norm_g, gla_norm_g, w_out, ln_g, ln_b):
    h = x
    for l in range(DEPTH):
        h = hybrid_layer(h, w_in[l], conv_w[l], dn_a_log[l], dn_dt_bias[l],
                         gla_gate_w2[l], gla_gate_b[l], dn_norm_g[l], gla_norm_g[l],
                         w_out[l], ln_g[l], ln_b[l])
    return h


GRID_W = 64
N_HEADS = 16
HEAD_DIM = D_MODEL // N_HEADS
NA_ROWS = 8
NA_COLS = 16
NA_QCOLS = NA_COLS
NA_KCOLS = 2 * NA_COLS
GQA_KV_HEADS = 4
GQA_GROUP = N_HEADS // GQA_KV_HEADS
Q_BLOCK = 128
ROPE_THETA = 10000.0
ROPE_PAIRS = HEAD_DIM // 4
N_GROUPS = 4
EXPERTS_PER_GROUP = 8
N_EXPERTS = N_GROUPS * EXPERTS_PER_GROUP
TOP_K = 2
D_EXPERT = D_MODEL // 2
MOE_BLOCK = 128
N_MIXERS = 2
N_NA_LAYERS = (DEPTH + 1) // 2
N_GQA_LAYERS = DEPTH // 2
DEEPNORM_ALPHA_2 = (2 * DEPTH) ** 0.25
DEEPNORM_BETA_2 = (8 * DEPTH) ** -0.25
ADA_INIT = 0.2
LN_EPS = 1e-5
RMS_EPS = 1e-6


def layer_norm_2(x, g, b):
    xf = x.astype(jnp.float32)
    mu = xf.mean(-1, keepdims=True)
    var = jnp.square(xf - mu).mean(-1, keepdims=True)
    return ((xf - mu) * lax.rsqrt(var + LN_EPS) * g.astype(jnp.float32) + b.astype(jnp.float32)).astype(x.dtype)

def rms_norm(x, g):
    xf = x.astype(jnp.float32)
    ms = jnp.square(xf).mean(-1, keepdims=True)
    return (xf * lax.rsqrt(ms + RMS_EPS) * g.astype(jnp.float32)).astype(x.dtype)

def neighbourhood_attention(q, k, v, rpb):
    B, S, H, hd = q.shape
    rows = S // GRID_W
    kr = min(NA_ROWS, rows)
    r = jnp.arange(rows, dtype=jnp.int32)
    row_start = jnp.clip(r - kr // 2, 0, rows - kr)
    key_rows = row_start[:, None] + jnp.arange(kr, dtype=jnp.int32)[None, :]
    dr = key_rows - r[:, None] + (NA_ROWS - 1)
    qg = q.reshape(B, rows, GRID_W, H, hd)
    kg = k.reshape(B, rows, GRID_W, H, hd)[:, key_rows]
    vg = v.reshape(B, rows, GRID_W, H, hd)[:, key_rows]
    outs = []
    for q0 in range(0, GRID_W, NA_QCOLS):
        b0 = min(max(q0 - NA_COLS // 2, 0), GRID_W - NA_KCOLS)
        qc = q0 + jnp.arange(NA_QCOLS, dtype=jnp.int32)
        kc = b0 + jnp.arange(NA_KCOLS, dtype=jnp.int32)
        win_start = jnp.clip(qc - NA_COLS // 2, 0, GRID_W - NA_COLS)
        valid = (kc[None, :] >= win_start[:, None]) & (kc[None, :] < win_start[:, None] + NA_COLS)
        dc = jnp.clip(kc[None, :] - qc[:, None] + NA_COLS - 1, 0, 2 * NA_COLS - 2)
        bias = rpb[:, dr[:, None, :, None], dc[None, :, None, :]]
        kb = kg[:, :, :, b0:b0 + NA_KCOLS]
        vb = vg[:, :, :, b0:b0 + NA_KCOLS]
        s = jnp.einsum('brqhd,brikhd->bhrqik', qg[:, :, q0:q0 + NA_QCOLS], kb).astype(jnp.float32)
        s = jnp.where(valid[:, None, :], s + bias.astype(jnp.float32), -jnp.inf)
        p = jax.nn.softmax(s.reshape(B, H, rows, NA_QCOLS, kr * NA_KCOLS), axis=-1)
        p = p.reshape(s.shape).astype(v.dtype)
        outs.append(jnp.einsum('bhrqik,brikhd->brqhd', p, vb))
    return jnp.concatenate(outs, axis=2).reshape(B, S, H, hd)

def neighbourhood_mixer(h, w_qkv, rpb, w_o):
    B, S, D = h.shape
    qkv = (h @ w_qkv).reshape(B, S, 3, N_HEADS, HEAD_DIM)
    q = qkv[:, :, 0] * (HEAD_DIM ** -0.5)
    o = neighbourhood_attention(q, qkv[:, :, 1], qkv[:, :, 2], rpb)
    return o.reshape(B, S, D) @ w_o

def axial_rope_tables(S):
    t = jnp.arange(S, dtype=jnp.int32)
    pos = jnp.stack([t // GRID_W, t % GRID_W], axis=-1).astype(jnp.float32)
    inv_freq = ROPE_THETA ** (-jnp.arange(ROPE_PAIRS, dtype=jnp.float32) / ROPE_PAIRS)
    ang = pos[:, :, None] * inv_freq
    return jnp.cos(ang), jnp.sin(ang)

def apply_axial_rope(x, cos, sin):
    B, S, H, hd = x.shape
    xr = x.astype(jnp.float32).reshape(B, S, H, 2, 2, ROPE_PAIRS)
    x1, x2 = xr[..., 0, :], xr[..., 1, :]
    c, s = cos[None, :, None], sin[None, :, None]
    out = jnp.stack([x1 * c - x2 * s, x2 * c + x1 * s], axis=-2)
    return out.reshape(B, S, H, hd).astype(x.dtype)

def block_gqa_attention(q, k, v):
    B, S, H, hd = q.shape
    nblk = S // Q_BLOCK
    qg = q.reshape(B, nblk, Q_BLOCK, GQA_KV_HEADS, GQA_GROUP, hd).transpose(1, 0, 2, 3, 4, 5)
    scale = HEAD_DIM ** -0.5

    def one_block(qb):
        s = jnp.einsum('bqkgd,bskd->bkgqs', qb, k).astype(jnp.float32) * scale
        p = jax.nn.softmax(s, axis=-1).astype(v.dtype)
        return jnp.einsum('bkgqs,bskd->bqkgd', p, v)

    o = lax.map(one_block, qg)
    return o.transpose(1, 0, 2, 3, 4, 5).reshape(B, S, H * hd)

def gqa_mixer(h, cos, sin, w_qkv, q_gain, k_gain, w_o):
    B, S, D = h.shape
    kvd = GQA_KV_HEADS * HEAD_DIM
    qkv = h @ w_qkv
    q = qkv[..., :D].reshape(B, S, N_HEADS, HEAD_DIM)
    k = qkv[..., D:D + kvd].reshape(B, S, GQA_KV_HEADS, HEAD_DIM)
    v = qkv[..., D + kvd:].reshape(B, S, GQA_KV_HEADS, HEAD_DIM)
    q = apply_axial_rope(rms_norm(q, q_gain), cos, sin)
    k = apply_axial_rope(rms_norm(k, k_gain), cos, sin)
    return block_gqa_attention(q, k, v) @ w_o

def hierarchical_moe(h, w_group, b_group, w_expert, b_expert, w_gate, w_up, w_down):
    B, S, D = h.shape
    N = B * S
    xt = h.reshape(N, D)
    pg = jax.nn.softmax((xt @ w_group).astype(jnp.float32) + b_group.astype(jnp.float32), axis=-1)
    g_prob, g_idx = lax.top_k(pg, 1)
    le = ((xt @ w_expert).astype(jnp.float32) + b_expert.astype(jnp.float32)).reshape(N, N_GROUPS, EXPERTS_PER_GROUP)
    le = le[jnp.arange(N), g_idx[:, 0]]
    e_prob, e_local = lax.top_k(jax.nn.softmax(le, axis=-1), TOP_K)
    e_prob = e_prob / e_prob.sum(-1, keepdims=True)
    gates = g_prob * e_prob
    experts = g_idx * EXPERTS_PER_GROUP + e_local
    A = N * TOP_K
    flat_e = experts.reshape(A).astype(jnp.int32)
    flat_tok = jnp.repeat(jnp.arange(N, dtype=jnp.int32), TOP_K)
    flat_gate = gates.reshape(A)
    order = jnp.argsort(flat_e)
    e_sorted = flat_e[order]
    counts = jnp.bincount(flat_e, length=N_EXPERTS).astype(jnp.int32)
    padded = (counts + MOE_BLOCK - 1) // MOE_BLOCK * MOE_BLOCK
    pad_end = jnp.cumsum(padded)
    pad_start = pad_end - padded
    seg_start = jnp.cumsum(counts) - counts
    dest = pad_start[e_sorted] + (jnp.arange(A, dtype=jnp.int32) - seg_start[e_sorted])
    n_blocks = -(-A // MOE_BLOCK) + N_EXPERTS
    n_rows = n_blocks * MOE_BLOCK
    row_tok = jnp.full((n_rows,), N, jnp.int32).at[dest].set(flat_tok[order])
    row_gate = jnp.zeros((n_rows,), jnp.float32).at[dest].set(flat_gate[order])
    block_expert = jnp.minimum(
        jnp.searchsorted(pad_end, jnp.arange(n_blocks, dtype=jnp.int32) * MOE_BLOCK, side='right'),
        N_EXPERTS - 1)
    x_pad = jnp.concatenate([xt, jnp.zeros((1, D), xt.dtype)], axis=0)
    xs = x_pad[row_tok].reshape(n_blocks, MOE_BLOCK, D)

    def expert_block(args):
        xb, e = args
        return (jax.nn.silu(xb @ w_gate[e]) * (xb @ w_up[e])) @ w_down[e]

    ys = lax.map(expert_block, (xs, block_expert)).reshape(n_rows, D)
    ys = ys * row_gate[:, None].astype(ys.dtype)
    out = jnp.zeros((N + 1, D), ys.dtype).at[row_tok].add(ys)[:N]
    return out.reshape(B, S, D)

def second_inputs(seed: int = 0) -> dict:
    key = jax.random.key(seed)
    ks = jax.random.split(key, 20)
    f32 = jnp.float32
    D = D_MODEL
    inv = D ** -0.5
    kvd = GQA_KV_HEADS * HEAD_DIM

    def nrm(k, shape, scale):
        return jax.random.normal(k, shape, f32) * scale

    na_cols = jnp.concatenate([jnp.ones((2 * D,), f32), jnp.full((D,), DEEPNORM_BETA_2, f32)])
    gqa_cols = jnp.concatenate([jnp.ones((D + kvd,), f32), jnp.full((kvd,), DEEPNORM_BETA_2, f32)])
    return {
        "x": nrm(ks[0], (BATCH, SEQ, D), 1.0),
        "c": nrm(ks[1], (BATCH, D), 1.0),
        "ada_w": nrm(ks[2], (DEPTH, D, 6 * D), ADA_INIT * inv),
        "ada_b": nrm(ks[3], (DEPTH, 6 * D), 0.01),
        "ln_g": 1.0 + nrm(ks[4], (DEPTH, 2, D), 0.01),
        "ln_b": nrm(ks[5], (DEPTH, 2, D), 0.01),
        "na_w_qkv": nrm(ks[6], (N_NA_LAYERS, D, 3 * D), inv) * na_cols,
        "na_rpb": nrm(ks[7], (N_NA_LAYERS, N_HEADS, 2 * NA_ROWS - 1, 2 * NA_COLS - 1), 0.1),
        "na_w_o": nrm(ks[8], (N_NA_LAYERS, D, D), inv * DEEPNORM_BETA_2),
        "gqa_w_qkv": nrm(ks[9], (N_GQA_LAYERS, D, D + 2 * kvd), inv) * gqa_cols,
        "gqa_q_norm": 1.0 + nrm(ks[10], (N_GQA_LAYERS, HEAD_DIM), 0.01),
        "gqa_k_norm": 1.0 + nrm(ks[11], (N_GQA_LAYERS, HEAD_DIM), 0.01),
        "gqa_w_o": nrm(ks[12], (N_GQA_LAYERS, D, D), inv * DEEPNORM_BETA_2),
        "moe_w_group": nrm(ks[13], (DEPTH, D, N_GROUPS), inv),
        "moe_b_group": nrm(ks[14], (DEPTH, N_GROUPS), 0.01),
        "moe_w_expert": nrm(ks[15], (DEPTH, D, N_EXPERTS), inv),
        "moe_b_expert": nrm(ks[16], (DEPTH, N_EXPERTS), 0.01),
        "moe_w_gate": nrm(ks[17], (DEPTH, N_EXPERTS, D, D_EXPERT), inv),
        "moe_w_up": nrm(ks[18], (DEPTH, N_EXPERTS, D, D_EXPERT), inv),
        "moe_w_down": nrm(ks[19], (DEPTH, N_EXPERTS, D_EXPERT, D), (D_EXPERT ** -0.5) * DEEPNORM_BETA_2),
    }

def second_block(x, c, ada_w, ada_b, ln_g, ln_b, na_w_qkv, na_rpb, na_w_o, gqa_w_qkv, gqa_q_norm,
              gqa_k_norm, gqa_w_o, moe_w_group, moe_b_group, moe_w_expert, moe_b_expert,
              moe_w_gate, moe_w_up, moe_w_down):
    B, S, D = x.shape
    cos, sin = axial_rope_tables(S)
    c_act = jax.nn.silu(c)
    for i in range(DEPTH):
        mod = c_act @ ada_w[i] + ada_b[i]
        sh1, sc1, g1, sh2, sc2, g2 = jnp.split(mod[:, None, :], 6, axis=-1)
        h = x * (1 + sc1) + sh1
        j = i // N_MIXERS
        if i % N_MIXERS == 0:
            y = neighbourhood_mixer(h, na_w_qkv[j], na_rpb[j], na_w_o[j])
        else:
            y = gqa_mixer(h, cos, sin, gqa_w_qkv[j], gqa_q_norm[j], gqa_k_norm[j], gqa_w_o[j])
        x = layer_norm_2(DEEPNORM_ALPHA_2 * x + (1 + g1) * y, ln_g[i, 0], ln_b[i, 0])
        h = x * (1 + sc2) + sh2
        y = hierarchical_moe(h, moe_w_group[i], moe_b_group[i], moe_w_expert[i], moe_b_expert[i],
                             moe_w_gate[i], moe_w_up[i], moe_w_down[i])
        x = layer_norm_2(DEEPNORM_ALPHA_2 * x + (1 + g2) * y, ln_g[i, 1], ln_b[i, 1])
    return x


def setup_inputs(seed=0):
    out = dict(first_inputs(seed))
    for name, value in second_inputs(seed + 1).items():
        if name != "x":
            out[name + "_2"] = value
    return out


def reference(
    x, w_in, conv_w, dn_a_log, dn_dt_bias, gla_gate_w2, gla_gate_b, dn_norm_g, gla_norm_g,
    w_out, ln_g, ln_b, c_2, ada_w_2, ada_b_2, ln_g_2, ln_b_2, na_w_qkv_2, na_rpb_2, na_w_o_2,
    gqa_w_qkv_2, gqa_q_norm_2, gqa_k_norm_2, gqa_w_o_2, moe_w_group_2, moe_b_group_2,
    moe_w_expert_2, moe_b_expert_2, moe_w_gate_2, moe_w_up_2, moe_w_down_2,
):
    x = first_block(
        x, w_in, conv_w, dn_a_log, dn_dt_bias, gla_gate_w2, gla_gate_b, dn_norm_g, gla_norm_g,
        w_out, ln_g, ln_b,
    )
    return second_block(
        x, c_2, ada_w_2, ada_b_2, ln_g_2, ln_b_2, na_w_qkv_2, na_rpb_2, na_w_o_2, gqa_w_qkv_2,
        gqa_q_norm_2, gqa_k_norm_2, gqa_w_o_2, moe_w_group_2, moe_b_group_2, moe_w_expert_2,
        moe_b_expert_2, moe_w_gate_2, moe_w_up_2, moe_w_down_2,
    )


_drawn_inputs = setup_inputs


def setup_inputs(seed=0):
    import zlib

    import numpy as np

    out = dict(_drawn_inputs(seed))
    spreads = {}
    factors = {'gla_gate_b': 3.873,
     'dn_norm_g': 7.421,
     'gla_norm_g': 6.919,
     'ada_b_2': 4.082,
     'na_rpb_2': 8.0,
     'gqa_q_norm_2': 33.707,
     'gqa_k_norm_2': 28.215,
     'moe_b_group_2': 8.0,
     'moe_b_expert_2': 6.409}
    for name, (base, spread) in spreads.items():
        noise = np.random.default_rng([zlib.crc32(name.encode()), seed]).standard_normal(out[name].shape)
        drawn = base * np.exp(spread * noise) if base else spread * noise
        out[name] = __import__('jax').numpy.asarray(drawn.astype(out[name].dtype))
    for name, factor in factors.items():
        out[name] = (out[name] * factor).astype(out[name].dtype)
    return out
```

```python
import numpy as np
import concourse.bass as bass
from concourse import mybir

F32 = mybir.dt.float32
I32 = mybir.dt.int32
U32 = mybir.dt.uint32
ALU = mybir.AluOpType
ACT = mybir.ActivationFunctionType
AX = mybir.AxisListType

P = 128
SEQ = 1024
D = 1024
NT = SEQ // P
NK = D // P
HALF = 512
DEPTH = 2
ALPHA = (2.0 * DEPTH) ** 0.25
NEG = -1e30

DN_HEADS, GLA_HEADS, DN_DK, GLA_DK, GLA_DV, RANK = 4, 4, 128, 64, 128, 16
C_DN = 0
C_BETA = 4 * 512
C_A = C_BETA + DN_HEADS
C_GQ = C_A + DN_HEADS
C_GK = C_GQ + GLA_HEADS * GLA_DK
C_GV = C_GK + GLA_HEADS * GLA_DK
C_GZ = C_GV + GLA_HEADS * GLA_DV
C_GR = C_GZ + GLA_HEADS * GLA_DV
LEVELS = [1, 2, 4, 8, 16, 32, 64]

K_IDENT = 0
K_ONES = K_IDENT + P
K_UPPER = K_ONES + P
K_STRICT = K_UPPER + P
K_LEVEL = K_STRICT + P
K_RESET = K_LEVEL + P * len(LEVELS)
K_IOTA = K_RESET + SEQ
K_COLS = K_IOTA + P
K_ROWS = K_COLS + 64
K_WIDTH = K_ROWS + 9


def shape_constants():
    t = np.zeros((P, K_WIDTH), np.float32)
    j, i = np.arange(P)[:, None], np.arange(P)[None, :]
    t[:, K_IDENT:K_IDENT + P] = j == i
    t[:, K_ONES:K_ONES + P] = 1
    t[:, K_UPPER:K_UPPER + P] = j <= i
    t[:, K_STRICT:K_STRICT + P] = j < i
    for n, s in enumerate(LEVELS):
        t[:, K_LEVEL + n * P:K_LEVEL + (n + 1) * P] = (
            (j // (2 * s) == i // (2 * s)) & (i % (2 * s) >= s) & (j % (2 * s) < s))
    t[:, K_RESET:K_RESET + SEQ] = np.arange(SEQ)[None, :] % P != 0
    t[:, K_IOTA:K_IOTA + P] = i
    query, key = j % GRID, i[:, :GRID]
    start = np.clip(query - 8, 0, GRID - 16)
    t[:, K_COLS:K_COLS + GRID] = np.where((key >= start) & (key < start + 16), 0, NEG)
    rho = np.arange(-4, 5)[None, :]
    t[:, K_ROWS:K_ROWS + 9] = np.where((rho - j // GRID >= -4) & (rho - j // GRID <= 3), 0, NEG)
    return t


class Places:
    pass


SEMAPHORES = (
    ["loaded_a", "loaded_b", "loaded_c", "loaded_d", "loaded_e", "stored", "prefetched",
     "pe_done", "act_done", "dve_done", "pool_done", "act_step", "dve_step", "pool_step"]
    + [f"signal_{n}" for n in range(24)])


def end_stage(nc, m):
    nc.gpsimd.sem_clear(m.sem_range)
    nc.all_engine_barrier()


class Steps:

    def __init__(self, engine, semaphore):
        self.engine, self.semaphore, self.count = engine, semaphore, 0

    def settle(self, instruction):
        self.count += 1
        instruction.then_inc(self.semaphore, 1)
        self.engine.wait_ge(self.semaphore, self.count)


def make_memory(nc):
    def sb(name, shape, dt=F32):
        return nc.alloc_sbuf_tensor("sb_" + name, shape, dt)

    m = Places()
    m.sem = {name: nc.alloc_semaphore(name) for name in SEMAPHORES}
    numbers = [s.num for s in m.sem.values()]
    m.sem_range = range(min(numbers), max(numbers) + 1)
    assert len(m.sem_range) == len(numbers)
    m.pool_dma = [{name: nc.alloc_semaphore(f"{name}_{l}") for name in
                   ("scattered", "gathered_a", "gathered_b", "gathered_more", "combined_a", "combined_b")}
                  for l in range(DEPTH)]
    m.ps = nc.alloc_psum_tensor("ps", [P, 8, HALF], F32)
    m.const = sb("const", [P, K_WIDTH])
    m.x_tok = sb("x_tok", [P, NT, D])
    m.xT = sb("xT", [P, NK, SEQ])
    m.mixT = sb("mixT", [P, NK, SEQ])
    m.work = sb("work", [P, 20 * SEQ])
    return m


def ident(m, n=P):
    return m.const[0:n, K_IDENT:K_IDENT + n]


def ones(m, rows=P):
    return m.const[0:rows, K_ONES:K_ONES + P]


def banks(m, b, rows=P):
    return m.ps[0:rows, b:b + 2, :].rearrange("p b n -> p (b n)")


def chunks(ap):
    return ap.rearrange("p (c n) -> p c n", n=P)


def spread(ap, n):
    return ap.unsqueeze(2).to_broadcast([ap.shape[0], ap.shape[1], n])


def each_chunk(ap, c=NT):
    return ap.unsqueeze(1).to_broadcast([ap.shape[0], c, ap.shape[1]])


def load_inputs_stage(nc, m, x, constants):
    loaded_a, loaded_b = m.sem["loaded_a"], m.sem["loaded_b"]
    with nc.Block() as block:
        @block.sync
        def _(sp):
            sp.dma_start(m.const[:], constants).then_inc(loaded_a, 16)
            sp.dma_start(m.x_tok[:], x[0].rearrange("(t p) d -> p t d", p=P)).then_inc(loaded_b, 16)
            sp.wait_ge(loaded_a, 16)
            sp.wait_ge(loaded_b, 16)
    end_stage(nc, m)


def transpose_stage(nc, m, src, dst):
    turned, copied_dve, copied_act = (m.sem[f"signal_{n}"] for n in range(3))
    groups = [(t, g) for t in range(NT) for g in range(2)]
    with nc.Block() as block:
        @block.tensor
        def _(pe):
            for n, (t, g) in enumerate(groups):
                if n >= 8:
                    pe.wait_ge(copied_dve if n % 2 == 0 else copied_act, (n - 8) // 2 + 1)
                for k in range(4):
                    last = pe.transpose(m.ps[:, n % 8, k * P:(k + 1) * P],
                                        src[:, t, (4 * g + k) * P:(4 * g + k + 1) * P], ident(m))
                last.then_inc(turned, 1)

        def copy_out(engine, operation, parity, copied):
            for n, (t, g) in enumerate(groups):
                if n % 2 == parity:
                    engine.wait_ge(turned, n + 1)
                    operation(dst[:, 4 * g:4 * g + 4, t * P:(t + 1) * P],
                              chunks(m.ps[:, n % 8, :])).then_inc(copied, 1)

        @block.vector
        def _(dve):
            copy_out(dve, dve.tensor_copy, 0, copied_dve)

        @block.scalar
        def _(act):
            copy_out(act, act.copy, 1, copied_act)
    end_stage(nc, m)


def hybrid_small_stage(nc, m, l, a):
    s = m.sem
    w_loaded, loaded, summed, stepped = s["loaded_a"], s["loaded_b"], s["signal_0"], s["act_step"]
    act_ready, dve_ready, turned, columns = (s[f"signal_{n}"] for n in range(1, 5))
    w = m.work
    w_beta = w[:, 0:32].rearrange("p (k n) -> p k n", k=NK)
    w_a = w[:, 32:64].rearrange("p (k n) -> p k n", k=NK)
    w_r = w[:, 64:192].rearrange("p (k n) -> p k n", k=NK)
    param_rows = w[0:52, 256:256 + P]
    abs_a, e_a, pos_a, g_rows = (w[0:4, 1024 * n:1024 * (n + 1)] for n in range(1, 5))
    beta, G = m.beta_row4[:], m.G_row4[:]
    with nc.Block() as block:
        @block.sync
        def _(sp):
            for dst, c, n in ((w_beta, C_BETA, 4), (w_a, C_A, 4), (w_r, C_GR, RANK)):
                sp.dma_start(dst, a["w_in"][l, :, c:c + n].rearrange("(k p) n -> p k n", p=P)).then_inc(w_loaded, 16)
            sp.dma_start(param_rows[0:48, :], a["conv_w"][l].rearrange("k (t p) -> (k t) p", p=P)).then_inc(loaded, 16)
            sp.dma_start(m.a_log[:], a["dn_a_log"][l].unsqueeze(1)).then_inc(loaded, 16)
            sp.dma_start(m.dt_bias[:], a["dn_dt_bias"][l].unsqueeze(1)).then_inc(loaded, 16)
            sp.dma_start(param_rows[48:49, :], a["dn_norm_g"][l].rearrange("(o p) -> o p", o=1)).then_inc(loaded, 16)
            sp.dma_start(param_rows[49:50, :], a["gla_norm_g"][l].rearrange("(o p) -> o p", o=1)).then_inc(loaded, 16)
            sp.dma_start(param_rows[50:52, :], a["gla_gate_b"][l].rearrange("(t p) -> t p", p=P)).then_inc(loaded, 16)
            sp.dma_start(m.gate_w2[:], a["gla_gate_w2"][l]).then_inc(loaded, 16)
            sp.wait_ge(loaded, 7 * 16)

        @block.tensor
        def _(pe):
            pe.wait_ge(w_loaded, 48)
            for n, wt in enumerate((w_beta, w_a, w_r)):
                for half in range(2):
                    for k in range(NK):
                        last = pe.matmul(m.ps[0:wt.shape[2], 2 * n + half, :], wt[:, k, :],
                                         m.xT[:, k, half * HALF:(half + 1) * HALF],
                                         start=(k == 0), stop=(k == NK - 1))
            last.then_inc(summed, 1)
            pe.wait_ge(loaded, 7 * 16)
            pe.transpose(m.ps[:, 6, 0:52], param_rows, ident(m, 52)).then_inc(turned, 1)
            pe.wait_ge(dve_ready, 3)
            for c in range(NT):
                pe.transpose(m.ps[:, 7, c * 4:c * 4 + 4], G[:, c * P:(c + 1) * P], ident(m, 4))
                last = pe.transpose(m.ps[:, 7, 64 + c * 4:64 + c * 4 + 4], beta[:, c * P:(c + 1) * P],
                                    ident(m, 4))
            last.then_inc(columns, 1)

        @block.scalar
        def _(act):
            st = Steps(act, stepped)
            act.wait_ge(summed, 1)
            act.wait_ge(loaded, 7 * 16)
            act.copy(m.rT[:], banks(m, 4, RANK))
            st.settle(act.activation(m.a_log[:], m.a_log[:], ACT.Exp))
            act.activation(beta, banks(m, 0, 4), ACT.Exp, scale=-1.0).then_inc(act_ready, 1)
            act.wait_ge(dve_ready, 1)
            st.settle(act.activation(e_a, abs_a, ACT.Exp))
            act.activation(g_rows, e_a, ACT.Ln, bias=m.one[0:4, :]).then_inc(act_ready, 1)

        @block.vector
        def _(dve):
            st = Steps(dve, s["dve_step"])
            dve.wait_ge(summed, 1)
            dve.wait_ge(loaded, 7 * 16)
            st.settle(dve.tensor_scalar(pos_a, banks(m, 2, 4), m.dt_bias[:], None, ALU.add))
            st.settle(dve.scalar_tensor_tensor(abs_a, pos_a, -1.0, pos_a, ALU.mult, ALU.min))
            dve.tensor_scalar(pos_a, pos_a, 0.0, None, ALU.max).then_inc(dve_ready, 1)
            dve.wait_ge(act_ready, 2)
            st.settle(dve.tensor_scalar(beta, beta, 1.0, None, ALU.add))
            dve.reciprocal(beta, beta).then_inc(dve_ready, 1)
            st.settle(dve.tensor_tensor(g_rows, g_rows, pos_a, ALU.add))
            st.settle(dve.tensor_scalar(g_rows, g_rows, m.a_log[:], -1.0, ALU.mult, ALU.mult))
            dve.tensor_tensor_scan(G, m.const[0:4, K_RESET:K_RESET + SEQ], g_rows, 0.0,
                                   ALU.mult, ALU.add).then_inc(dve_ready, 1)
            dve.wait_ge(turned, 1)
            dve.tensor_copy(m.conv[:], m.ps[:, 6, 0:52])
            dve.wait_ge(columns, 1)
            dve.tensor_copy(m.G_col[:], m.ps[:, 7, 0:32].rearrange("p (c h) -> p h c", h=4))
            dve.tensor_copy(m.beta_col[:], m.ps[:, 7, 64:96].rearrange("p (c h) -> p h c", h=4))
    end_stage(nc, m)


def load_columns(engine, dst, w, column, n, semaphore):
    engine.dma_start(dst, w[:, bass.ds(column, n)].rearrange("(k p) n -> p k n", p=P)).then_inc(semaphore, 16)


def project_T(pe, m, w_tile, bank):
    for half in range(2):
        for k in range(NK):
            last = pe.matmul(m.ps[:, bank + half, :], w_tile[:, k, :],
                             m.xT[:, k, half * HALF:(half + 1) * HALF], start=(k == 0), stop=(k == NK - 1))
    return last


def sum_features(pe, m, src, bank):
    for half in range(2):
        last = pe.matmul(m.ps[:, bank + half, :], ones(m), src[:, half * HALF:(half + 1) * HALF],
                         start=True, stop=True)
    return last


def delta_head(nc, m, l, a, h):
    s = m.sem
    W = [m.work[:, n * SEQ:(n + 1) * SEQ] for n in range(20)]
    wq = [m.work[:, n * SEQ:(n + 1) * SEQ].rearrange("p (k n) -> p k n", k=NK) for n in range(4)]
    pads = [m.pad[:, n, :] for n in range(3)]
    qT, kT, vT, zT = W[4], W[5], W[6], W[7]
    r_q, r_k = W[8], W[9]
    G_row, decay = W[10], W[11]
    LT, attnT = W[12], W[13]
    w_loaded = s["loaded_a"]
    projected, evicted, convolved, silued, squared, normed, summed, rooted, spreaded = (
        s[f"signal_{n}"] for n in range(9))

    with nc.Block() as block:
        @block.sync
        def _(sp):
            for j in range(4):
                load_columns(sp, wq[j], a["w_in"][l], h * P + j * 512, P, s[f"loaded_{'abcd'[j]}"])

        @block.tensor
        def _(pe):
            for j in range(4):
                pe.wait_ge(s[f"loaded_{'abcd'[j]}"], 16)
                project_T(pe, m, wq[j], 2 * j).then_inc(projected, 1)
            for n in range(2):
                pe.wait_ge(squared, n + 1)
                sum_features(pe, m, (r_q, r_k)[n], 2 * n).then_inc(summed, 1)
            pe.wait_ge(evicted, 3)
            pe.wait_ge(s["signal_10"], 1)
            for half in range(2):
                pe.matmul(m.ps[:, 4 + half, :], m.pick[:], m.G_row4[:, half * HALF:(half + 1) * HALF],
                          start=True, stop=True)
            pe.wait_ge(silued, 4)
            for half in range(2):
                last = pe.matmul(m.ps[:, 6 + half, :], m.pick[:], m.beta_row4[:, half * HALF:(half + 1) * HALF],
                                 start=True, stop=True)
            last.then_inc(spreaded, 1)

        @block.scalar
        def _(act):
            for j in range(3):
                act.wait_ge(projected, j + 1)
                act.copy(pads[j][:, 3:3 + SEQ], banks(m, 2 * j)).then_inc(evicted, 1)
            act.wait_ge(projected, 4)
            for j, x in enumerate((qT, kT, vT)):
                act.wait_ge(convolved, j + 1)
                act.activation(x, x, ACT.Silu).then_inc(silued, 1)
            act.activation(zT, banks(m, 6), ACT.Silu).then_inc(silued, 1)
            for n, x in enumerate((qT, kT)):
                act.wait_ge(silued, n + 1)
                act.activation((r_q, r_k)[n], x, ACT.Square).then_inc(squared, 1)
            for n in range(2):
                act.wait_ge(summed, n + 1)
                act.activation((r_q, r_k)[n], banks(m, 2 * n), ACT.Ln, bias=m.eps6[:]).then_inc(rooted, 1)
            for n in range(2):
                act.wait_ge(rooted, n + 1)
                act.activation((r_q, r_k)[n], (r_q, r_k)[n], ACT.Exp, scale=-0.5).then_inc(rooted, 1)
            act.wait_ge(spreaded, 1)
            act.copy(W[14], banks(m, 6)).then_inc(s["signal_9"], 1)

        @block.vector
        def _(dve):
            st = Steps(dve, s["dve_step"])
            dve.tensor_scalar(m.pick[:], ones(m, 4), m.const[0:4, bass.ds(h + K_IDENT, 1)], None,
                              ALU.mult).then_inc(s["signal_10"], 1)
            st.settle(dve.memset(m.pad[:, :, 0:3], 0.0))
            for j, x in enumerate((qT, kT, vT)):
                dve.wait_ge(evicted, j + 1)
                taps = [m.conv[:, bass.ds(h + (k * 12 + j * 4), 1)] for k in range(4)]
                st.settle(dve.tensor_scalar(x, pads[j][:, 0:SEQ], taps[0], None, ALU.mult))
                for k in range(1, 3):
                    st.settle(dve.scalar_tensor_tensor(x, pads[j][:, k:k + SEQ], taps[k], x, ALU.mult, ALU.add))
                dve.scalar_tensor_tensor(x, pads[j][:, 3:3 + SEQ], taps[3], x, ALU.mult,
                                         ALU.add).then_inc(convolved, 1)
            dve.wait_ge(rooted, 4)
            dve.wait_ge(squared, 2)
            dve.scalar_tensor_tensor(qT, qT, DN_DK ** -0.5, r_q, ALU.mult, ALU.mult)
            dve.tensor_tensor(kT, kT, r_k, ALU.mult)
            dve.wait_ge(spreaded, 1)
            dve.tensor_copy(G_row, banks(m, 4))
    end_stage(nc, m)

    G_col, beta_col = m.G_col[:, h, :], m.beta_col[:, h, :]
    beta_row = W[14]
    k_beta, k_decay, v_beta, expG = W[15], W[16], W[17], W[18]
    c_bg, c_dec = m.cols[:, 0:8], m.cols[:, 8:16]
    kk_ready, qk_ready, k_turned, v_turned, diff_ready, exp_ready, cols_ready = (
        s[f"signal_{n}"] for n in range(7))
    with nc.Block() as block:
        @block.tensor
        def _(pe):
            for c in range(NT):
                at = slice(c * P, (c + 1) * P)
                last = pe.matmul(banks(m, 0)[:, at], kT[:, at], kT[:, at], start=True, stop=True)
            last.then_inc(kk_ready, 1)
            for c in range(NT):
                at = slice(c * P, (c + 1) * P)
                last = pe.matmul(banks(m, 2)[:, at], kT[:, at], qT[:, at], start=True, stop=True)
            last.then_inc(qk_ready, 1)
            for c in range(NT):
                at = slice(c * P, (c + 1) * P)
                last = pe.transpose(banks(m, 4)[:, at], kT[:, at], ident(m))
            last.then_inc(k_turned, 1)
            for c in range(NT):
                at = slice(c * P, (c + 1) * P)
                last = pe.transpose(banks(m, 6)[:, at], vT[:, at], ident(m))
            last.then_inc(v_turned, 1)

        @block.scalar
        def _(act):
            st = Steps(act, s["act_step"])
            act.activation(expG, G_row, ACT.Exp)
            act.activation(c_bg, G_col, ACT.Exp).then_inc(cols_ready, 1)
            act.wait_ge(diff_ready, 1)
            act.activation(c_dec, c_dec, ACT.Exp).then_inc(cols_ready, 1)
            act.wait_ge(diff_ready, 2)
            act.activation(decay, decay, ACT.Exp).then_inc(exp_ready, 1)

        @block.vector
        def _(dve):
            st = Steps(dve, s["dve_step"])
            dve.tensor_tensor(c_dec, chunks(G_row)[:, :, P - 1:P].rearrange("p c n -> p (c n)"), G_col,
                              ALU.subtract).then_inc(diff_ready, 1)
            st.settle(dve.tensor_tensor(chunks(decay), chunks(G_row), spread(G_col, P), ALU.subtract))
            dve.tensor_scalar(decay, decay, 0.0, None, ALU.min).then_inc(diff_ready, 1)
            dve.wait_ge(cols_ready, 2)
            st.settle(dve.tensor_tensor(c_bg, c_bg, beta_col, ALU.mult))
            dve.wait_ge(k_turned, 1)
            dve.tensor_tensor(chunks(k_beta), chunks(banks(m, 4)), spread(c_bg, P), ALU.mult)
            dve.tensor_tensor(chunks(k_decay), chunks(banks(m, 4)), spread(c_dec, P), ALU.mult)
            dve.wait_ge(v_turned, 1)
            dve.tensor_tensor(chunks(v_beta), chunks(banks(m, 6)), spread(beta_col, P), ALU.mult)
            dve.wait_ge(exp_ready, 1)
            dve.wait_ge(kk_ready, 1)
            st.settle(dve.tensor_tensor(LT, banks(m, 0), decay, ALU.mult))
            dve.tensor_tensor(LT, LT, beta_row, ALU.mult)
            dve.wait_ge(qk_ready, 1)
            st.settle(dve.tensor_tensor(attnT, banks(m, 2), decay, ALU.mult))
            dve.tensor_tensor(chunks(attnT), chunks(attnT), each_chunk(m.const[:, K_UPPER:K_UPPER + P]), ALU.mult)
    end_stage(nc, m)

    X, XT, BT, T1 = W[0], W[1], W[2], W[3]
    b_ready, t_ready, t_copied, p_ready, x_ready, xt_ready = (s[f"signal_{n}"] for n in range(6))
    with nc.Block() as block:
        @block.tensor
        def _(pe):
            for n in range(len(LEVELS)):
                pe.wait_ge(b_ready, n + 1)
                pe.wait_ge(x_ready, n + 1)
                pe.wait_ge(xt_ready, n + 1)
                for c in range(NT):
                    at = slice(c * P, (c + 1) * P)
                    last = pe.matmul(banks(m, 0)[:, at], BT[:, at], X[:, at], start=True, stop=True)
                    if c % 4 == 3:
                        last.then_inc(t_ready, 1)
                for c in range(NT):
                    at = slice(c * P, (c + 1) * P)
                    if c % 4 == 0:
                        pe.wait_ge(t_copied, 2 * n + c // 4 + 1)
                    pe.matmul(banks(m, 2)[:, at], XT[:, at], T1[:, at], start=True, stop=True)
                    last = pe.matmul(banks(m, 4)[:, at], T1[:, at], XT[:, at], start=True, stop=True)
                last.then_inc(p_ready, 1)

        @block.scalar
        def _(act):
            for n in range(len(LEVELS)):
                for half in range(2):
                    act.wait_ge(t_ready, 2 * n + half + 1)
                    act.copy(T1[:, half * HALF:(half + 1) * HALF], m.ps[:, half, :]).then_inc(t_copied, 1)

        @block.gpsimd
        def _(pool):
            for n in range(len(LEVELS)):
                if n:
                    pool.wait_ge(t_ready, 2 * n)
                mask = m.const[:, K_LEVEL + n * P:K_LEVEL + (n + 1) * P]
                pool.tensor_tensor(chunks(BT), chunks(LT), each_chunk(mask), ALU.mult).then_inc(b_ready, 1)

        @block.vector
        def _(dve):
            dve.tensor_copy(chunks(X), each_chunk(ident(m))).then_inc(x_ready, 1)
            dve.tensor_copy(chunks(XT), each_chunk(ident(m))).then_inc(xt_ready, 1)
            for n in range(len(LEVELS)):
                dve.wait_ge(p_ready, n + 1)
                dve.wait_ge(x_ready, n + 1)
                dve.tensor_tensor(X, X, banks(m, 2), ALU.subtract).then_inc(x_ready, 1)
                dve.wait_ge(xt_ready, n + 1)
                dve.tensor_tensor(XT, XT, banks(m, 4), ALU.subtract).then_inc(xt_ready, 1)
    end_stage(nc, m)

    wT, u, qg, vn, S, oT = W[19], W[12], W[3], W[11], m.state, W[2]
    w_ready, u_ready, w_copied, u_copied, q_scaled, ws_ready, vn_ready, s_ready, s_done, o_ready = (
        s[f"signal_{n}"] for n in range(10))
    with nc.Block() as block:
        @block.tensor
        def _(pe):
            for c in range(NT):
                at = slice(c * P, (c + 1) * P)
                last = pe.matmul(banks(m, 0)[:, at], k_beta[:, at], XT[:, at], start=True, stop=True)
            last.then_inc(w_ready, 1)
            for c in range(NT):
                at = slice(c * P, (c + 1) * P)
                last = pe.matmul(banks(m, 2)[:, at], XT[:, at], v_beta[:, at], start=True, stop=True)
            last.then_inc(u_ready, 1)
            pe.wait_ge(w_copied, 1)
            pe.wait_ge(q_scaled, 1)
            for c in range(NT):
                at = slice(c * P, (c + 1) * P)
                pe.wait_ge(s_done, c + 1)
                pe.matmul(m.ps[:, 4, (c % 2) * P:(c % 2 + 1) * P], wT[:, at], S[:, c % 2, :],
                          start=True, stop=True).then_inc(ws_ready, 1)
                pe.matmul(m.ps[:, 6 + c // 4, (c % 4) * P:(c % 4 + 1) * P], S[:, c % 2, :], qg[:, at],
                          start=True, stop=False)
                pe.wait_ge(vn_ready, c + 1)
                pe.matmul(m.ps[:, 5, (c % 2) * P:(c % 2 + 1) * P], k_decay[:, at], vn[:, at],
                          start=True, stop=True).then_inc(s_ready, 1)
                pe.matmul(m.ps[:, 6 + c // 4, (c % 4) * P:(c % 4 + 1) * P], vn[:, at], attnT[:, at],
                          start=False, stop=True).then_inc(o_ready, 1)

        @block.scalar
        def _(act):
            act.wait_ge(w_ready, 1)
            act.copy(wT, banks(m, 0)).then_inc(w_copied, 1)
            for half in range(2):
                act.wait_ge(o_ready, 4 * (half + 1))
                act.copy(oT[:, half * HALF:(half + 1) * HALF], m.ps[:, 6 + half, :])

        @block.vector
        def _(dve):
            dve.memset(S[:, 0, :], 0.0).then_inc(s_done, 1)
            dve.tensor_tensor(qg, qT, expG, ALU.mult).then_inc(q_scaled, 1)
            dve.wait_ge(u_ready, 1)
            dve.tensor_copy(u, banks(m, 2)).then_inc(u_copied, 1)
            dve.wait_ge(u_copied, 1)
            for c in range(NT):
                at = slice(c * P, (c + 1) * P)
                dve.wait_ge(ws_ready, c + 1)
                dve.tensor_tensor(vn[:, at], u[:, at], m.ps[:, 4, (c % 2) * P:(c % 2 + 1) * P],
                                  ALU.subtract).then_inc(vn_ready, 1)
                dve.wait_ge(s_ready, c + 1)
                dve.wait_ge(s_done, c + 1)
                dve.scalar_tensor_tensor(S[:, (c + 1) % 2, :], S[:, c % 2, :], expG[:, c * P + P - 1:c * P + P],
                                         m.ps[:, 5, (c % 2) * P:(c % 2 + 1) * P], ALU.mult,
                                         ALU.add).then_inc(s_done, 1)
    end_stage(nc, m)
    gated_norm_stage(nc, m, oT, zT, m.dn_g, h)


def gated_norm_stage(nc, m, oT, zT, gain, slot):
    s = m.sem
    r = m.work[:, 0:SEQ]
    squared, summed = s["signal_0"], s["signal_1"]
    with nc.Block() as block:
        @block.tensor
        def _(pe):
            pe.wait_ge(squared, 1)
            sum_features(pe, m, r, 0).then_inc(summed, 1)

        @block.scalar
        def _(act):
            st = Steps(act, s["act_step"])
            act.activation(r, oT, ACT.Square).then_inc(squared, 1)
            act.wait_ge(summed, 1)
            st.settle(act.activation(r, banks(m, 0), ACT.Ln, bias=m.eps6[:], scale=1.0 / P))
            act.activation(r, r, ACT.Exp, scale=-0.5).then_inc(s["signal_2"], 1)

        @block.vector
        def _(dve):
            st = Steps(dve, s["dve_step"])
            dve.wait_ge(s["signal_2"], 1)
            st.settle(dve.scalar_tensor_tensor(oT, oT, gain[:], r, ALU.mult, ALU.mult))
            dve.tensor_tensor(m.mixT[:, slot, :], oT, zT, ALU.mult)
    end_stage(nc, m)


def more_memory(nc, m):
    def sb(name, shape, dt=F32):
        return nc.alloc_sbuf_tensor("sb_" + name, shape, dt)

    m.rT = m.mixT[0:RANK, NK - 1, :]
    m.beta_row4, m.G_row4, m.pick = sb("beta_row4", [4, SEQ]), sb("G_row4", [4, SEQ]), sb("pick", [4, P])
    m.a_log, m.dt_bias = sb("a_log", [4, 1]), sb("dt_bias", [4, 1])
    m.gate_w2 = sb("gate_w2", [RANK, GLA_HEADS * GLA_DK])
    m.one, m.eps6, m.eps5 = sb("one", [P, 1]), sb("eps6", [P, 1]), sb("eps5", [P, 1])
    m.conv, m.G_col, m.beta_col = sb("conv", [P, 52]), sb("G_col", [P, 4, NT]), sb("beta_col", [P, 4, NT])
    m.dn_g, m.gla_g, m.gate_b = m.conv[:, 48:49], m.conv[:, 49:50], m.conv[:, 50:52]
    m.cols, m.cols2 = sb("cols", [P, 64]), sb("cols2", [P, 64])
    m.stats, m.moments = sb("stats", [P, 2, 2, 6]), sb("moments", [P, NT, 2])
    m.mods = nc.dram_tensor("scratch_mods", [DEPTH, 6 * D], F32, kind="Internal").ap()
    m.gates, m.dest = sb("gates", [P, NT, TOP_K]), sb("dest", [P, TOP_K, NT], I32)
    m.overflow, m.slots = sb("overflow", [P, OVERFLOW + 1], I32), sb("slots", [P, N_BLOCKS], I32)
    m.index = sb("index", [P, 2], I32)
    m.h_dram = nc.dram_tensor("scratch_h", [SEQ, D], F32, kind="Internal").ap()
    m.y_dram = nc.dram_tensor("scratch_y", [P * N_BLOCKS, D], F32, kind="Internal").ap()
    m.slot_token = nc.dram_tensor("scratch_slots", [P * N_BLOCKS, 1], I32, kind="Internal").ap()
    m.bias_dram = nc.dram_tensor("scratch_bias", [64, 240, 64], F32, kind="Internal").ap()
    m.state = sb("state", [P, 2, P])
    m.gla_state = m.state
    m.pick_w = sb("pick_w", [RANK, P])
    m.pad = m.work[:, 15 * SEQ:15 * SEQ + 3 * (3 + SEQ)].rearrange("p (j n) -> p j n", j=3)


def constants_stage(nc, m):
    with nc.Block() as block:
        @block.vector
        def _(dve):
            dve.memset(m.one[:], 1.0)
            dve.memset(m.eps6[:], 1e-6)
            dve.memset(m.eps5[:], 1e-5)
            dve.memset(m.work[:, 0:SEQ], 0.0).then_inc(m.sem["dve_done"], 1)

        @block.sync
        def _(sp):
            sp.wait_ge(m.sem["dve_done"], 1)
            y_blocks = m.y_dram.rearrange("(p b) d -> p b d", p=P)
            for b in range(N_EXPERTS, N_BLOCKS):
                sp.dma_start(y_blocks[:, b, :], m.work[:, 0:SEQ]).then_inc(m.sem["stored"], 16)
            sp.wait_ge(m.sem["stored"], 16 * OVERFLOW)
    end_stage(nc, m)


def gla_pair(nc, m, l, a, pair):
    s = m.sem
    W = [m.work[:, n * SEQ:(n + 1) * SEQ] for n in range(20)]
    wt = [m.work[:, n * SEQ:(n + 1) * SEQ].rearrange("p (k n) -> p k n", k=NK) for n in range(6)]
    qT, kT, zT, v_tok = W[6], W[7], (W[8], W[9]), (W[10], W[11])
    B, e_abs, pos = W[12], W[13], W[14]
    loads = [s[f"loaded_{x}"] for x in "abcde"] + [s["prefetched"]]
    projected, logits, abs_ready, e_ready, ln_ready, z_ready = (s[f"signal_{n}"] for n in range(6))
    with nc.Block() as block:
        @block.sync
        def _(sp):
            columns = [C_GQ + pair * P, C_GK + pair * P, C_GZ + pair * 2 * P, C_GZ + pair * 2 * P + P,
                       C_GV + pair * 2 * P, C_GV + pair * 2 * P + P]
            for j in range(6):
                load_columns(sp, wt[j], a["w_in"][l], columns[j], P, loads[j])
            for j in range(6):
                sp.wait_ge(loads[j], 16)

        @block.tensor
        def _(pe):
            pe.wait_ge(s["signal_6"], 1)
            for half in range(2):
                last = pe.matmul(m.ps[:, 6 + half, :], m.pick_w[:], m.rT[:, half * HALF:(half + 1) * HALF],
                                 start=True, stop=True)
            last.then_inc(logits, 1)
            for j in range(3):
                pe.wait_ge(loads[j], 16)
                project_T(pe, m, wt[j], 2 * j).then_inc(projected, 1)
            pe.wait_ge(loads[3], 16)
            pe.wait_ge(abs_ready, 1)
            project_T(pe, m, wt[3], 6).then_inc(projected, 1)
            for j in range(2):
                pe.wait_ge(loads[4 + j], 16)
                pe.wait_ge(s["signal_7"], j + 1)
                for t in range(NT):
                    for k in range(NK):
                        last = pe.matmul(banks(m, 2 * j)[:, t * P:(t + 1) * P],
                                         m.xT[:, k, t * P:(t + 1) * P], wt[4 + j][:, k, :],
                                         start=(k == 0), stop=(k == NK - 1))
                last.then_inc(projected, 1)

        @block.scalar
        def _(act):
            st = Steps(act, s["act_step"])
            act.wait_ge(abs_ready, 1)
            st.settle(act.activation(e_abs, e_abs, ACT.Exp))
            act.activation(e_abs, e_abs, ACT.Ln, bias=m.one[:]).then_inc(ln_ready, 1)
            act.wait_ge(projected, 1)
            act.mul(qT, banks(m, 0), GLA_DK ** -0.5).then_inc(s["signal_7"], 1)
            act.wait_ge(projected, 2)
            act.copy(kT, banks(m, 2)).then_inc(s["signal_7"], 1)
            act.wait_ge(projected, 3)
            act.activation(zT[0], banks(m, 4), ACT.Silu)
            act.wait_ge(projected, 4)
            act.activation(zT[1], banks(m, 6), ACT.Silu)
            for j in range(2):
                act.wait_ge(projected, 5 + j)
                act.copy(v_tok[j], banks(m, 2 * j))

        @block.vector
        def _(dve):
            st = Steps(dve, s["dve_step"])
            dve.tensor_copy(m.pick_w[:], m.gate_w2[:, bass.ds(pair * P, P)]).then_inc(s["signal_6"], 1)
            dve.wait_ge(logits, 1)
            st.settle(dve.tensor_scalar(pos, banks(m, 6), m.gate_b[:, bass.ds(pair, 1)], -1.0, ALU.add, ALU.mult))
            dve.scalar_tensor_tensor(e_abs, pos, -1.0, pos, ALU.mult, ALU.min).then_inc(abs_ready, 1)
            dve.wait_ge(abs_ready, 1)
            st.settle(dve.tensor_scalar(pos, pos, 0.0, None, ALU.max))
            dve.wait_ge(ln_ready, 1)
            st.settle(dve.tensor_tensor(pos, pos, e_abs, ALU.add))
            st.settle(dve.tensor_scalar(pos, pos, -1.0 / 16.0, None, ALU.mult))
            dve.tensor_tensor_scan(B, m.const[:, K_RESET:K_RESET + SEQ], pos, 0.0, ALU.mult, ALU.add)
    end_stage(nc, m)

    attn = (W[15], W[16])
    E, qs, ks = (W[0], W[1]), (W[2], W[3]), (W[4], W[5])
    expB, qg, k_dec, k_dec_tok = W[17], W[18], W[13], W[14]
    d_ready, min_ready, exp_ready, q_ready, k_ready, a_ready, a_taken = (s[f"signal_{n}"] for n in range(7))
    n_levels = len(LEVELS)
    with nc.Block() as block:
        @block.tensor
        def _(pe):
            for n in range(n_levels + 1):
                if n < n_levels:
                    pe.wait_ge(q_ready, n + 1)
                    pe.wait_ge(k_ready, n + 1)
                for head in range(2):
                    bank = 4 * (n % 2) + 2 * head
                    if n >= 2:
                        pe.wait_ge(a_taken, 2 * (n - 2) + head + 1)
                    rows = slice(64 * head, 64 * head + 64)
                    q_at, k_at = (qs[n % 2], ks[n % 2]) if n < n_levels else (qT, kT)
                    for c in range(NT):
                        at = slice(c * P, (c + 1) * P)
                        last = pe.matmul(banks(m, bank)[:, at], k_at[rows, at], q_at[rows, at],
                                         start=True, stop=True)
                    last.then_inc(a_ready, 1)

        @block.gpsimd
        def _(pool):
            for n in range(n_levels):
                pool.wait_ge(exp_ready, n + 1)
                if n >= 2:
                    pool.wait_ge(a_ready, 2 * (n - 1))
                pool.tensor_tensor(ks[n % 2], kT, E[n % 2], ALU.mult).then_inc(k_ready, 1)

        @block.scalar
        def _(act):
            for n in range(n_levels):
                act.wait_ge(min_ready, n + 1)
                act.activation(E[n % 2], E[n % 2], ACT.Exp).then_inc(exp_ready, 1)
            act.activation(expB, B, ACT.Exp)

        @block.vector
        def _(dve):
            st = Steps(dve, s["dve_step"])

            def exponent(n):
                size = 2 * LEVELS[n]
                blocks = B.rearrange("p (b n) -> p b n", n=size)
                middle = blocks[:, :, LEVELS[n] - 1:LEVELS[n]].to_broadcast([P, SEQ // size, size])
                if n >= 2:
                    dve.wait_ge(q_ready, n - 1)
                    dve.wait_ge(k_ready, n - 1)
                e = E[n % 2]
                st.settle(dve.tensor_tensor(e.rearrange("p (b n) -> p b n", n=size), blocks, middle, ALU.subtract))
                dve.scalar_tensor_tensor(e, e, -1.0, e, ALU.mult, ALU.min).then_inc(min_ready, 1)

            def scaled_q(n):
                dve.wait_ge(exp_ready, n + 1)
                if n >= 2:
                    dve.wait_ge(a_ready, 2 * (n - 1))
                dve.tensor_tensor(qs[n % 2], qT, E[n % 2], ALU.mult).then_inc(q_ready, 1)

            dve.memset(attn[0], 0.0).then_inc(s["signal_7"], 1)
            dve.memset(attn[1], 0.0).then_inc(s["signal_7"], 1)
            exponent(0)
            for n in range(n_levels + 1):
                if n < n_levels:
                    scaled_q(n)
                if n + 1 < n_levels:
                    exponent(n + 1)
                column = K_LEVEL + n * P if n < n_levels else K_IDENT
                mask = each_chunk(m.const[:, column:column + P].bitcast(I32))
                for head in range(2):
                    dve.wait_ge(a_ready, 2 * n + head + 1)
                    dve.wait_ge(s["signal_7"], 2)
                    if n:
                        dve.wait_ge(a_taken, 2 * (n - 1) + head + 1)
                    dve.copy_predicated(chunks(attn[head]), mask, chunks(banks(m, 4 * (n % 2) + 2 * head))
                                        ).then_inc(a_taken, 1)
    end_stage(nc, m)

    oT = (W[2], W[3])
    state = m.gla_state
    turned, turned_out, kd_ready, scaled, s_done, ds_ready, o_ready, eb_ready = (
        s[f"signal_{n}"] for n in range(8))
    with nc.Block() as block:
        @block.tensor
        def _(pe):
            pe.wait_ge(kd_ready, 1)
            for c in range(NT):
                at = slice(c * P, (c + 1) * P)
                last = pe.transpose(banks(m, 0)[:, at], k_dec[:, at], ident(m))
            last.then_inc(turned, 1)
            pe.wait_ge(turned_out, 1)
            pe.wait_ge(scaled, 1)
            for c in range(NT):
                at = slice(c * P, (c + 1) * P)
                for head in range(2):
                    if c >= 2:
                        pe.wait_ge(s_done, c)
                    last = pe.matmul(m.ps[:, 2 + c % 2, head * P:(head + 1) * P], k_dec_tok[:, at],
                                     v_tok[head][:, at], start=True, stop=True)
                last.then_inc(ds_ready, 1)
                pe.wait_ge(s_done, c + 1)
                for head in range(2):
                    rows = slice(64 * head, 64 * head + 64)
                    out = m.ps[:, 4 + 2 * head + c // 4, (c % 4) * P:(c % 4 + 1) * P]
                    pe.matmul(out, state[rows, c % 2, :], qg[rows, at], start=True, stop=False)
                    last = pe.matmul(out, v_tok[head][:, at], attn[head][:, at], start=False, stop=True)
                last.then_inc(o_ready, 1)

        @block.scalar
        def _(act):
            act.wait_ge(s["signal_8"], 1)
            act.activation(k_dec, k_dec, ACT.Exp).then_inc(eb_ready, 1)
            act.wait_ge(turned, 1)
            act.copy(k_dec_tok, banks(m, 0)).then_inc(turned_out, 1)
            for half in range(2):
                act.wait_ge(o_ready, 4 * (half + 1))
                for head in range(2):
                    act.copy(oT[head][:, half * HALF:(half + 1) * HALF], m.ps[:, 4 + 2 * head + half, :])

        @block.vector
        def _(dve):
            last_B = chunks(B)[:, :, P - 1:P].to_broadcast([P, NT, P])
            dve.tensor_tensor(chunks(k_dec), last_B, chunks(B), ALU.subtract).then_inc(s["signal_8"], 1)
            dve.memset(state[:, 0, :], 0.0).then_inc(s_done, 1)
            dve.tensor_tensor(qg, qT, expB, ALU.mult).then_inc(scaled, 1)
            dve.wait_ge(eb_ready, 1)
            dve.tensor_tensor(k_dec, k_dec, kT, ALU.mult).then_inc(kd_ready, 1)
            for c in range(NT):
                dve.wait_ge(ds_ready, c + 1)
                dve.wait_ge(s_done, c + 1)
                if c:
                    dve.wait_ge(o_ready, c)
                for head in range(2):
                    rows = slice(64 * head, 64 * head + 64)
                    last = dve.scalar_tensor_tensor(
                        state[rows, (c + 1) % 2, :], state[rows, c % 2, :],
                        expB[rows, c * P + P - 1:c * P + P], m.ps[rows, 2 + c % 2, head * P:(head + 1) * P],
                        ALU.mult, ALU.add)
                last.then_inc(s_done, 1)
    end_stage(nc, m)
    for head in range(2):
        gated_norm_stage(nc, m, oT[head], zT[head], m.gla_g, pair * 2 + (4 + head))


def out_stage(nc, m, w_out, ln_g, ln_b, eps, gate=None):
    s = m.sem
    w = m.work[:, 0:8 * SEQ].rearrange("p (k n) -> p k n", k=NK)
    g_row, b_row, gate_row = (m.work[:, n * SEQ:(n + 1) * SEQ] for n in (8, 9, 10))
    y = [m.work[:, n * SEQ:(n + 1) * SEQ] for n in (11, 12)]
    y_ready, y_taken, var_ready, root_ready, scaled = (s[f"signal_{n}"] for n in range(5))
    ln_ready = s["signal_5"]
    with nc.Block() as block:
        @block.sync
        def _(sp):
            if w_out is not None:
                for k in range(NK):
                    sp.dma_start(w[:, k, :], w_out[k * P:(k + 1) * P, :]).then_inc(s["loaded_a"], 16)
            rows = [(g_row, ln_g), (b_row, ln_b)] + ([(gate_row, gate)] if gate is not None else [])
            for dst, src in rows:
                sp.dma_start(dst, src.partition_broadcast(P)).then_inc(s["loaded_b"], 16)
            sp.wait_ge(s["loaded_b"], 16 * len(rows))
            if w_out is not None:
                sp.wait_ge(s["loaded_a"], 16 * NK)

        @block.tensor
        def _(pe):
            if w_out is None:
                return
            pe.wait_ge(s["loaded_a"], 16 * NK)
            for t in range(NT):
                if t >= 4:
                    pe.wait_ge(y_taken, t - 3)
                for half in range(2):
                    for k in range(NK):
                        last = pe.matmul(m.ps[:, 2 * (t % 4) + half, :], m.mixT[:, k, t * P:(t + 1) * P],
                                         w[:, k, half * HALF:(half + 1) * HALF],
                                         start=(k == 0), stop=(k == NK - 1))
                last.then_inc(y_ready, 1)

        @block.scalar
        def _(act):
            for t in range(NT):
                act.wait_ge(var_ready, t + 1)
                act.activation(m.cols[:, t:t + 1], m.moments[:, t, 1:2], ACT.Ln, bias=eps[:]).then_inc(ln_ready, 1)
                act.wait_ge(ln_ready, t + 1)
                act.activation(m.cols[:, t:t + 1], m.cols[:, t:t + 1], ACT.Exp, scale=-0.5).then_inc(root_ready, 1)

        @block.vector
        def _(dve):
            st = Steps(dve, s["dve_step"])
            dve.wait_ge(s["loaded_b"], 16 * (3 if gate is not None else 2))
            if gate is not None:
                st.settle(dve.tensor_scalar(gate_row, gate_row, 1.0, None, ALU.add))

            def normalise(t):
                dve.wait_ge(root_ready, t + 1)
                dve.tensor_scalar(m.x_tok[:, t, :], m.x_tok[:, t, :], m.moments[:, t, 0:1], m.cols[:, t:t + 1],
                                  ALU.subtract, ALU.mult).then_inc(scaled, 1)

            for t in range(NT):
                x = m.x_tok[:, t, :]
                y_t = m.mixT[:, t, :]
                if w_out is not None:
                    y_t = banks(m, 2 * (t % 4))
                    dve.wait_ge(y_ready, t + 1)
                if gate is not None:
                    st.settle(dve.tensor_tensor(y[t % 2], y_t, gate_row, ALU.mult))
                    y_t = y[t % 2]
                dve.scalar_tensor_tensor(x, x, ALPHA, y_t, ALU.mult, ALU.add).then_inc(y_taken, 1)
                dve.wait_ge(y_taken, t + 1)
                for half in range(2):
                    last = dve.bn_stats(m.stats[:, t % 2, half, :], x[:, half * HALF:(half + 1) * HALF])
                st.settle(last)
                dve.bn_aggr(m.moments[:, t, :], m.stats[:, t % 2, :, :]).then_inc(var_ready, 1)
                if t:
                    normalise(t - 1)
            dve.wait_ge(var_ready, NT)
            normalise(NT - 1)

        @block.gpsimd
        def _(pool):
            for t in range(NT):
                x = m.x_tok[:, t, :]
                pool.wait_ge(scaled, t + 1)
                pool.tensor_tensor(x, x, g_row, ALU.mult).then_inc(s["pool_step"], 1)
                pool.wait_ge(s["pool_step"], t + 1)
                pool.tensor_tensor(x, x, b_row, ALU.add)
    end_stage(nc, m)


def modulation_stage(nc, m, a):
    s = m.sem
    groups = 6 * D // HALF
    c_rows, c_cols = m.work[0:8, 0:P], m.cols[:, 0:8]
    bias, row = m.work[0:1, SEQ:7 * SEQ], m.work[0:1, 7 * SEQ:13 * SEQ]
    w = [m.mixT[:, 4 * n:4 * n + 4, :].rearrange("p a (b n) -> p (a b) n", n=HALF) for n in range(2)]
    silued, turned, columns, summed, added = (s[f"signal_{n}"] for n in range(5))
    with nc.Fori(0, DEPTH) as l:
        with nc.Block() as block:
            @block.sync
            def _(sp):
                sp.dma_start(c_rows, a["c_2"][0].rearrange("(k p) -> k p", p=P)).then_inc(s["loaded_c"], 16)
                sp.dma_start(bias, a["ada_b_2"][bass.ds(l, 1), :]).then_inc(s["loaded_d"], 16)
                for g in range(groups):
                    if g >= 2:
                        sp.wait_ge(summed, g - 1)
                    src = a["ada_w_2"][bass.ds(l, 1), :, g * HALF:(g + 1) * HALF]
                    sp.dma_start(w[g % 2], src.rearrange("a (k p) n -> p (a k) n", p=P)).then_inc(
                        s["loaded_a" if g % 2 == 0 else "loaded_b"], 16)
                sp.wait_ge(added, groups)
                sp.dma_start(m.mods[bass.ds(l, 1), :], row).then_inc(s["stored"], 16)
                sp.wait_ge(s["stored"], 16)

            @block.scalar
            def _(act):
                act.wait_ge(s["loaded_c"], 16)
                act.activation(c_rows, c_rows, ACT.Silu).then_inc(silued, 1)

            @block.tensor
            def _(pe):
                pe.wait_ge(silued, 1)
                pe.transpose(m.ps[:, 0, 0:8], c_rows, ident(m, 8)).then_inc(turned, 1)
                pe.wait_ge(columns, 1)
                for g in range(groups):
                    pe.wait_ge(s["loaded_a" if g % 2 == 0 else "loaded_b"], 16 * (g // 2 + 1))
                    if g >= 4:
                        pe.wait_ge(added, g - 3)
                    for k in range(NK):
                        last = pe.matmul(m.ps[0:1, 1 + g % 4, :], c_cols[:, k:k + 1], w[g % 2][:, k, :],
                                         start=(k == 0), stop=(k == NK - 1))
                    last.then_inc(summed, 1)

            @block.vector
            def _(dve):
                dve.wait_ge(turned, 1)
                dve.tensor_copy(c_cols, m.ps[:, 0, 0:8]).then_inc(columns, 1)
                dve.wait_ge(s["loaded_d"], 16)
                for g in range(groups):
                    at = slice(g * HALF, (g + 1) * HALF)
                    dve.wait_ge(summed, g + 1)
                    dve.tensor_tensor(row[:, at], m.ps[0:1, 1 + g % 4, :], bias[:, at], ALU.add).then_inc(added, 1)
        end_stage(nc, m)


def modulate_stage(nc, m, shift, scale, store=None):
    s = m.sem
    h = m.work[:, 0:8 * SEQ].rearrange("p (t n) -> p t n", t=NT)
    sc, sh = m.work[:, 8 * SEQ:9 * SEQ], m.work[:, 9 * SEQ:10 * SEQ]
    with nc.Block() as block:
        @block.sync
        def _(sp):
            sp.dma_start(sc, scale.partition_broadcast(P)).then_inc(s["loaded_a"], 16)
            sp.dma_start(sh, shift.partition_broadcast(P)).then_inc(s["loaded_b"], 16)
            sp.wait_ge(s["loaded_a"], 16)
            sp.wait_ge(s["loaded_b"], 16)
            if store is not None:
                for t in range(NT):
                    sp.wait_ge(s["pool_done"], t + 1)
                    sp.dma_start(store[t * P:(t + 1) * P, :], h[:, t, :]).then_inc(s["stored"], 16)
                sp.wait_ge(s["stored"], 16 * NT)

        @block.vector
        def _(dve):
            dve.wait_ge(s["loaded_a"], 16)
            for t in range(NT):
                dve.scalar_tensor_tensor(h[:, t, :], sc, 1.0, m.x_tok[:, t, :], ALU.add,
                                         ALU.mult).then_inc(s["dve_done"], 1)

        @block.gpsimd
        def _(pool):
            pool.wait_ge(s["loaded_b"], 16)
            for t in range(NT):
                pool.wait_ge(s["dve_done"], t + 1)
                pool.tensor_tensor(h[:, t, :], h[:, t, :], sh, ALU.add).then_inc(s["pool_done"], 1)
    end_stage(nc, m)
    return h


HD = 64
GRID = 64
NA_RHO = 14


def attention_steps(nc, m, block, steps, scale, bias):
    s = m.sem
    (s_ready, s_taken, max_ready, p_ready, turned, copied_dve, copied_act, o_ready, o_done, added) = (
        s[f"signal_{n}"] for n in range(10))
    prob = [m.mixT[:, n, :] for n in range(2)]
    probT = [m.mixT[:, 2 + n, :] for n in range(2)]
    neg_max, total, inverse = m.cols[:, 0:32], m.cols[:, 32:64], m.cols2[:, 0:32]

    def pieces(n):
        return [(at, min(P, n - at)) for at in range(0, n, P)]

    @block.tensor
    def _(pe):
        def scores(i):
            q, keys, _, _, n = steps[i]
            if i >= 2:
                pe.wait_ge(s_taken, i - 1)
            for b in range(0, n, HALF):
                w = min(HALF, n - b)
                last = pe.matmul(m.ps[:, 2 * (i % 2) + b // HALF, 0:w], q, keys[:, b:b + w], start=True, stop=True)
            last.then_inc(s_ready, 1)

        def turn(i):
            n = steps[i][4]
            pe.wait_ge(p_ready, i + 1)
            if i:
                pe.wait_ge(copied_dve, i)
                pe.wait_ge(copied_act, i)
            for at, w in pieces(n):
                last = pe.transpose(banks(m, 4)[0:w, at:at + P], prob[i % 2][:, at:at + w], ident(m))
            last.then_inc(turned, 1)

        def weigh(i):
            n = steps[i][4]
            pe.wait_ge(copied_dve, i + 1)
            pe.wait_ge(copied_act, i + 1)
            if i >= 2:
                pe.wait_ge(o_done, i - 1)
            values = steps[i][2]
            for b, (at, w) in enumerate(pieces(n)):
                last = pe.matmul(m.ps[:, 6 + i % 2, 0:HD], probT[i % 2][0:w, at:at + P], values[b],
                                 start=(b == 0), stop=(b == len(pieces(n)) - 1))
            last.then_inc(o_ready, 1)

        scores(0)
        for i in range(len(steps)):
            if i + 1 < len(steps):
                scores(i + 1)
            turn(i)
            if i:
                weigh(i - 1)
        weigh(len(steps) - 1)

    @block.scalar
    def _(act):
        def copy_out(i):
            n = steps[i][4]
            act.wait_ge(turned, i + 1)
            if i >= 2:
                act.wait_ge(o_ready, i - 1)
            act.copy(probT[i % 2][:, 0:HALF], m.ps[:, 4, :]).then_inc(copied_act, 1)

        for i in range(len(steps)):
            n = steps[i][4]
            act.wait_ge(max_ready, i + 1)
            src = prob[i % 2][:, 0:n] if bias else banks(m, 2 * (i % 2))[:, 0:n]
            if i >= 2:
                act.wait_ge(turned, i - 1)
            ins = act.activation(prob[i % 2][:, 0:n], src, ACT.Exp, bias=neg_max[:, i:i + 1], scale=scale,
                                 accum_out=total[:, i:i + 1])
            ins.then_inc(p_ready, 1)
            if not bias:
                act.wait_ge(p_ready, i + 1)
                act.sem_inc(s_taken, 1)
            if i:
                copy_out(i - 1)
        copy_out(len(steps) - 1)

    @block.vector
    def _(dve):
        def copy_out(i):
            n = steps[i][4]
            dve.wait_ge(turned, i + 1)
            if i >= 2:
                dve.wait_ge(o_ready, i - 1)
            if n > HALF:
                rows = P if (n - HALF) % P == 0 else (n - HALF) % P
                dve.tensor_copy(probT[i % 2][0:rows, HALF:HALF + (n - HALF + P - 1) // P * P],
                                m.ps[0:rows, 5, 0:(n - HALF + P - 1) // P * P]).then_inc(copied_dve, 1)
            else:
                dve.sem_inc(copied_dve, 1)

        def finish(i):
            dve.wait_ge(p_ready, i + 1)
            dve.reciprocal(inverse[:, i:i + 1], total[:, i:i + 1]).then_inc(s["dve_step"], 1)
            dve.wait_ge(s["dve_step"], i + 1)
            dve.wait_ge(o_ready, i + 1)
            dve.tensor_scalar(steps[i][3], m.ps[:, 6 + i % 2, 0:HD], inverse[:, i:i + 1], None,
                              ALU.mult).then_inc(o_done, 1)

        for i in range(len(steps)):
            n = steps[i][4]
            dve.wait_ge(s_ready, i + 1)
            src = banks(m, 2 * (i % 2))[:, 0:n]
            if bias:
                if i >= 2:
                    dve.wait_ge(turned, i - 1)
                src = prob[i % 2][:, 0:n]
                dve.tensor_tensor(src, banks(m, 2 * (i % 2))[:, 0:n], bias[i], ALU.add).then_inc(s_taken, 1)
                dve.wait_ge(s_taken, i + 1)
            dve.tensor_reduce(neg_max[:, i:i + 1], src, AX.X, ALU.max, negate=True).then_inc(added, 1)
            dve.wait_ge(added, i + 1)
            dve.tensor_scalar(neg_max[:, i:i + 1], neg_max[:, i:i + 1], scale, None, ALU.mult).then_inc(max_ready, 1)
            if i:
                copy_out(i - 1)
            if i >= 2:
                finish(i - 2)
        copy_out(len(steps) - 1)
        for i in range(len(steps) - 2, len(steps)):
            finish(i)


def relative_bias_stage(nc, m, a):
    s = m.sem
    rows = m.work[0:120, 0:2 * P].rearrange("p (j n) -> p j n", j=2)
    table = a["na_rpb_2"][0].rearrange("h r c -> (h r) c").rearrange("(j p) c -> p j c", p=120)
    with nc.Block() as block:
        @block.vector
        def _(dve):
            dve.memset(rows, 0.0).then_inc(s["dve_done"], 1)

        @block.sync
        def _(sp):
            sp.wait_ge(s["dve_done"], 1)
            sp.dma_start(rows[:, :, 48:48 + 31], table).then_inc(s["loaded_a"], 16)
            sp.wait_ge(s["loaded_a"], 16)
            with sp.Fori(0, GRID) as i:
                dst = m.bias_dram[bass.ds((GRID - 1) - i, 1), :, :]
                sp.dma_start(dst.rearrange("a (j p) k -> p (a j) k", p=120),
                             rows[:, :, bass.ds(i, GRID)]).then_inc(s["stored"], 16)
            sp.wait_ge(s["stored"], 16 * GRID)
    end_stage(nc, m)


def neighbourhood_pair(nc, m, a, pair, o_tok):
    s = m.sem
    W = [m.work[:, n * SEQ:(n + 1) * SEQ] for n in range(12)]
    wt = [W[n].rearrange("p (k n) -> p k n", k=NK) for n in range(3)]
    qT, kT = W[3], W[4]
    v_tok = W[5].rearrange("p (t n) -> p t n", t=NT)
    full = [W[6 + n][:, 0:NA_RHO * GRID].rearrange("p (r k) -> p r k", k=GRID) for n in range(2)]
    inner = [W[8 + n][:, 0:9 * GRID].rearrange("p (r k) -> p r k", k=GRID) for n in range(2)]
    projected, masked = s["signal_0"], s["signal_1"]
    loads = [s[f"loaded_{x}"] for x in "abc"]
    with nc.Block() as block:
        @block.sync
        def _(sp):
            for j in range(3):
                load_columns(sp, wt[j], a["na_w_qkv_2"][0], pair * P + j * D, P, loads[j])
            for head in range(2):
                for row in range(2):
                    sp.dma_start(full[head][64 * row:64 * row + 64, :, :],
                                 m.bias_dram[:, bass.ds(pair * 30 + (head * 15 + 1 - row), NA_RHO), :]).then_inc(
                                     s["loaded_d"], 16)
            for j in range(3):
                sp.wait_ge(loads[j], 16)
            sp.wait_ge(s["loaded_d"], 64)

        @block.tensor
        def _(pe):
            for j in range(2):
                pe.wait_ge(loads[j], 16)
                project_T(pe, m, wt[j], 2 * j).then_inc(projected, 1)
            pe.wait_ge(loads[2], 16)
            for t in range(NT):
                for k in range(NK):
                    last = pe.matmul(banks(m, 4)[:, t * P:(t + 1) * P], m.xT[:, k, t * P:(t + 1) * P],
                                     wt[2][:, k, :], start=(k == 0), stop=(k == NK - 1))
            last.then_inc(projected, 1)

        @block.scalar
        def _(act):
            act.wait_ge(projected, 1)
            act.mul(qT, banks(m, 0), HD ** -0.5)
            act.wait_ge(projected, 2)
            act.copy(kT, banks(m, 2))
            act.wait_ge(projected, 3)
            act.copy(W[5], banks(m, 4))

        @block.vector
        def _(dve):
            dve.wait_ge(s["loaded_d"], 64)
            for head in range(2):
                dve.tensor_tensor(full[head], full[head], each_chunk(m.const[:, K_COLS:K_COLS + GRID], NA_RHO),
                                  ALU.add).then_inc(masked, 1)
                dve.wait_ge(masked, head + 1)
                dve.tensor_tensor(inner[head], full[head][:, 2:11, :],
                                  spread(m.const[:, K_ROWS:K_ROWS + 9], GRID), ALU.add)
    end_stage(nc, m)
    steps, bias = [], []
    for head in range(2):
        rows = slice(64 * head, 64 * head + 64)
        for t in range(NT):
            first = min(max(2 * t - 4, 0), 8)
            n_rows = 9 if 2 <= t <= 5 else 8
            keys = kT[rows, first * GRID:(first + n_rows) * GRID]
            values = [v_tok[0:min(P, n_rows * GRID - b * P), first // 2 + b, rows]
                      for b in range((n_rows + 1) // 2)]
            steps.append((qT[rows, t * P:(t + 1) * P], keys, values,
                          o_tok[:, t, bass.ds(pair * P + head * HD, HD)], n_rows * GRID))
            tile = inner[head] if n_rows == 9 else full[head][:, first - 2 * t + 6:first - 2 * t + 14, :]
            bias.append(tile.rearrange("p r k -> p (r k)"))
    with nc.Block() as block:
        attention_steps(nc, m, block, steps, 1.0, bias)
    end_stage(nc, m)


KV_HEADS, GROUP = 4, 4
ROPE_HALF = 16


def rope_table():
    t = np.arange(SEQ, dtype=np.int32)
    pos = np.stack([t // GRID, t % GRID], axis=-1).astype(np.float32)
    inv_freq = np.float32(10000.0) ** (-np.arange(ROPE_HALF, dtype=np.float32) / ROPE_HALF)
    angle = (pos[:, :, None] * inv_freq).reshape(SEQ, 2 * ROPE_HALF)
    return np.concatenate([np.cos(angle), np.sin(angle)], axis=1).astype(np.float32)


def grouped_query_group(nc, m, a, g, o_tok):
    s = m.sem
    W = [m.work[:, n * SEQ:(n + 1) * SEQ] for n in range(12)]
    WIDE = (GROUP + 2) * HD
    w = m.work[:, 0:3 * SEQ].rearrange("p (k n) -> p k n", k=NK)
    raw = m.work[:, 3 * SEQ:6 * SEQ].rearrange("p (t n) -> p t n", t=NT)
    n_norm = GROUP + 1
    square = m.work[:, 6 * SEQ:6 * SEQ + NT * n_norm * HD]
    q2, k2, v_tok = (W[6], W[7]), W[8], W[9][:, 0:NT * HD].rearrange("p (t n) -> p t n", t=NT)
    gain_q, gain_k = W[10][:, 0:HD], W[10][:, HD:2 * HD]
    rope = W[10][:, 512:1024].rearrange("p (t n) -> p t n", t=NT)
    heads = raw[:, :, 0:n_norm * HD].rearrange("p t (h d) -> p t h d", d=HD)
    part = [x[:, 0:NT * n_norm * ROPE_HALF].rearrange("p (t h d) -> p t h d", t=NT, h=n_norm)
            for x in (W[6], W[7], W[8], W[11])]
    root = m.cols2[:, 0:NT * n_norm]
    projected, evicted, squared, summed, rooted, roped, turned = (s[f"signal_{n}"] for n in range(7))
    with nc.Block() as block:
        @block.sync
        def _(sp):
            wq = a["gqa_w_qkv_2"][0]
            for dst, column, n in ((slice(0, 4 * HD), g * 4 * HD, 4 * HD),
                                   (slice(4 * HD, 5 * HD), g * HD + D, HD),
                                   (slice(5 * HD, 6 * HD), g * HD + (D + KV_HEADS * HD), HD)):
                load_columns(sp, w[:, :, dst], wq, column, n, s["loaded_a"])
            sp.dma_start(gain_q, a["gqa_q_norm_2"][0].partition_broadcast(P)).then_inc(s["loaded_b"], 16)
            sp.dma_start(gain_k, a["gqa_k_norm_2"][0].partition_broadcast(P)).then_inc(s["loaded_b"], 16)
            sp.dma_start(rope, a["rope"].rearrange("(t p) n -> p t n", p=P)).then_inc(s["loaded_b"], 16)
            sp.wait_ge(s["loaded_a"], 48)
            sp.wait_ge(s["loaded_b"], 48)

        @block.tensor
        def _(pe):
            pe.wait_ge(s["loaded_a"], 48)
            for t in range(NT):
                for k in range(NK):
                    last = pe.matmul(m.ps[:, t, 0:WIDE], m.xT[:, k, t * P:(t + 1) * P], w[:, k, :],
                                     start=(k == 0), stop=(k == NK - 1))
                last.then_inc(projected, 1)
            pe.wait_ge(roped, 1)
            for j in range(3):
                for t in range(NT):
                    last = pe.transpose(banks(m, 2 * j)[:, t * P:(t + 1) * P], raw[:, t, j * P:(j + 1) * P], ident(m))
                last.then_inc(turned, 1)

        @block.scalar
        def _(act):
            st = Steps(act, s["act_step"])
            for t in range(NT):
                act.wait_ge(projected, t + 1)
                act.copy(raw[:, t, :], m.ps[:, t, 0:WIDE]).then_inc(evicted, 1)
            act.wait_ge(evicted, NT)
            act.activation(square.rearrange("p (t n) -> p t n", t=NT), raw[:, :, 0:n_norm * HD],
                           ACT.Square).then_inc(squared, 1)
            act.wait_ge(summed, 1)
            st.settle(act.activation(root, root, ACT.Ln, bias=m.eps6[:], scale=1.0 / HD))
            act.activation(root, root, ACT.Exp, scale=-0.5).then_inc(rooted, 1)
            for j, dst in enumerate((q2[0], q2[1], k2)):
                act.wait_ge(turned, j + 1)
                act.copy(dst, banks(m, 2 * j))

        @block.vector
        def _(dve):
            st = Steps(dve, s["dve_step"])
            dve.wait_ge(s["loaded_b"], 48)
            dve.wait_ge(squared, 1)
            dve.tensor_reduce(root, square.rearrange("p (h d) -> p h d", d=HD), AX.X, ALU.add).then_inc(summed, 1)
            dve.tensor_copy(v_tok, raw[:, :, 5 * HD:6 * HD])
            dve.wait_ge(rooted, 1)
            spread_root = root.rearrange("p (t h) -> p t h", t=NT).unsqueeze(3).to_broadcast([P, NT, n_norm, HD])
            st.settle(dve.tensor_tensor(heads, heads, spread_root, ALU.mult))
            for at, gain, n in ((slice(0, GROUP), gain_q, GROUP), (slice(GROUP, n_norm), gain_k, 1)):
                last = dve.tensor_tensor(heads[:, :, at, :], heads[:, :, at, :],
                                         gain.unsqueeze(1).unsqueeze(1).to_broadcast([P, NT, n, HD]), ALU.mult)
            st.settle(last)
            for axis in range(2):
                x1 = heads[:, :, :, axis * 32:axis * 32 + 16]
                x2 = heads[:, :, :, axis * 32 + 16:axis * 32 + 32]
                cos, sin = (rope[:, :, f * 32 + axis * 16:f * 32 + axis * 16 + 16].unsqueeze(2).to_broadcast(
                    [P, NT, n_norm, ROPE_HALF]) for f in range(2))
                dve.tensor_tensor(part[0], x1, cos, ALU.mult)
                dve.tensor_tensor(part[1], x2, sin, ALU.mult)
                dve.tensor_tensor(part[2], x2, cos, ALU.mult)
                st.settle(dve.tensor_tensor(part[3], x1, sin, ALU.mult))
                dve.tensor_tensor(x1, part[0], part[1], ALU.subtract)
                st.settle(dve.tensor_tensor(x2, part[2], part[3], ALU.add))
            dve.tensor_copy(raw[:, :, 5 * HD:6 * HD], raw[:, :, 4 * HD:5 * HD]).then_inc(roped, 1)
    end_stage(nc, m)
    steps = []
    for head in range(GROUP):
        rows = slice(64 * (head % 2), 64 * (head % 2) + 64)
        for t in range(NT):
            steps.append((q2[head // 2][rows, t * P:(t + 1) * P], k2[rows, :],
                          [v_tok[:, b, :] for b in range(NT)],
                          o_tok[:, t, bass.ds(g * (GROUP * HD) + head * HD, HD)], SEQ))
    with nc.Block() as block:
        attention_steps(nc, m, block, steps, HD ** -0.5, None)
    end_stage(nc, m)


N_GROUPS, PER_GROUP, N_EXPERTS, D_EXPERT, TOP_K = 4, 8, 32, 512, 2
OVERFLOW = SEQ * TOP_K // P
N_BLOCKS = N_EXPERTS + OVERFLOW
MAX_MORE = NT - 1


def route_stage(nc, m, a, l):
    s = m.sem
    NL = N_GROUPS + N_EXPERTS
    base = 8 * SEQ
    at = [base]

    def take(*shape):
        n = int(np.prod(shape))
        view = m.work[:, at[0]:at[0] + n]
        at[0] += n
        if len(shape) == 2:
            view = view.rearrange("p (a b) -> p a b", b=shape[1])
        return view

    w, bias, logits = take(NK, NL), take(NL), take(NT, NL)
    padded, top_g, top_e, chosen, tmp8 = (take(NT, 8) for _ in range(5))
    index = take(NT, 8).bitcast(U32)
    g_id, e_loc, e_id, first, prob, e2, den = (take(NT, 2) for _ in range(7))
    onehot_g = take(NT, N_GROUPS)
    hot = [take(NT, N_EXPERTS) for _ in range(2)]
    both, rank, over_q, slot, tmp = (take(NT, N_EXPERTS) for _ in range(5))
    counts, more, ends, starts = (take(N_EXPERTS) for _ in range(4))
    compare = take(OVERFLOW, N_EXPERTS)
    ids = take(OVERFLOW)
    iota = m.const[:, K_IOTA:K_IOTA + N_EXPERTS]
    table_zero = take(N_BLOCKS).bitcast(I32)
    tokens = take(NT).bitcast(I32)
    summed, hot_ready, ranked, exp_in, exp_out, dest_ready, table_clear = (s[f"signal_{n}"] for n in range(7))
    with nc.Block() as block:
        @block.sync
        def _(sp):
            sp.dma_start(w[:, :, 0:N_GROUPS], a["moe_w_group_2"][l].rearrange("(k p) n -> p k n", p=P)).then_inc(
                s["loaded_a"], 16)
            sp.dma_start(w[:, :, N_GROUPS:NL], a["moe_w_expert_2"][l].rearrange("(k p) n -> p k n", p=P)).then_inc(
                s["loaded_a"], 16)
            sp.dma_start(bias[:, 0:N_GROUPS], a["moe_b_group_2"][l].partition_broadcast(P)).then_inc(s["loaded_b"], 16)
            sp.dma_start(bias[:, N_GROUPS:NL], a["moe_b_expert_2"][l].partition_broadcast(P)).then_inc(s["loaded_b"], 16)
            sp.wait_ge(s["loaded_b"], 32)
            sp.wait_ge(s["pool_step"], 1)
            sp.dma_start(m.slot_token.rearrange("(p b) o -> p (b o)", p=P), table_zero).then_inc(table_clear, 16)
            sp.wait_ge(table_clear, 16)
            sp.wait_ge(m.pool_dma[l]["scattered"], 16 * TOP_K * NT)
            sp.dma_start(m.slots[:], m.slot_token.rearrange("(p b) o -> p (b o)", p=P)).then_inc(s["loaded_c"], 16)
            sp.wait_ge(s["loaded_c"], 16)

        @block.tensor
        def _(pe):
            pe.wait_ge(s["loaded_a"], 32)
            for t in range(NT):
                for k in range(NK):
                    last = pe.matmul(m.ps[:, 0, t * NL:(t + 1) * NL], m.xT[:, k, t * P:(t + 1) * P], w[:, k, :],
                                     start=(k == 0), stop=(k == NK - 1))
            last.then_inc(summed, 1)
            pe.wait_ge(hot_ready, 1)
            for t in range(NT):
                out = m.ps[:, 1, t * N_EXPERTS:(t + 1) * N_EXPERTS]
                for b in range(t):
                    pe.matmul(out, ones(m), both[:, b, :], start=(b == 0), stop=False)
                pe.matmul(out, m.const[:, K_STRICT:K_STRICT + P], both[:, t, :], start=(t == 0), stop=True)
            for b in range(NT):
                last = pe.matmul(m.ps[:, 2, 0:N_EXPERTS], ones(m), both[:, b, :], start=(b == 0), stop=(b == NT - 1))
            last.then_inc(ranked, 1)

        @block.scalar
        def _(act):
            for n in range(2):
                act.wait_ge(exp_in, n + 1)
                dst = tmp8[:, :, 0:N_GROUPS] if n == 0 else e2[:, :, 0:1]
                act.activation(dst, dst, ACT.Exp).then_inc(exp_out, 1)

        @block.gpsimd
        def _(pool):
            pool.memset(table_zero, 0).then_inc(s["pool_step"], 1)
            pool.iota(tokens, pattern=[[P, NT]], base=0, channel_multiplier=1).then_inc(s["pool_step"], 1)
            pool.wait_ge(s["pool_step"], 2)
            pool.wait_ge(table_clear, 16)
            pool.wait_ge(dest_ready, 1)
            for t in range(NT):
                for c in range(TOP_K):
                    pool.indirect_dma_start(
                        m.slot_token, bass.IndirectOffsetOnAxis(m.dest[:, c, t:t + 1], 0),
                        tokens[:, t:t + 1], None).then_inc(m.pool_dma[l]["scattered"], 16)

        @block.vector
        def _(dve):
            st = Steps(dve, s["dve_step"])
            do = st.settle
            dve.wait_ge(s["loaded_b"], 32)
            do(dve.memset(padded, NEG))
            dve.wait_ge(summed, 1)
            do(dve.tensor_tensor(logits, m.ps[:, 0, 0:NT * NL].rearrange("p (t n) -> p t n", t=NT),
                                 each_chunk(bias), ALU.add))
            do(dve.tensor_copy(padded[:, :, 0:N_GROUPS], logits[:, :, 0:N_GROUPS]))
            for t in range(NT):
                do(dve.max(top_g[:, t, :], padded[:, t, :]))
                do(dve.max_index(index[:, t, :], top_g[:, t, :], padded[:, t, :]))
            dve.tensor_tensor(tmp8[:, :, 0:N_GROUPS], padded[:, :, 0:N_GROUPS],
                              top_g[:, :, 0:1].to_broadcast([P, NT, N_GROUPS]), ALU.subtract).then_inc(exp_in, 1)
            do(dve.tensor_copy(g_id[:, :, 0:1], index[:, :, 0:1]))
            do(dve.tensor_tensor(onehot_g, each_chunk(iota[:, 0:N_GROUPS]),
                                 g_id[:, :, 0:1].to_broadcast([P, NT, N_GROUPS]), ALU.is_equal))
            for g in range(N_GROUPS):
                part = logits[:, :, N_GROUPS + g * PER_GROUP:N_GROUPS + (g + 1) * PER_GROUP]
                mask = onehot_g[:, :, g:g + 1].to_broadcast([P, NT, PER_GROUP])
                if g == 0:
                    do(dve.tensor_tensor(chosen, part, mask, ALU.mult))
                else:
                    do(dve.tensor_tensor(top_e, part, mask, ALU.mult))
                    do(dve.tensor_tensor(chosen, chosen, top_e, ALU.add))
            for t in range(NT):
                do(dve.max(top_e[:, t, :], chosen[:, t, :]))
                do(dve.max_index(index[:, t, :], top_e[:, t, :], chosen[:, t, :]))
            do(dve.tensor_copy(e_loc, index[:, :, 0:2]))
            do(dve.scalar_tensor_tensor(e_id, g_id[:, :, 0:1].to_broadcast([P, NT, 2]), float(PER_GROUP), e_loc,
                                        ALU.mult, ALU.add))
            dve.tensor_tensor(e2[:, :, 0:1], top_e[:, :, 1:2], top_e[:, :, 0:1], ALU.subtract).then_inc(exp_in, 1)
            for c in range(TOP_K):
                last = dve.tensor_tensor(hot[c], each_chunk(iota), e_id[:, :, c:c + 1].to_broadcast(
                    [P, NT, N_EXPERTS]), ALU.is_equal)
            do(last)
            dve.tensor_tensor(both, hot[0], hot[1], ALU.add).then_inc(hot_ready, 1)
            dve.wait_ge(exp_out, 2)
            do(dve.tensor_reduce(prob[:, :, 0:1], tmp8[:, :, 0:N_GROUPS], AX.X, ALU.add))
            do(dve.tensor_scalar(den[:, :, 0:1], e2[:, :, 0:1], 1.0, None, ALU.add))
            do(dve.tensor_tensor(den[:, :, 0:1], den[:, :, 0:1], prob[:, :, 0:1], ALU.mult))
            do(dve.reciprocal(first[:, :, 0:1], den[:, :, 0:1]))
            dve.tensor_copy(m.gates[:, :, 0:1], first[:, :, 0:1])
            do(dve.tensor_tensor(m.gates[:, :, 1:2], first[:, :, 0:1], e2[:, :, 0:1], ALU.mult))
            dve.wait_ge(ranked, 1)
            do(dve.tensor_copy(counts, m.ps[:, 2, 0:N_EXPERTS]))
            do(dve.tensor_copy(rank, m.ps[:, 1, 0:NT * N_EXPERTS].rearrange("p (t n) -> p t n", t=NT)))
            do(dve.tensor_scalar(more, counts, float(P), None, ALU.is_gt))
            do(dve.tensor_scalar(over_q, rank, float(P), None, ALU.is_ge))
            for q in range(2, MAX_MORE + 1):
                do(dve.scalar_tensor_tensor(more, counts, float(P * q), more, ALU.is_gt, ALU.add))
                do(dve.scalar_tensor_tensor(over_q, rank, float(P * q), over_q, ALU.is_ge, ALU.add))
            do(dve.tensor_tensor_scan(ends, ones(m)[:, 0:N_EXPERTS], more, 0.0, ALU.mult, ALU.add))
            do(dve.tensor_tensor(starts, ends, more, ALU.subtract))
            do(dve.scalar_tensor_tensor(starts, starts, float(N_EXPERTS - 1), iota, ALU.add, ALU.subtract))
            do(dve.tensor_tensor(tmp, over_q, each_chunk(starts), ALU.add))
            do(dve.tensor_scalar(slot, over_q, 0.0, None, ALU.is_gt))
            do(dve.tensor_tensor(slot, slot, tmp, ALU.mult))
            do(dve.tensor_tensor(slot, slot, each_chunk(iota), ALU.add))
            do(dve.scalar_tensor_tensor(tmp, over_q, -float(P), rank, ALU.mult, ALU.add))
            do(dve.scalar_tensor_tensor(slot, tmp, float(N_BLOCKS), slot, ALU.mult, ALU.add))
            for c in range(TOP_K):
                do(dve.tensor_tensor(tmp, slot, hot[c], ALU.mult))
                do(dve.tensor_reduce(first[:, :, c:c + 1], tmp, AX.X, ALU.add))
                last = dve.tensor_copy(m.dest[:, c, :], first[:, :, c:c + 1].rearrange("p t o -> p (t o)"))
            do(last)
            do(dve.tensor_tensor(compare, ends.unsqueeze(1).to_broadcast([P, OVERFLOW, N_EXPERTS]),
                                 spread(m.const[:, K_IOTA:K_IOTA + OVERFLOW], N_EXPERTS), ALU.is_le))
            do(dve.tensor_reduce(ids, compare, AX.X, ALU.add))
            do(dve.tensor_scalar(ids, ids, float(N_EXPERTS - 1), None, ALU.min))
            dve.tensor_copy(m.overflow[:, 0:OVERFLOW], ids)
            do(dve.tensor_copy(m.overflow[:, OVERFLOW:OVERFLOW + 1], ends[:, N_EXPERTS - 1:N_EXPERTS]))
            dve.sem_inc(dest_ready, 1)
    end_stage(nc, m)


def expert_buffers(m):
    mix, xT, work = (t.rearrange("p a n -> p (a n)") for t in (m.mixT[:], m.xT[:], m.work[:].unsqueeze(1)))
    k8 = lambda v: v.rearrange("p (k n) -> p k n", n=D_EXPERT)
    k4 = lambda v: v.rearrange("p (k n) -> p k n", n=D)
    gate = [k8(work[:, 0:4096]), k8(mix[:, 0:4096])]
    up = [k8(work[:, 4096:8192]), k8(mix[:, 4096:8192])]
    down = [k4(work[:, 8192:12288]), k4(xT[:, 0:4096])]
    x = [xT[:, 4096:5120], xT[:, 5120:6144]]
    x_turned = [xT[:, 6144:7168], xT[:, 7168:8192]]
    act = [work[:, 12288 + n * 1024:12288 + n * 1024 + 512] for n in range(2)]
    act_turned = [work[:, 12800 + n * 1024:13312 + n * 1024] for n in range(2)]
    y = [work[:, 14336 + n * 1024:15360 + n * 1024] for n in range(2)]
    b = Places()
    b.gate, b.up, b.down, b.x, b.x_turned, b.act, b.act_turned, b.y = (
        gate, up, down, x, x_turned, act, act_turned, y)
    return b


def load_expert(sp, m, a, l, buffers, n, expert, semaphore):
    for dst, w, k in ((buffers.gate[n], a["moe_w_gate_2"], 8), (buffers.up[n], a["moe_w_up_2"], 8),
                      (buffers.down[n], a["moe_w_down_2"], 4)):
        sp.dma_start(dst, w[l, bass.ds(expert, 1)].rearrange("a (k p) n -> p (a k) n", p=P)).then_inc(semaphore, 16)


def gather_tokens(pool, m, buffers, n, column, copied, copied_count, gathered):
    pool.tensor_copy(m.index[:, n:n + 1], column).then_inc(copied, 1)
    pool.wait_ge(copied, copied_count)
    pool.indirect_dma_start(buffers.x[n], None, m.h_dram,
                            bass.IndirectOffsetOnAxis(m.index[:, n:n + 1], 0)).then_inc(gathered, 16)


def expert_engines(nc, m, block, b, n_blocks, loaded, gathered):
    s = m.sem
    x_turned, x_copied, up_ready, silued, multiplied, h_turned, h_copied, y_ready, y_copied = (
        s[f"signal_{n}"] for n in range(9))

    @block.tensor
    def _(pe):
        def turn_x(n):
            if gathered[n]:
                pe.wait_ge(*gathered[n])
            for k in range(NK):
                last = pe.transpose(banks(m, 0)[:, k * P:(k + 1) * P], b.x[n][:, k * P:(k + 1) * P], ident(m))
            last.then_inc(x_turned, 1)

        def gate_up(n):
            if loaded[n]:
                pe.wait_ge(*loaded[n])
            pe.wait_ge(x_copied, 2 * (n + 1))
            for w, bank in ((b.gate[n], 2), (b.up[n], 3)):
                if n:
                    pe.wait_ge(multiplied, n)
                for k in range(NK):
                    last = pe.matmul(m.ps[:, bank, :], b.x_turned[n][:, k * P:(k + 1) * P], w[:, k, :],
                                     start=(k == 0), stop=(k == NK - 1))
                last.then_inc(up_ready, 1)

        def down(n):
            pe.wait_ge(multiplied, n + 1)
            for k in range(4):
                last = pe.transpose(m.ps[:, 4, k * P:(k + 1) * P], b.act[n][:, k * P:(k + 1) * P], ident(m))
            last.then_inc(h_turned, 1)
            pe.wait_ge(h_copied, n + 1)
            for half in range(2):
                for k in range(4):
                    last = pe.matmul(m.ps[:, 5 + half, :], b.act_turned[n][:, k * P:(k + 1) * P],
                                     b.down[n][:, k, half * HALF:(half + 1) * HALF], start=(k == 0), stop=(k == 3))
                last.then_inc(y_ready, 1)

        turn_x(0)
        gate_up(0)
        if n_blocks == 2:
            turn_x(1)
        down(0)
        if n_blocks == 2:
            gate_up(1)
            pe.wait_ge(y_copied, 2)
            down(1)

    @block.scalar
    def _(act):
        def copy_x(n):
            act.wait_ge(x_turned, n + 1)
            act.copy(b.x_turned[n][:, 0:HALF], m.ps[:, 0, :]).then_inc(x_copied, 1)

        copy_x(0)
        for n in range(n_blocks):
            act.wait_ge(up_ready, 2 * n + 1)
            act.activation(b.act[n], m.ps[:, 2, :], ACT.Silu).then_inc(silued, 1)
            if n + 1 < n_blocks:
                copy_x(n + 1)
            act.wait_ge(h_turned, n + 1)
            act.copy(b.act_turned[n], m.ps[:, 4, :]).then_inc(h_copied, 1)
            act.wait_ge(y_ready, 2 * n + 2)
            act.copy(b.y[n][:, HALF:D], m.ps[:, 6, :]).then_inc(y_copied, 1)

    @block.vector
    def _(dve):
        def copy_x(n):
            dve.wait_ge(x_turned, n + 1)
            dve.tensor_copy(b.x_turned[n][:, HALF:D], m.ps[:, 1, :]).then_inc(x_copied, 1)

        copy_x(0)
        for n in range(n_blocks):
            dve.wait_ge(up_ready, 2 * n + 2)
            dve.wait_ge(silued, n + 1)
            dve.tensor_tensor(b.act[n], b.act[n], m.ps[:, 3, :], ALU.mult).then_inc(multiplied, 1)
            if n + 1 < n_blocks:
                copy_x(n + 1)
            dve.wait_ge(y_ready, 2 * n + 1)
            dve.tensor_copy(b.y[n][:, 0:HALF], m.ps[:, 5, :]).then_inc(y_copied, 1)


def following(e):
    return (e + 2) % N_EXPERTS


def experts_stage(nc, m, a, l):
    s = m.sem
    b = expert_buffers(m)
    y_blocks = m.y_dram.rearrange("(p b) d -> p b d", p=P)
    x_turned, y_ready, y_copied, tokens_ready = s["signal_0"], s["signal_7"], s["signal_8"], s["signal_9"]
    gathered_a, gathered_b = m.pool_dma[l]["gathered_a"], m.pool_dma[l]["gathered_b"]
    with nc.Block() as block:
        @block.sync
        def _(sp):
            load_expert(sp, m, a, l, b, 0, 0, s["loaded_a"])
            sp.wait_ge(s["loaded_a"], 48)

        @block.gpsimd
        def _(pool):
            gather_tokens(pool, m, b, 0, m.slots[:, 0:1], s["pool_step"], 1, gathered_a)
            pool.wait_ge(gathered_a, 16)
    end_stage(nc, m)
    with nc.Fori(0, N_EXPERTS // 2) as pair:
        e = pair * 2
        with nc.Block() as block:
            @block.sync
            def _(sp):
                load_expert(sp, m, a, l, b, 1, e + 1, s["loaded_b"])
                sp.wait_ge(y_ready, 2)
                load_expert(sp, m, a, l, b, 0, following(e), s["loaded_a"])
                for n in range(2):
                    sp.wait_ge(y_copied, 2 * n + 2)
                    sp.dma_start(y_blocks[:, bass.ds(e + n, 1), :], b.y[n].unsqueeze(1)).then_inc(s["stored"], 16)
                sp.wait_ge(s["loaded_a"], 48)
                sp.wait_ge(s["loaded_b"], 48)
                sp.wait_ge(s["stored"], 32)

            @block.gpsimd
            def _(pool):
                gather_tokens(pool, m, b, 1, m.slots[:, bass.ds(e + 1, 1)], s["pool_step"], 1, gathered_b)
                pool.wait_ge(gathered_b, (pair + 1) * 16)
                pool.sem_inc(tokens_ready, 1)
                pool.wait_ge(x_turned, 1)
                gather_tokens(pool, m, b, 0, m.slots[:, bass.ds(following(e), 1)], s["pool_step"], 2,
                              gathered_a)
                pool.wait_ge(gathered_a, (pair + 2) * 16)

            expert_engines(nc, m, block, b, 2, [None, (s["loaded_b"], 48)],
                           [None, (tokens_ready, 1)])
        end_stage(nc, m)
    overflow_blocks = nc.values_load(m.overflow[0:1, OVERFLOW:OVERFLOW + 1], min_val=0, max_val=OVERFLOW)
    with nc.Fori(0, OVERFLOW) as o:
        with nc.If(overflow_blocks > o):
            with nc.Block() as block:
                @block.sync
                def _(sp):
                    expert = sp.value_load(m.overflow[0:1, bass.ds(o, 1)], min_val=0, max_val=N_EXPERTS - 1)
                    load_expert(sp, m, a, l, b, 0, expert, s["loaded_a"])
                    sp.wait_ge(y_copied, 2)
                    sp.dma_start(y_blocks[:, bass.ds(o + N_EXPERTS, 1), :], b.y[0].unsqueeze(1)).then_inc(s["stored"], 16)
                    sp.wait_ge(s["loaded_a"], 48)
                    sp.wait_ge(s["stored"], 16)

                @block.gpsimd
                def _(pool):
                    gather_tokens(pool, m, b, 0, m.slots[:, bass.ds(o + N_EXPERTS, 1)], s["pool_step"], 1,
                                  m.pool_dma[l]["gathered_more"])
                    pool.wait_ge(m.pool_dma[l]["gathered_more"], (o + 1) * 16)
                    pool.sem_inc(tokens_ready, 1)

                expert_engines(nc, m, block, b, 1, [(s["loaded_a"], 48)], [(tokens_ready, 1)])
            end_stage(nc, m)


def combine_stage(nc, m, l):
    s = m.sem
    y = [[m.work[:, (13 + 2 * n + c) * SEQ:(14 + 2 * n + c) * SEQ] for c in range(2)] for n in range(2)]
    weighted = s["signal_0"]
    done = [m.pool_dma[l]["combined_a"], m.pool_dma[l]["combined_b"]]
    with nc.Block() as block:
        @block.gpsimd
        def _(pool):
            for t in range(NT):
                if t >= 2:
                    pool.wait_ge(weighted, t - 1)
                for c in range(TOP_K):
                    pool.indirect_dma_start(y[t % 2][c], None, m.y_dram, bass.IndirectOffsetOnAxis(
                        m.dest[:, c, t:t + 1], 0)).then_inc(done[t % 2], 16)

        @block.vector
        def _(dve):
            st = Steps(dve, s["dve_step"])
            for t in range(NT):
                dve.wait_ge(done[t % 2], 32 * (t // 2 + 1))
                st.settle(dve.tensor_scalar(m.mixT[:, t, :], y[t % 2][0], m.gates[:, t, 0:1], None, ALU.mult))
                dve.scalar_tensor_tensor(m.mixT[:, t, :], y[t % 2][1], m.gates[:, t, 1:2], m.mixT[:, t, :],
                                         ALU.mult, ALU.add).then_inc(weighted, 1)
    end_stage(nc, m)


def program(nc, a, out):
    m = make_memory(nc)
    more_memory(nc, m)
    load_inputs_stage(nc, m, a["x"], a["constants"])
    constants_stage(nc, m)
    modulation_stage(nc, m, a)
    relative_bias_stage(nc, m, a)
    for l in range(DEPTH):
        transpose_stage(nc, m, m.x_tok, m.xT)
        hybrid_small_stage(nc, m, l, a)
        with nc.Fori(0, DN_HEADS) as h:
            delta_head(nc, m, l, a, h)
        with nc.Fori(0, GLA_HEADS // 2) as pair:
            gla_pair(nc, m, l, a, pair)
        out_stage(nc, m, a["w_out"][l], a["ln_g"][l], a["ln_b"][l], m.eps6)
    second_block(nc, m, a)
    with nc.Block() as block:
        @block.sync
        def _(sp):
            sp.dma_start(out[0].rearrange("(t p) d -> p t d", p=P), m.x_tok[:]).then_inc(m.sem["stored"], 16)
            sp.wait_ge(m.sem["stored"], 16)


def second_block(nc, m, a, layers=range(DEPTH)):
    o_tok = m.work[:, 12 * SEQ:20 * SEQ].rearrange("p (t n) -> p t n", t=NT)
    for l in layers:
        mod = [m.mods[l, n * D:(n + 1) * D] for n in range(6)]
        h = modulate_stage(nc, m, mod[0], mod[1])
        transpose_stage(nc, m, h, m.xT)
        if l % 2 == 0:
            with nc.Fori(0, D // P) as pair:
                neighbourhood_pair(nc, m, a, pair, o_tok)
        else:
            with nc.Fori(0, KV_HEADS) as g:
                grouped_query_group(nc, m, a, g, o_tok)
        transpose_stage(nc, m, o_tok, m.mixT)
        w_o = a["na_w_o_2"][0] if l % 2 == 0 else a["gqa_w_o_2"][0]
        out_stage(nc, m, w_o, a["ln_g_2"][l, 0], a["ln_b_2"][l, 0], m.eps5, mod[2])
        h = modulate_stage(nc, m, mod[3], mod[4], m.h_dram)
        transpose_stage(nc, m, h, m.xT)
        route_stage(nc, m, a, l)
        experts_stage(nc, m, a, l)
        combine_stage(nc, m, l)
        out_stage(nc, m, None, a["ln_g_2"][l, 1], a["ln_b_2"][l, 1], m.eps5, mod[5])


INPUTS = ["x", "w_in", "conv_w", "dn_a_log", "dn_dt_bias", "gla_gate_w2", "gla_gate_b", "dn_norm_g", "gla_norm_g",
          "w_out", "ln_g", "ln_b", "c_2", "ada_w_2", "ada_b_2", "ln_g_2", "ln_b_2", "na_w_qkv_2", "na_rpb_2",
          "na_w_o_2", "gqa_w_qkv_2", "gqa_q_norm_2", "gqa_k_norm_2", "gqa_w_o_2", "moe_w_group_2", "moe_b_group_2",
          "moe_w_expert_2", "moe_b_expert_2", "moe_w_gate_2", "moe_w_up_2", "moe_w_down_2"]


def kernel(**inputs):
    import concourse.bacc as bacc
    from concourse.bass_utils import run_bass_kernel_spmd

    nc = bacc.Bacc("TRN2", target_bir_lowering=False, num_devices=1)
    arrays = {name: np.ascontiguousarray(inputs[name]) for name in INPUTS}
    arrays["constants"] = shape_constants()
    arrays["rope"] = rope_table()
    a = {name: nc.dram_tensor(name, v.shape, mybir.dt.from_np(v.dtype), kind="ExternalInput").ap()
         for name, v in arrays.items()}
    out = nc.dram_tensor("out", (1, SEQ, D), F32, kind="ExternalOutput").ap()
    program(nc, a, out)
    result = run_bass_kernel_spmd(nc, [arrays], core_ids=[0])
    return result.results[0]["out"]
```

```python
import numpy as np
import concourse.bass as bass
from concourse import mybir

F32 = mybir.dt.float32
I32 = mybir.dt.int32
U32 = mybir.dt.uint32
ALU = mybir.AluOpType
ACT = mybir.ActivationFunctionType
AX = mybir.AxisListType

P = 128
SEQ = 1024
D = 1024
NT = SEQ // P
NK = D // P
HALF = 512
DEPTH = 2
ALPHA = (2.0 * DEPTH) ** 0.25
NEG = -1e30

DN_HEADS, GLA_HEADS, DN_DK, GLA_DK, GLA_DV, RANK = 4, 4, 128, 64, 128, 16
C_DN = 0
C_BETA = 4 * 512
C_A = C_BETA + DN_HEADS
C_GQ = C_A + DN_HEADS
C_GK = C_GQ + GLA_HEADS * GLA_DK
C_GV = C_GK + GLA_HEADS * GLA_DK
C_GZ = C_GV + GLA_HEADS * GLA_DV
C_GR = C_GZ + GLA_HEADS * GLA_DV
LEVELS = [1, 2, 4, 8, 16, 32, 64]

K_IDENT = 0
K_ONES = K_IDENT + P
K_UPPER = K_ONES + P
K_STRICT = K_UPPER + P
K_LEVEL = K_STRICT + P
K_RESET = K_LEVEL + P * len(LEVELS)
K_IOTA = K_RESET + SEQ
K_COLS = K_IOTA + P
K_ROWS = K_COLS + 64
K_WIDTH = K_ROWS + 9


def shape_constants():
    t = np.zeros((P, K_WIDTH), np.float32)
    j, i = np.arange(P)[:, None], np.arange(P)[None, :]
    t[:, K_IDENT:K_IDENT + P] = j == i
    t[:, K_ONES:K_ONES + P] = 1
    t[:, K_UPPER:K_UPPER + P] = j <= i
    t[:, K_STRICT:K_STRICT + P] = j < i
    for n, s in enumerate(LEVELS):
        t[:, K_LEVEL + n * P:K_LEVEL + (n + 1) * P] = (
            (j // (2 * s) == i // (2 * s)) & (i % (2 * s) >= s) & (j % (2 * s) < s))
    t[:, K_RESET:K_RESET + SEQ] = np.arange(SEQ)[None, :] % P != 0
    t[:, K_IOTA:K_IOTA + P] = i
    query, key = j % GRID, i[:, :GRID]
    start = np.clip(query - 8, 0, GRID - 16)
    t[:, K_COLS:K_COLS + GRID] = np.where((key >= start) & (key < start + 16), 0, NEG)
    rho = np.arange(-4, 5)[None, :]
    t[:, K_ROWS:K_ROWS + 9] = np.where((rho - j // GRID >= -4) & (rho - j // GRID <= 3), 0, NEG)
    return t


class Places:
    pass


SEMAPHORES = (
    ["loaded_a", "loaded_b", "loaded_c", "loaded_d", "loaded_e", "stored", "prefetched",
     "pe_done", "act_done", "dve_done", "pool_done", "act_step", "dve_step", "pool_step"]
    + [f"signal_{n}" for n in range(24)])


def end_stage(nc, m):
    nc.gpsimd.sem_clear(m.sem_range)
    nc.all_engine_barrier()


class Steps:

    def __init__(self, engine, semaphore):
        self.engine, self.semaphore, self.count = engine, semaphore, 0

    def settle(self, instruction):
        self.count += 1
        instruction.then_inc(self.semaphore, 1)
        self.engine.wait_ge(self.semaphore, self.count)


def make_memory(nc):
    def sb(name, shape, dt=F32):
        return nc.alloc_sbuf_tensor("sb_" + name, shape, dt)

    m = Places()
    m.sem = {name: nc.alloc_semaphore(name) for name in SEMAPHORES}
    numbers = [s.num for s in m.sem.values()]
    m.sem_range = range(min(numbers), max(numbers) + 1)
    assert len(m.sem_range) == len(numbers)
    m.pool_dma = [{name: nc.alloc_semaphore(f"{name}_{l}") for name in
                   ("scattered", "gathered_a", "gathered_b", "gathered_more", "combined_a", "combined_b")}
                  for l in range(DEPTH)]
    m.ps = nc.alloc_psum_tensor("ps", [P, 8, HALF], F32)
    m.const = sb("const", [P, K_WIDTH])
    m.x_tok = sb("x_tok", [P, NT, D])
    m.xT = sb("xT", [P, NK, SEQ])
    m.mixT = sb("mixT", [P, NK, SEQ])
    m.work = sb("work", [P, 20 * SEQ])
    return m


def ident(m, n=P):
    return m.const[0:n, K_IDENT:K_IDENT + n]


def ones(m, rows=P):
    return m.const[0:rows, K_ONES:K_ONES + P]


def banks(m, b, rows=P):
    return m.ps[0:rows, b:b + 2, :].rearrange("p b n -> p (b n)")


def chunks(ap):
    return ap.rearrange("p (c n) -> p c n", n=P)


def spread(ap, n):
    return ap.unsqueeze(2).to_broadcast([ap.shape[0], ap.shape[1], n])


def each_chunk(ap, c=NT):
    return ap.unsqueeze(1).to_broadcast([ap.shape[0], c, ap.shape[1]])


def load_inputs_stage(nc, m, x, constants):
    loaded_a, loaded_b = m.sem["loaded_a"], m.sem["loaded_b"]
    with nc.Block() as block:
        @block.sync
        def _(sp):
            sp.dma_start(m.const[:], constants).then_inc(loaded_a, 16)
            sp.dma_start(m.x_tok[:], x[0].rearrange("(t p) d -> p t d", p=P)).then_inc(loaded_b, 16)
            sp.wait_ge(loaded_a, 16)
            sp.wait_ge(loaded_b, 16)
    end_stage(nc, m)


def transpose_stage(nc, m, src, dst):
    turned, copied_dve, copied_act = (m.sem[f"signal_{n}"] for n in range(3))
    groups = [(t, g) for t in range(NT) for g in range(2)]
    with nc.Block() as block:
        @block.tensor
        def _(pe):
            for n, (t, g) in enumerate(groups):
                if n >= 8:
                    pe.wait_ge(copied_dve if n % 2 == 0 else copied_act, (n - 8) // 2 + 1)
                for k in range(4):
                    last = pe.transpose(m.ps[:, n % 8, k * P:(k + 1) * P],
                                        src[:, t, (4 * g + k) * P:(4 * g + k + 1) * P], ident(m))
                last.then_inc(turned, 1)

        def copy_out(engine, operation, parity, copied):
            for n, (t, g) in enumerate(groups):
                if n % 2 == parity:
                    engine.wait_ge(turned, n + 1)
                    operation(dst[:, 4 * g:4 * g + 4, t * P:(t + 1) * P],
                              chunks(m.ps[:, n % 8, :])).then_inc(copied, 1)

        @block.vector
        def _(dve):
            copy_out(dve, dve.tensor_copy, 0, copied_dve)

        @block.scalar
        def _(act):
            copy_out(act, act.copy, 1, copied_act)
    end_stage(nc, m)


def hybrid_small_stage(nc, m, l, a):
    s = m.sem
    w_loaded, loaded, summed, stepped = s["loaded_a"], s["loaded_b"], s["signal_0"], s["act_step"]
    act_ready, dve_ready, turned, columns = (s[f"signal_{n}"] for n in range(1, 5))
    w = m.work
    w_beta = w[:, 0:32].rearrange("p (k n) -> p k n", k=NK)
    w_a = w[:, 32:64].rearrange("p (k n) -> p k n", k=NK)
    w_r = w[:, 64:192].rearrange("p (k n) -> p k n", k=NK)
    param_rows = w[0:52, 256:256 + P]
    abs_a, e_a, pos_a, g_rows = (w[0:4, 1024 * n:1024 * (n + 1)] for n in range(1, 5))
    beta, G = m.beta_row4[:], m.G_row4[:]
    with nc.Block() as block:
        @block.sync
        def _(sp):
            for dst, c, n in ((w_beta, C_BETA, 4), (w_a, C_A, 4), (w_r, C_GR, RANK)):
                sp.dma_start(dst, a["w_in"][l, :, c:c + n].rearrange("(k p) n -> p k n", p=P)).then_inc(w_loaded, 16)
            sp.dma_start(param_rows[0:48, :], a["conv_w"][l].rearrange("k (t p) -> (k t) p", p=P)).then_inc(loaded, 16)
            sp.dma_start(m.a_log[:], a["dn_a_log"][l].unsqueeze(1)).then_inc(loaded, 16)
            sp.dma_start(m.dt_bias[:], a["dn_dt_bias"][l].unsqueeze(1)).then_inc(loaded, 16)
            sp.dma_start(param_rows[48:49, :], a["dn_norm_g"][l].rearrange("(o p) -> o p", o=1)).then_inc(loaded, 16)
            sp.dma_start(param_rows[49:50, :], a["gla_norm_g"][l].rearrange("(o p) -> o p", o=1)).then_inc(loaded, 16)
            sp.dma_start(param_rows[50:52, :], a["gla_gate_b"][l].rearrange("(t p) -> t p", p=P)).then_inc(loaded, 16)
            sp.dma_start(m.gate_w2[:], a["gla_gate_w2"][l]).then_inc(loaded, 16)
            sp.wait_ge(loaded, 7 * 16)

        @block.tensor
        def _(pe):
            pe.wait_ge(w_loaded, 48)
            for n, wt in enumerate((w_beta, w_a, w_r)):
                for half in range(2):
                    for k in range(NK):
                        last = pe.matmul(m.ps[0:wt.shape[2], 2 * n + half, :], wt[:, k, :],
                                         m.xT[:, k, half * HALF:(half + 1) * HALF],
                                         start=(k == 0), stop=(k == NK - 1))
            last.then_inc(summed, 1)
            pe.wait_ge(loaded, 7 * 16)
            pe.transpose(m.ps[:, 6, 0:52], param_rows, ident(m, 52)).then_inc(turned, 1)
            pe.wait_ge(dve_ready, 3)
            for c in range(NT):
                pe.transpose(m.ps[:, 7, c * 4:c * 4 + 4], G[:, c * P:(c + 1) * P], ident(m, 4))
                last = pe.transpose(m.ps[:, 7, 64 + c * 4:64 + c * 4 + 4], beta[:, c * P:(c + 1) * P],
                                    ident(m, 4))
            last.then_inc(columns, 1)

        @block.scalar
        def _(act):
            st = Steps(act, stepped)
            act.wait_ge(summed, 1)
            act.wait_ge(loaded, 7 * 16)
            act.copy(m.rT[:], banks(m, 4, RANK))
            st.settle(act.activation(m.a_log[:], m.a_log[:], ACT.Exp))
            act.activation(beta, banks(m, 0, 4), ACT.Exp, scale=-1.0).then_inc(act_ready, 1)
            act.wait_ge(dve_ready, 1)
            st.settle(act.activation(e_a, abs_a, ACT.Exp))
            act.activation(g_rows, e_a, ACT.Ln, bias=m.one[0:4, :]).then_inc(act_ready, 1)

        @block.vector
        def _(dve):
            st = Steps(dve, s["dve_step"])
            dve.wait_ge(summed, 1)
            dve.wait_ge(loaded, 7 * 16)
            st.settle(dve.tensor_scalar(pos_a, banks(m, 2, 4), m.dt_bias[:], None, ALU.add))
            st.settle(dve.scalar_tensor_tensor(abs_a, pos_a, -1.0, pos_a, ALU.mult, ALU.min))
            dve.tensor_scalar(pos_a, pos_a, 0.0, None, ALU.max).then_inc(dve_ready, 1)
            dve.wait_ge(act_ready, 2)
            st.settle(dve.tensor_scalar(beta, beta, 1.0, None, ALU.add))
            dve.reciprocal(beta, beta).then_inc(dve_ready, 1)
            st.settle(dve.tensor_tensor(g_rows, g_rows, pos_a, ALU.add))
            st.settle(dve.tensor_scalar(g_rows, g_rows, m.a_log[:], -1.0, ALU.mult, ALU.mult))
            dve.tensor_tensor_scan(G, m.const[0:4, K_RESET:K_RESET + SEQ], g_rows, 0.0,
                                   ALU.mult, ALU.add).then_inc(dve_ready, 1)
            dve.wait_ge(turned, 1)
            dve.tensor_copy(m.conv[:], m.ps[:, 6, 0:52])
            dve.wait_ge(columns, 1)
            dve.tensor_copy(m.G_col[:], m.ps[:, 7, 0:32].rearrange("p (c h) -> p h c", h=4))
            dve.tensor_copy(m.beta_col[:], m.ps[:, 7, 64:96].rearrange("p (c h) -> p h c", h=4))
    end_stage(nc, m)


def load_columns(engine, dst, w, column, n, semaphore):
    engine.dma_start(dst, w[:, bass.ds(column, n)].rearrange("(k p) n -> p k n", p=P)).then_inc(semaphore, 16)


def project_T(pe, m, w_tile, bank):
    for half in range(2):
        for k in range(NK):
            last = pe.matmul(m.ps[:, bank + half, :], w_tile[:, k, :],
                             m.xT[:, k, half * HALF:(half + 1) * HALF], start=(k == 0), stop=(k == NK - 1))
    return last


def sum_features(pe, m, src, bank):
    for half in range(2):
        last = pe.matmul(m.ps[:, bank + half, :], ones(m), src[:, half * HALF:(half + 1) * HALF],
                         start=True, stop=True)
    return last


def delta_weights(m):
    return [m.work[:, n * SEQ:(n + 1) * SEQ].rearrange("p (k n) -> p k n", k=NK) for n in (12, 13, 1, 3)]


def load_delta_weights(sp, m, a, l, h):
    for j, dst in enumerate(delta_weights(m)):
        load_columns(sp, dst, a["w_in"][l], h * P + j * 512, P, m.sem["loaded_a"])
    sp.wait_ge(m.sem["loaded_a"], 64)


def first_delta_weights_stage(nc, m, a, l):
    with nc.Block() as block:
        @block.sync
        def _(sp):
            load_delta_weights(sp, m, a, l, 0)
    end_stage(nc, m)


def delta_head(nc, m, l, a, h):
    s = m.sem
    W = [m.work[:, n * SEQ:(n + 1) * SEQ] for n in range(20)]
    wq = delta_weights(m)
    pads = [m.pad[:, n, :] for n in range(3)]
    qT, kT, vT, zT = W[4], W[5], W[6], W[7]
    r_q, r_k = W[8], W[9]
    G_row, decay = W[10], W[11]
    LT, attnT = W[12], W[13]
    projected, evicted, convolved, silued, squared, normed, summed, rooted, spreaded = (
        s[f"signal_{n}"] for n in range(9))

    with nc.Block() as block:
        @block.tensor
        def _(pe):
            for j in range(4):
                project_T(pe, m, wq[j], 2 * j).then_inc(projected, 1)
            for n in range(2):
                pe.wait_ge(squared, n + 1)
                sum_features(pe, m, (r_q, r_k)[n], 2 * n).then_inc(summed, 1)
            pe.wait_ge(evicted, 3)
            pe.wait_ge(s["signal_10"], 1)
            for half in range(2):
                pe.matmul(m.ps[:, 4 + half, :], m.pick[:], m.G_row4[:, half * HALF:(half + 1) * HALF],
                          start=True, stop=True)
            pe.wait_ge(silued, 4)
            for half in range(2):
                last = pe.matmul(m.ps[:, 6 + half, :], m.pick[:], m.beta_row4[:, half * HALF:(half + 1) * HALF],
                                 start=True, stop=True)
            last.then_inc(spreaded, 1)

        @block.scalar
        def _(act):
            for j in range(3):
                act.wait_ge(projected, j + 1)
                act.copy(pads[j][:, 3:3 + SEQ], banks(m, 2 * j)).then_inc(evicted, 1)
            act.wait_ge(projected, 4)
            for j, x in enumerate((qT, kT, vT)):
                act.wait_ge(convolved, j + 1)
                act.activation(x, x, ACT.Silu).then_inc(silued, 1)
            act.activation(zT, banks(m, 6), ACT.Silu).then_inc(silued, 1)
            for n, x in enumerate((qT, kT)):
                act.wait_ge(silued, n + 1)
                act.activation((r_q, r_k)[n], x, ACT.Square).then_inc(squared, 1)
            for n in range(2):
                act.wait_ge(summed, n + 1)
                act.activation((r_q, r_k)[n], banks(m, 2 * n), ACT.Ln, bias=m.eps6[:]).then_inc(rooted, 1)
            for n in range(2):
                act.wait_ge(rooted, n + 1)
                act.activation((r_q, r_k)[n], (r_q, r_k)[n], ACT.Exp, scale=-0.5).then_inc(rooted, 1)
            act.wait_ge(spreaded, 1)
            act.copy(W[14], banks(m, 6)).then_inc(s["signal_9"], 1)

        @block.vector
        def _(dve):
            st = Steps(dve, s["dve_step"])
            dve.tensor_scalar(m.pick[:], ones(m, 4), m.const[0:4, bass.ds(h + K_IDENT, 1)], None,
                              ALU.mult).then_inc(s["signal_10"], 1)
            st.settle(dve.memset(m.pad[:, :, 0:3], 0.0))
            for j, x in enumerate((qT, kT, vT)):
                dve.wait_ge(evicted, j + 1)
                taps = [m.conv[:, bass.ds(h + (k * 12 + j * 4), 1)] for k in range(4)]
                st.settle(dve.tensor_scalar(x, pads[j][:, 0:SEQ], taps[0], None, ALU.mult))
                for k in range(1, 3):
                    st.settle(dve.scalar_tensor_tensor(x, pads[j][:, k:k + SEQ], taps[k], x, ALU.mult, ALU.add))
                dve.scalar_tensor_tensor(x, pads[j][:, 3:3 + SEQ], taps[3], x, ALU.mult,
                                         ALU.add).then_inc(convolved, 1)
            dve.wait_ge(rooted, 4)
            dve.wait_ge(squared, 2)
            dve.scalar_tensor_tensor(qT, qT, DN_DK ** -0.5, r_q, ALU.mult, ALU.mult)
            dve.tensor_tensor(kT, kT, r_k, ALU.mult)
            dve.wait_ge(spreaded, 1)
            dve.tensor_copy(G_row, banks(m, 4))
    end_stage(nc, m)

    G_col, beta_col = m.G_col[:, h, :], m.beta_col[:, h, :]
    beta_row = W[14]
    k_beta, k_decay, v_beta, expG = W[15], W[16], W[17], W[18]
    c_bg, c_dec = m.cols[:, 0:8], m.cols[:, 8:16]
    kk_ready, qk_ready, k_turned, v_turned, diff_ready, exp_ready, cols_ready = (
        s[f"signal_{n}"] for n in range(7))
    with nc.Block() as block:
        @block.tensor
        def _(pe):
            for c in range(NT):
                at = slice(c * P, (c + 1) * P)
                last = pe.matmul(banks(m, 0)[:, at], kT[:, at], kT[:, at], start=True, stop=True)
            last.then_inc(kk_ready, 1)
            for c in range(NT):
                at = slice(c * P, (c + 1) * P)
                last = pe.matmul(banks(m, 2)[:, at], kT[:, at], qT[:, at], start=True, stop=True)
            last.then_inc(qk_ready, 1)
            for c in range(NT):
                at = slice(c * P, (c + 1) * P)
                last = pe.transpose(banks(m, 4)[:, at], kT[:, at], ident(m))
            last.then_inc(k_turned, 1)
            for c in range(NT):
                at = slice(c * P, (c + 1) * P)
                last = pe.transpose(banks(m, 6)[:, at], vT[:, at], ident(m))
            last.then_inc(v_turned, 1)

        @block.scalar
        def _(act):
            st = Steps(act, s["act_step"])
            act.activation(expG, G_row, ACT.Exp)
            act.activation(c_bg, G_col, ACT.Exp).then_inc(cols_ready, 1)
            act.wait_ge(diff_ready, 1)
            act.activation(c_dec, c_dec, ACT.Exp).then_inc(cols_ready, 1)
            act.wait_ge(diff_ready, 2)
            act.activation(decay, decay, ACT.Exp).then_inc(exp_ready, 1)

        @block.vector
        def _(dve):
            st = Steps(dve, s["dve_step"])
            dve.tensor_tensor(c_dec, chunks(G_row)[:, :, P - 1:P].rearrange("p c n -> p (c n)"), G_col,
                              ALU.subtract).then_inc(diff_ready, 1)
            st.settle(dve.tensor_tensor(chunks(decay), chunks(G_row), spread(G_col, P), ALU.subtract))
            dve.tensor_scalar(decay, decay, 0.0, None, ALU.min).then_inc(diff_ready, 1)
            dve.wait_ge(cols_ready, 2)
            st.settle(dve.tensor_tensor(c_bg, c_bg, beta_col, ALU.mult))
            dve.wait_ge(k_turned, 1)
            dve.tensor_tensor(chunks(k_beta), chunks(banks(m, 4)), spread(c_bg, P), ALU.mult)
            dve.tensor_tensor(chunks(k_decay), chunks(banks(m, 4)), spread(c_dec, P), ALU.mult)
            dve.wait_ge(v_turned, 1)
            dve.tensor_tensor(chunks(v_beta), chunks(banks(m, 6)), spread(beta_col, P), ALU.mult)
            dve.wait_ge(exp_ready, 1)
            dve.wait_ge(kk_ready, 1)
            st.settle(dve.tensor_tensor(LT, banks(m, 0), decay, ALU.mult))
            dve.tensor_tensor(LT, LT, beta_row, ALU.mult)
            dve.wait_ge(qk_ready, 1)
            st.settle(dve.tensor_tensor(attnT, banks(m, 2), decay, ALU.mult))
            dve.tensor_tensor(chunks(attnT), chunks(attnT), each_chunk(m.const[:, K_UPPER:K_UPPER + P]), ALU.mult)
    end_stage(nc, m)

    X, XT, BT, T1 = W[0], W[1], W[2], W[3]
    b_ready, t_ready, t_copied, p_ready, x_ready, xt_ready = (s[f"signal_{n}"] for n in range(6))
    with nc.Block() as block:
        @block.tensor
        def _(pe):
            for n in range(len(LEVELS)):
                pe.wait_ge(b_ready, n + 1)
                pe.wait_ge(x_ready, n + 1)
                pe.wait_ge(xt_ready, n + 1)
                for c in range(NT):
                    at = slice(c * P, (c + 1) * P)
                    last = pe.matmul(banks(m, 0)[:, at], BT[:, at], X[:, at], start=True, stop=True)
                    if c % 4 == 3:
                        last.then_inc(t_ready, 1)
                for c in range(NT):
                    at = slice(c * P, (c + 1) * P)
                    if c % 4 == 0:
                        pe.wait_ge(t_copied, 2 * n + c // 4 + 1)
                    pe.matmul(banks(m, 2)[:, at], XT[:, at], T1[:, at], start=True, stop=True)
                    last = pe.matmul(banks(m, 4)[:, at], T1[:, at], XT[:, at], start=True, stop=True)
                last.then_inc(p_ready, 1)

        @block.scalar
        def _(act):
            for n in range(len(LEVELS)):
                for half in range(2):
                    act.wait_ge(t_ready, 2 * n + half + 1)
                    act.copy(T1[:, half * HALF:(half + 1) * HALF], m.ps[:, half, :]).then_inc(t_copied, 1)

        @block.gpsimd
        def _(pool):
            for n in range(len(LEVELS)):
                if n:
                    pool.wait_ge(t_ready, 2 * n)
                mask = m.const[:, K_LEVEL + n * P:K_LEVEL + (n + 1) * P]
                pool.tensor_tensor(chunks(BT), chunks(LT), each_chunk(mask), ALU.mult).then_inc(b_ready, 1)

        @block.vector
        def _(dve):
            dve.tensor_copy(chunks(X), each_chunk(ident(m))).then_inc(x_ready, 1)
            dve.tensor_copy(chunks(XT), each_chunk(ident(m))).then_inc(xt_ready, 1)
            for n in range(len(LEVELS)):
                dve.wait_ge(p_ready, n + 1)
                dve.wait_ge(x_ready, n + 1)
                dve.tensor_tensor(X, X, banks(m, 2), ALU.subtract).then_inc(x_ready, 1)
                dve.wait_ge(xt_ready, n + 1)
                dve.tensor_tensor(XT, XT, banks(m, 4), ALU.subtract).then_inc(xt_ready, 1)
    end_stage(nc, m)

    wT, u, qg, vn, S, oT = W[19], W[12], W[3], W[11], m.state, W[2]
    w_ready, u_ready, w_copied, u_copied, q_scaled, ws_ready, vn_ready, s_ready, s_done, o_ready = (
        s[f"signal_{n}"] for n in range(10))
    with nc.Block() as block:
        @block.tensor
        def _(pe):
            for c in range(NT):
                at = slice(c * P, (c + 1) * P)
                last = pe.matmul(banks(m, 0)[:, at], k_beta[:, at], XT[:, at], start=True, stop=True)
            last.then_inc(w_ready, 1)
            for c in range(NT):
                at = slice(c * P, (c + 1) * P)
                last = pe.matmul(banks(m, 2)[:, at], XT[:, at], v_beta[:, at], start=True, stop=True)
            last.then_inc(u_ready, 1)
            pe.wait_ge(w_copied, 1)
            pe.wait_ge(q_scaled, 1)
            for c in range(NT):
                at = slice(c * P, (c + 1) * P)
                pe.wait_ge(s_done, c + 1)
                pe.matmul(m.ps[:, 4, (c % 2) * P:(c % 2 + 1) * P], wT[:, at], S[:, c % 2, :],
                          start=True, stop=True).then_inc(ws_ready, 1)
                pe.matmul(m.ps[:, 6 + c // 4, (c % 4) * P:(c % 4 + 1) * P], S[:, c % 2, :], qg[:, at],
                          start=True, stop=False)
                pe.wait_ge(vn_ready, c + 1)
                pe.matmul(m.ps[:, 5, (c % 2) * P:(c % 2 + 1) * P], k_decay[:, at], vn[:, at],
                          start=True, stop=True).then_inc(s_ready, 1)
                pe.matmul(m.ps[:, 6 + c // 4, (c % 4) * P:(c % 4 + 1) * P], vn[:, at], attnT[:, at],
                          start=False, stop=True).then_inc(o_ready, 1)

        @block.scalar
        def _(act):
            act.wait_ge(w_ready, 1)
            act.copy(wT, banks(m, 0)).then_inc(w_copied, 1)
            for half in range(2):
                act.wait_ge(o_ready, 4 * (half + 1))
                act.copy(oT[:, half * HALF:(half + 1) * HALF], m.ps[:, 6 + half, :])

        @block.vector
        def _(dve):
            dve.memset(S[:, 0, :], 0.0).then_inc(s_done, 1)
            dve.tensor_tensor(qg, qT, expG, ALU.mult).then_inc(q_scaled, 1)
            dve.wait_ge(u_ready, 1)
            dve.tensor_copy(u, banks(m, 2)).then_inc(u_copied, 1)
            dve.wait_ge(u_copied, 1)
            for c in range(NT):
                at = slice(c * P, (c + 1) * P)
                dve.wait_ge(ws_ready, c + 1)
                dve.tensor_tensor(vn[:, at], u[:, at], m.ps[:, 4, (c % 2) * P:(c % 2 + 1) * P],
                                  ALU.subtract).then_inc(vn_ready, 1)
                dve.wait_ge(s_ready, c + 1)
                dve.wait_ge(s_done, c + 1)
                dve.scalar_tensor_tensor(S[:, (c + 1) % 2, :], S[:, c % 2, :], expG[:, c * P + P - 1:c * P + P],
                                         m.ps[:, 5, (c % 2) * P:(c % 2 + 1) * P], ALU.mult,
                                         ALU.add).then_inc(s_done, 1)
    end_stage(nc, m)
    gated_norm_stage(nc, m, oT, zT, m.dn_g, h, lambda sp: load_delta_weights(sp, m, a, l, (h + 1) % DN_HEADS))


def gated_norm_stage(nc, m, oT, zT, gain, slot, background=None):
    s = m.sem
    r = m.work[:, 0:SEQ]
    squared, summed = s["signal_0"], s["signal_1"]
    with nc.Block() as block:
        @block.sync
        def _(sp):
            if background is not None:
                background(sp)

        @block.tensor
        def _(pe):
            pe.wait_ge(squared, 1)
            sum_features(pe, m, r, 0).then_inc(summed, 1)

        @block.scalar
        def _(act):
            st = Steps(act, s["act_step"])
            act.activation(r, oT, ACT.Square).then_inc(squared, 1)
            act.wait_ge(summed, 1)
            st.settle(act.activation(r, banks(m, 0), ACT.Ln, bias=m.eps6[:], scale=1.0 / P))
            act.activation(r, r, ACT.Exp, scale=-0.5).then_inc(s["signal_2"], 1)

        @block.vector
        def _(dve):
            st = Steps(dve, s["dve_step"])
            dve.wait_ge(s["signal_2"], 1)
            st.settle(dve.scalar_tensor_tensor(oT, oT, gain[:], r, ALU.mult, ALU.mult))
            dve.tensor_tensor(m.mixT[:, slot, :], oT, zT, ALU.mult)
    end_stage(nc, m)


def more_memory(nc, m):
    def sb(name, shape, dt=F32):
        return nc.alloc_sbuf_tensor("sb_" + name, shape, dt)

    m.rT = m.mixT[0:RANK, NK - 1, :]
    m.beta_row4, m.G_row4, m.pick = sb("beta_row4", [4, SEQ]), sb("G_row4", [4, SEQ]), sb("pick", [4, P])
    m.a_log, m.dt_bias = sb("a_log", [4, 1]), sb("dt_bias", [4, 1])
    m.gate_w2 = sb("gate_w2", [RANK, GLA_HEADS * GLA_DK])
    m.one, m.eps6, m.eps5 = sb("one", [P, 1]), sb("eps6", [P, 1]), sb("eps5", [P, 1])
    m.conv, m.G_col, m.beta_col = sb("conv", [P, 52]), sb("G_col", [P, 4, NT]), sb("beta_col", [P, 4, NT])
    m.dn_g, m.gla_g, m.gate_b = m.conv[:, 48:49], m.conv[:, 49:50], m.conv[:, 50:52]
    m.cols, m.cols2 = sb("cols", [P, 64]), sb("cols2", [P, 64])
    m.stats, m.moments = sb("stats", [P, 2, 2, 6]), sb("moments", [P, NT, 2])
    m.mods = nc.dram_tensor("scratch_mods", [DEPTH, 6 * D], F32, kind="Internal").ap()
    m.gates, m.dest = sb("gates", [P, NT, TOP_K]), sb("dest", [P, TOP_K, NT], I32)
    m.overflow, m.slots = sb("overflow", [P, OVERFLOW + 1], I32), sb("slots", [P, N_BLOCKS], I32)
    m.index = sb("index", [P, 2], I32)
    m.h_dram = nc.dram_tensor("scratch_h", [SEQ, D], F32, kind="Internal").ap()
    m.y_dram = nc.dram_tensor("scratch_y", [P * N_BLOCKS, D], F32, kind="Internal").ap()
    m.slot_token = nc.dram_tensor("scratch_slots", [P * N_BLOCKS, 1], I32, kind="Internal").ap()
    m.bias_dram = nc.dram_tensor("scratch_bias", [64, 240, 64], F32, kind="Internal").ap()
    m.state = sb("state", [P, 2, P])
    m.gla_state = m.state
    m.pick_w = sb("pick_w", [RANK, P])
    m.pad = m.work[:, 15 * SEQ:15 * SEQ + 3 * (3 + SEQ)].rearrange("p (j n) -> p j n", j=3)


def constants_stage(nc, m):
    with nc.Block() as block:
        @block.vector
        def _(dve):
            dve.memset(m.one[:], 1.0)
            dve.memset(m.eps6[:], 1e-6)
            dve.memset(m.eps5[:], 1e-5)
    end_stage(nc, m)


def gla_pair(nc, m, l, a, pair):
    s = m.sem
    W = [m.work[:, n * SEQ:(n + 1) * SEQ] for n in range(20)]
    wt = [m.work[:, n * SEQ:(n + 1) * SEQ].rearrange("p (k n) -> p k n", k=NK) for n in range(6)]
    qT, kT, zT, v_tok = W[6], W[7], (W[8], W[9]), (W[10], W[11])
    B, e_abs, pos = W[12], W[13], W[14]
    loads = [s[f"loaded_{x}"] for x in "abcde"] + [s["prefetched"]]
    projected, logits, abs_ready, e_ready, ln_ready, z_ready = (s[f"signal_{n}"] for n in range(6))
    with nc.Block() as block:
        @block.sync
        def _(sp):
            columns = [C_GQ + pair * P, C_GK + pair * P, C_GZ + pair * 2 * P, C_GZ + pair * 2 * P + P,
                       C_GV + pair * 2 * P, C_GV + pair * 2 * P + P]
            for j in range(6):
                load_columns(sp, wt[j], a["w_in"][l], columns[j], P, loads[j])
            for j in range(6):
                sp.wait_ge(loads[j], 16)

        @block.tensor
        def _(pe):
            pe.wait_ge(s["signal_6"], 1)
            for half in range(2):
                last = pe.matmul(m.ps[:, 6 + half, :], m.pick_w[:], m.rT[:, half * HALF:(half + 1) * HALF],
                                 start=True, stop=True)
            last.then_inc(logits, 1)
            for j in range(3):
                pe.wait_ge(loads[j], 16)
                project_T(pe, m, wt[j], 2 * j).then_inc(projected, 1)
            pe.wait_ge(loads[3], 16)
            pe.wait_ge(abs_ready, 1)
            project_T(pe, m, wt[3], 6).then_inc(projected, 1)
            for j in range(2):
                pe.wait_ge(loads[4 + j], 16)
                pe.wait_ge(s["signal_7"], j + 1)
                for t in range(NT):
                    for k in range(NK):
                        last = pe.matmul(banks(m, 2 * j)[:, t * P:(t + 1) * P],
                                         m.xT[:, k, t * P:(t + 1) * P], wt[4 + j][:, k, :],
                                         start=(k == 0), stop=(k == NK - 1))
                last.then_inc(projected, 1)

        @block.scalar
        def _(act):
            st = Steps(act, s["act_step"])
            act.wait_ge(abs_ready, 1)
            st.settle(act.activation(e_abs, e_abs, ACT.Exp))
            act.activation(e_abs, e_abs, ACT.Ln, bias=m.one[:]).then_inc(ln_ready, 1)
            act.wait_ge(projected, 1)
            act.mul(qT, banks(m, 0), GLA_DK ** -0.5).then_inc(s["signal_7"], 1)
            act.wait_ge(projected, 2)
            act.copy(kT, banks(m, 2)).then_inc(s["signal_7"], 1)
            act.wait_ge(projected, 3)
            act.activation(zT[0], banks(m, 4), ACT.Silu)
            act.wait_ge(projected, 4)
            act.activation(zT[1], banks(m, 6), ACT.Silu)
            for j in range(2):
                act.wait_ge(projected, 5 + j)
                act.copy(v_tok[j], banks(m, 2 * j))

        @block.vector
        def _(dve):
            st = Steps(dve, s["dve_step"])
            dve.tensor_copy(m.pick_w[:], m.gate_w2[:, bass.ds(pair * P, P)]).then_inc(s["signal_6"], 1)
            dve.wait_ge(logits, 1)
            st.settle(dve.tensor_scalar(pos, banks(m, 6), m.gate_b[:, bass.ds(pair, 1)], -1.0, ALU.add, ALU.mult))
            dve.scalar_tensor_tensor(e_abs, pos, -1.0, pos, ALU.mult, ALU.min).then_inc(abs_ready, 1)
            dve.wait_ge(abs_ready, 1)
            st.settle(dve.tensor_scalar(pos, pos, 0.0, None, ALU.max))
            dve.wait_ge(ln_ready, 1)
            st.settle(dve.tensor_tensor(pos, pos, e_abs, ALU.add))
            st.settle(dve.tensor_scalar(pos, pos, -1.0 / 16.0, None, ALU.mult))
            dve.tensor_tensor_scan(B, m.const[:, K_RESET:K_RESET + SEQ], pos, 0.0, ALU.mult, ALU.add)
    end_stage(nc, m)

    attn = (W[15], W[16])
    E, qs, ks = (W[0], W[1]), (W[2], W[3]), (W[4], W[5])
    expB, qg, k_dec, k_dec_tok = W[17], W[18], W[13], W[14]
    d_ready, min_ready, exp_ready, q_ready, k_ready, a_ready, a_taken = (s[f"signal_{n}"] for n in range(7))
    n_levels = len(LEVELS)
    with nc.Block() as block:
        @block.tensor
        def _(pe):
            for n in range(n_levels + 1):
                if n < n_levels:
                    pe.wait_ge(q_ready, n + 1)
                    pe.wait_ge(k_ready, n + 1)
                for head in range(2):
                    bank = 4 * (n % 2) + 2 * head
                    if n >= 2:
                        pe.wait_ge(a_taken, 2 * (n - 2) + head + 1)
                    rows = slice(64 * head, 64 * head + 64)
                    q_at, k_at = (qs[n % 2], ks[n % 2]) if n < n_levels else (qT, kT)
                    for c in range(NT):
                        at = slice(c * P, (c + 1) * P)
                        last = pe.matmul(banks(m, bank)[:, at], k_at[rows, at], q_at[rows, at],
                                         start=True, stop=True)
                    last.then_inc(a_ready, 1)

        @block.gpsimd
        def _(pool):
            for n in range(n_levels):
                pool.wait_ge(exp_ready, n + 1)
                if n >= 2:
                    pool.wait_ge(a_ready, 2 * (n - 1))
                pool.tensor_tensor(ks[n % 2], kT, E[n % 2], ALU.mult).then_inc(k_ready, 1)

        @block.scalar
        def _(act):
            for n in range(n_levels):
                act.wait_ge(min_ready, n + 1)
                act.activation(E[n % 2], E[n % 2], ACT.Exp).then_inc(exp_ready, 1)
            act.activation(expB, B, ACT.Exp)

        @block.vector
        def _(dve):
            st = Steps(dve, s["dve_step"])

            def exponent(n):
                size = 2 * LEVELS[n]
                blocks = B.rearrange("p (b n) -> p b n", n=size)
                middle = blocks[:, :, LEVELS[n] - 1:LEVELS[n]].to_broadcast([P, SEQ // size, size])
                if n >= 2:
                    dve.wait_ge(q_ready, n - 1)
                    dve.wait_ge(k_ready, n - 1)
                e = E[n % 2]
                st.settle(dve.tensor_tensor(e.rearrange("p (b n) -> p b n", n=size), blocks, middle, ALU.subtract))
                dve.scalar_tensor_tensor(e, e, -1.0, e, ALU.mult, ALU.min).then_inc(min_ready, 1)

            def scaled_q(n):
                dve.wait_ge(exp_ready, n + 1)
                if n >= 2:
                    dve.wait_ge(a_ready, 2 * (n - 1))
                dve.tensor_tensor(qs[n % 2], qT, E[n % 2], ALU.mult).then_inc(q_ready, 1)

            dve.memset(attn[0], 0.0).then_inc(s["signal_7"], 1)
            dve.memset(attn[1], 0.0).then_inc(s["signal_7"], 1)
            exponent(0)
            for n in range(n_levels + 1):
                if n < n_levels:
                    scaled_q(n)
                if n + 1 < n_levels:
                    exponent(n + 1)
                column = K_LEVEL + n * P if n < n_levels else K_IDENT
                mask = each_chunk(m.const[:, column:column + P].bitcast(I32))
                for head in range(2):
                    dve.wait_ge(a_ready, 2 * n + head + 1)
                    dve.wait_ge(s["signal_7"], 2)
                    if n:
                        dve.wait_ge(a_taken, 2 * (n - 1) + head + 1)
                    dve.copy_predicated(chunks(attn[head]), mask, chunks(banks(m, 4 * (n % 2) + 2 * head))
                                        ).then_inc(a_taken, 1)
    end_stage(nc, m)

    oT = (W[2], W[3])
    state = m.gla_state
    turned, turned_out, kd_ready, scaled, s_done, ds_ready, o_ready, eb_ready = (
        s[f"signal_{n}"] for n in range(8))
    with nc.Block() as block:
        @block.tensor
        def _(pe):
            pe.wait_ge(kd_ready, 1)
            for c in range(NT):
                at = slice(c * P, (c + 1) * P)
                last = pe.transpose(banks(m, 0)[:, at], k_dec[:, at], ident(m))
            last.then_inc(turned, 1)
            pe.wait_ge(turned_out, 1)
            pe.wait_ge(scaled, 1)
            for c in range(NT):
                at = slice(c * P, (c + 1) * P)
                for head in range(2):
                    if c >= 2:
                        pe.wait_ge(s_done, c)
                    last = pe.matmul(m.ps[:, 2 + c % 2, head * P:(head + 1) * P], k_dec_tok[:, at],
                                     v_tok[head][:, at], start=True, stop=True)
                last.then_inc(ds_ready, 1)
                pe.wait_ge(s_done, c + 1)
                for head in range(2):
                    rows = slice(64 * head, 64 * head + 64)
                    out = m.ps[:, 4 + 2 * head + c // 4, (c % 4) * P:(c % 4 + 1) * P]
                    pe.matmul(out, state[rows, c % 2, :], qg[rows, at], start=True, stop=False)
                    last = pe.matmul(out, v_tok[head][:, at], attn[head][:, at], start=False, stop=True)
                last.then_inc(o_ready, 1)

        @block.scalar
        def _(act):
            act.wait_ge(s["signal_8"], 1)
            act.activation(k_dec, k_dec, ACT.Exp).then_inc(eb_ready, 1)
            act.wait_ge(turned, 1)
            act.copy(k_dec_tok, banks(m, 0)).then_inc(turned_out, 1)
            for half in range(2):
                act.wait_ge(o_ready, 4 * (half + 1))
                for head in range(2):
                    act.copy(oT[head][:, half * HALF:(half + 1) * HALF], m.ps[:, 4 + 2 * head + half, :])

        @block.vector
        def _(dve):
            last_B = chunks(B)[:, :, P - 1:P].to_broadcast([P, NT, P])
            dve.tensor_tensor(chunks(k_dec), last_B, chunks(B), ALU.subtract).then_inc(s["signal_8"], 1)
            dve.memset(state[:, 0, :], 0.0).then_inc(s_done, 1)
            dve.tensor_tensor(qg, qT, expB, ALU.mult).then_inc(scaled, 1)
            dve.wait_ge(eb_ready, 1)
            dve.tensor_tensor(k_dec, k_dec, kT, ALU.mult).then_inc(kd_ready, 1)
            for c in range(NT):
                dve.wait_ge(ds_ready, c + 1)
                dve.wait_ge(s_done, c + 1)
                if c:
                    dve.wait_ge(o_ready, c)
                for head in range(2):
                    rows = slice(64 * head, 64 * head + 64)
                    last = dve.scalar_tensor_tensor(
                        state[rows, (c + 1) % 2, :], state[rows, c % 2, :],
                        expB[rows, c * P + P - 1:c * P + P], m.ps[rows, 2 + c % 2, head * P:(head + 1) * P],
                        ALU.mult, ALU.add)
                last.then_inc(s_done, 1)
    end_stage(nc, m)
    for head in range(2):
        gated_norm_stage(nc, m, oT[head], zT[head], m.gla_g, pair * 2 + (4 + head))


def out_stage(nc, m, w_out, ln_g, ln_b, eps, gate=None, background=None):
    s = m.sem
    w = m.work[:, 0:8 * SEQ].rearrange("p (k n) -> p k n", k=NK)
    g_row, b_row, gate_row = (m.work[:, n * SEQ:(n + 1) * SEQ] for n in (8, 9, 10))
    y = [m.work[:, n * SEQ:(n + 1) * SEQ] for n in (11, 12)]
    y_ready, y_taken, var_ready, root_ready, scaled = (s[f"signal_{n}"] for n in range(5))
    ln_ready, gated = s["signal_5"], s["signal_6"]
    w_loaded = s["loaded_a"], s["loaded_e"]
    with nc.Block() as block:
        @block.sync
        def _(sp):
            if w_out is not None:
                for half, done in enumerate(w_loaded):
                    at = slice(half * HALF, (half + 1) * HALF)
                    for k in range(0, NK, 2):
                        sp.dma_start(w[:, k:k + 2, at], w_out[k * P:(k + 2) * P, at].rearrange(
                            "(k p) n -> p k n", p=P)).then_inc(done, 16)
            rows = [(g_row, ln_g), (b_row, ln_b)] + ([(gate_row, gate)] if gate is not None else [])
            for dst, src in rows:
                sp.dma_start(dst, src.partition_broadcast(P)).then_inc(s["loaded_b"], 16)
            if background is not None:
                background(sp)
            sp.wait_ge(s["loaded_b"], 16 * len(rows))
            if w_out is not None:
                for done in w_loaded:
                    sp.wait_ge(done, 16 * (NK // 2))

        @block.tensor
        def _(pe):
            if w_out is None:
                return
            for t in range(NT):
                if t >= 4:
                    pe.wait_ge(y_taken, t - 3)
                for half in range(2):
                    if t == 0:
                        pe.wait_ge(w_loaded[half], 16 * (NK // 2))
                    for k in range(NK):
                        last = pe.matmul(m.ps[:, 2 * (t % 4) + half, :], m.mixT[:, k, t * P:(t + 1) * P],
                                         w[:, k, half * HALF:(half + 1) * HALF],
                                         start=(k == 0), stop=(k == NK - 1))
                last.then_inc(y_ready, 1)

        @block.scalar
        def _(act):
            for t in range(NT):
                act.wait_ge(var_ready, t + 1)
                act.activation(m.cols[:, t:t + 1], m.moments[:, t, 1:2], ACT.Ln, bias=eps[:]).then_inc(ln_ready, 1)
                act.wait_ge(ln_ready, t + 1)
                act.activation(m.cols[:, t:t + 1], m.cols[:, t:t + 1], ACT.Exp, scale=-0.5).then_inc(root_ready, 1)

        @block.vector
        def _(dve):
            st = Steps(dve, s["dve_step"])
            dve.memset(m.work[:, 14 * SEQ:15 * SEQ], 0.0).then_inc(s["dve_done"], 1)
            dve.wait_ge(s["loaded_b"], 16 * (3 if gate is not None else 2))
            if gate is not None:
                dve.tensor_scalar(gate_row, gate_row, 1.0, None, ALU.add).then_inc(s["dve_done"], 1)
                dve.wait_ge(s["dve_done"], 2)

            def normalise(t):
                x = m.x_tok[:, t, :]
                dve.scalar_tensor_tensor(x, x, m.moments[:, t, 0:1], g_row, ALU.subtract, ALU.mult).then_inc(scaled, 1)
                dve.wait_ge(root_ready, t + 1)
                dve.wait_ge(scaled, t + 1)
                dve.scalar_tensor_tensor(x, x, m.cols[:, t:t + 1], b_row, ALU.mult, ALU.add)

            for t in range(NT):
                x = m.x_tok[:, t, :]
                y_t = m.mixT[:, t, :]
                if w_out is not None:
                    y_t = banks(m, 2 * (t % 4))
                    dve.wait_ge(y_ready, t + 1)
                if gate is not None and w_out is not None:
                    st.settle(dve.tensor_tensor(y[t % 2], y_t, gate_row, ALU.mult))
                    y_t = y[t % 2]
                elif gate is not None:
                    dve.wait_ge(gated, t + 1)
                dve.scalar_tensor_tensor(x, x, ALPHA, y_t, ALU.mult, ALU.add).then_inc(y_taken, 1)
                dve.wait_ge(y_taken, t + 1)
                for half in range(2):
                    last = dve.bn_stats(m.stats[:, t % 2, half, :], x[:, half * HALF:(half + 1) * HALF])
                st.settle(last)
                dve.bn_aggr(m.moments[:, t, :], m.stats[:, t % 2, :, :]).then_inc(var_ready, 1)
                if t:
                    normalise(t - 1)
            dve.wait_ge(var_ready, NT)
            normalise(NT - 1)

        @block.gpsimd
        def _(pool):
            if w_out is None and gate is not None:
                pool.wait_ge(s["dve_done"], 2)
                for t in range(NT):
                    pool.tensor_tensor(m.mixT[:, t, :], m.mixT[:, t, :], gate_row, ALU.mult).then_inc(gated, 1)
    end_stage(nc, m)


def modulation_stage(nc, m, a):
    s = m.sem
    groups = 6 * D // HALF
    c_rows, c_cols = m.work[0:8, 0:P], m.cols[:, 0:8]
    bias, row = m.work[0:1, SEQ:7 * SEQ], m.work[0:1, 7 * SEQ:13 * SEQ]
    w = [m.mixT[:, 4 * n:4 * n + 4, :].rearrange("p a (b n) -> p (a b) n", n=HALF) for n in range(2)]
    silued, turned, columns, summed, added = (s[f"signal_{n}"] for n in range(5))
    with nc.Fori(0, DEPTH) as l:
        with nc.Block() as block:
            @block.sync
            def _(sp):
                sp.dma_start(c_rows, a["c_2"][0].rearrange("(k p) -> k p", p=P)).then_inc(s["loaded_c"], 16)
                sp.dma_start(bias, a["ada_b_2"][bass.ds(l, 1), :]).then_inc(s["loaded_d"], 16)
                for g in range(groups):
                    if g >= 2:
                        sp.wait_ge(summed, g - 1)
                    src = a["ada_w_2"][bass.ds(l, 1), :, g * HALF:(g + 1) * HALF]
                    sp.dma_start(w[g % 2], src.rearrange("a (k p) n -> p (a k) n", p=P)).then_inc(
                        s["loaded_a" if g % 2 == 0 else "loaded_b"], 16)
                sp.wait_ge(added, groups)
                sp.dma_start(m.mods[bass.ds(l, 1), :], row).then_inc(s["stored"], 16)
                sp.wait_ge(s["stored"], 16)

            @block.scalar
            def _(act):
                act.wait_ge(s["loaded_c"], 16)
                act.activation(c_rows, c_rows, ACT.Silu).then_inc(silued, 1)

            @block.tensor
            def _(pe):
                pe.wait_ge(silued, 1)
                pe.transpose(m.ps[:, 0, 0:8], c_rows, ident(m, 8)).then_inc(turned, 1)
                pe.wait_ge(columns, 1)
                for g in range(groups):
                    pe.wait_ge(s["loaded_a" if g % 2 == 0 else "loaded_b"], 16 * (g // 2 + 1))
                    if g >= 4:
                        pe.wait_ge(added, g - 3)
                    for k in range(NK):
                        last = pe.matmul(m.ps[0:1, 1 + g % 4, :], c_cols[:, k:k + 1], w[g % 2][:, k, :],
                                         start=(k == 0), stop=(k == NK - 1))
                    last.then_inc(summed, 1)

            @block.vector
            def _(dve):
                dve.wait_ge(turned, 1)
                dve.tensor_copy(c_cols, m.ps[:, 0, 0:8]).then_inc(columns, 1)
                dve.wait_ge(s["loaded_d"], 16)
                for g in range(groups):
                    at = slice(g * HALF, (g + 1) * HALF)
                    dve.wait_ge(summed, g + 1)
                    dve.tensor_tensor(row[:, at], m.ps[0:1, 1 + g % 4, :], bias[:, at], ALU.add).then_inc(added, 1)
        end_stage(nc, m)


def modulate_stage(nc, m, shift, scale, store=None):
    s = m.sem
    h = m.work[:, 0:8 * SEQ].rearrange("p (t n) -> p t n", t=NT)
    sc, sh = m.work[:, 8 * SEQ:9 * SEQ], m.work[:, 9 * SEQ:10 * SEQ]
    scaled, shifted = s["signal_0"], s["signal_1"]
    with nc.Block() as block:
        @block.sync
        def _(sp):
            sp.dma_start(sc, scale.partition_broadcast(P)).then_inc(s["loaded_a"], 16)
            sp.dma_start(sh, shift.partition_broadcast(P)).then_inc(s["loaded_b"], 16)
            sp.wait_ge(s["loaded_a"], 16)
            sp.wait_ge(s["loaded_b"], 16)
            if store is not None:
                for t in range(NT):
                    sp.wait_ge(shifted, t + 1)
                    sp.dma_start(store[t * P:(t + 1) * P, :], h[:, t, :]).then_inc(s["stored"], 16)
                sp.wait_ge(s["stored"], 16 * NT)

        @block.vector
        def _(dve):
            dve.wait_ge(s["loaded_a"], 16)
            for t in range(NT):
                dve.scalar_tensor_tensor(h[:, t, :], sc, 1.0, m.x_tok[:, t, :], ALU.add,
                                         ALU.mult).then_inc(scaled, 1)
                if t == 0:
                    dve.wait_ge(s["loaded_b"], 16)
                dve.wait_ge(scaled, t + 1)
                dve.tensor_tensor(h[:, t, :], h[:, t, :], sh, ALU.add).then_inc(shifted, 1)
    end_stage(nc, m)
    return h


HD = 64
GRID = 64
NA_RHO = 14


def attention_steps(nc, m, block, steps, scale, bias):
    s = m.sem
    (s_ready, s_taken, max_ready, p_ready, turned, copied_dve, copied_act, o_ready, o_done, normalised) = (
        s[f"signal_{n}"] for n in range(10))
    prob = [m.work[:, (12 + n) * SEQ:(13 + n) * SEQ] for n in range(2)]
    probT = [m.work[:, (14 + n) * SEQ:(15 + n) * SEQ] for n in range(2)]
    top, total, inverse, inverted = m.cols[:, 0:32], m.cols[:, 32:64], m.cols2[:, 0:32], s["signal_10"]
    widths = [step[5] for step in steps]
    count = len(steps)

    def pieces(n):
        return [(at, min(P, n - at)) for at in range(0, n, P)]

    @block.tensor
    def _(pe):
        def scores(i):
            q, keys = steps[i][0:2]
            if i >= 2:
                pe.wait_ge(s_taken, i - 1)
            for b in range(0, widths[i], HALF):
                w = min(HALF, widths[i] - b)
                last = pe.matmul(m.ps[:, 2 * (i % 2) + b // HALF, 0:w], q, keys[:, b:b + w], start=True, stop=True)
            last.then_inc(s_ready, 1)

        def turn(i):
            pe.wait_ge(normalised, i + 1)
            if i:
                pe.wait_ge(copied_dve, i)
                pe.wait_ge(copied_act, i)
            for at, w in pieces(widths[i]):
                last = pe.transpose(banks(m, 4)[0:w, at:at + P], prob[i % 2][:, at:at + w], ident(m))
            last.then_inc(turned, 1)

        def weigh(i):
            pe.wait_ge(copied_dve, i + 1)
            pe.wait_ge(copied_act, i + 1)
            if i >= 2:
                pe.wait_ge(o_done, i - 1)
            blocks = pieces(widths[i])
            for b, (at, w) in enumerate(blocks):
                last = pe.matmul(m.ps[:, 6 + i % 2, 0:P], steps[i][2][b], probT[i % 2][0:w, at:at + P],
                                 start=(b == 0), stop=(b == len(blocks) - 1))
            last.then_inc(o_ready, 1)

        scores(0)
        scores(1)
        for i in range(count):
            if i + 2 < count:
                scores(i + 2)
            if i:
                weigh(i - 1)
            turn(i)
        weigh(count - 1)

    @block.scalar
    def _(act):
        def copy_out(i):
            act.wait_ge(turned, i + 1)
            if i >= 2:
                act.wait_ge(o_ready, i - 1)
            act.copy(probT[i % 2][:, 0:HALF], m.ps[:, 4, :]).then_inc(copied_act, 1)

        for i in range(count):
            n = widths[i]
            act.wait_ge(max_ready, i + 1)
            if i >= 2:
                act.wait_ge(turned, i - 1)
            src = prob[i % 2][:, 0:n] if bias else banks(m, 2 * (i % 2))[:, 0:n]
            act.activation(prob[i % 2][:, 0:n], src, ACT.Exp, bias=top[:, i:i + 1], scale=scale,
                           accum_out=total[:, i:i + 1]).then_inc(p_ready, 1)
            if not bias:
                act.wait_ge(p_ready, i + 1)
                act.sem_inc(s_taken, 1)
            if i:
                copy_out(i - 1)
        copy_out(count - 1)

    @block.vector
    def _(dve):
        def copy_out(i):
            n = widths[i]
            dve.wait_ge(turned, i + 1)
            if i >= 2:
                dve.wait_ge(o_ready, i - 1)
            if n > HALF:
                rows, w = min(P, n - HALF), max(P, n - HALF)
                dve.tensor_copy(probT[i % 2][0:rows, HALF:HALF + w], m.ps[0:rows, 5, 0:w]).then_inc(copied_dve, 1)
            else:
                dve.sem_inc(copied_dve, 1)

        def normalise(i):
            dve.wait_ge(p_ready, i + 1)
            dve.reciprocal(inverse[:, i:i + 1], total[:, i:i + 1]).then_inc(inverted, 1)
            dve.wait_ge(inverted, i + 1)
            p = prob[i % 2][:, 0:widths[i]]
            dve.tensor_scalar(p, p, inverse[:, i:i + 1], None, ALU.mult).then_inc(normalised, 1)

        def finish(i):
            dve.wait_ge(o_ready, i + 1)
            dve.tensor_copy(steps[i][3], m.ps[steps[i][4], 6 + i % 2, 0:P]).then_inc(o_done, 1)

        for i in range(count):
            n = widths[i]
            dve.wait_ge(s_ready, i + 1)
            src = banks(m, 2 * (i % 2))[:, 0:n]
            if bias:
                if i >= 2:
                    dve.wait_ge(turned, i - 1)
                dve.tensor_tensor(prob[i % 2][:, 0:n], src, bias[i], ALU.add).then_inc(s_taken, 1)
                dve.wait_ge(s_taken, i + 1)
                src = prob[i % 2][:, 0:n]
            dve.tensor_reduce(top[:, i:i + 1], src, AX.X, ALU.max, negate=True).then_inc(max_ready, 1)
            if i:
                normalise(i - 1)
            if i >= 2:
                copy_out(i - 2)
            if i >= 3:
                finish(i - 3)
        normalise(count - 1)
        copy_out(count - 2)
        finish(count - 3)
        copy_out(count - 1)
        finish(count - 2)
        finish(count - 1)


def relative_bias(sp, m, a):
    s = m.sem
    rows = m.work[0:120, 14 * SEQ:14 * SEQ + 2 * P].rearrange("p (j n) -> p j n", j=2)
    table = a["na_rpb_2"][0].rearrange("h r c -> (h r) c").rearrange("(j p) c -> p j c", p=120)
    sp.wait_ge(s["dve_done"], 1)
    sp.dma_start(rows[:, :, 48:48 + 31], table).then_inc(s["loaded_c"], 16)
    sp.wait_ge(s["loaded_c"], 16)
    with sp.Fori(0, GRID) as i:
        dst = m.bias_dram[bass.ds((GRID - 1) - i, 1), :, :]
        sp.dma_start(dst.rearrange("a (j p) k -> p (a j) k", p=120),
                     rows[:, :, bass.ds(i, GRID)]).then_inc(s["stored"], 16)
    sp.wait_ge(s["stored"], 16 * GRID)


def clear_overflow(sp, m):
    s = m.sem
    sp.wait_ge(s["dve_done"], 1)
    y_blocks = m.y_dram.rearrange("(p b) d -> p b d", p=P)
    for b in range(N_EXPERTS, N_BLOCKS):
        sp.dma_start(y_blocks[:, b, :], m.work[:, 14 * SEQ:15 * SEQ]).then_inc(s["stored"], 16)
    sp.wait_ge(s["stored"], 16 * OVERFLOW)


def load_neighbourhood_weights(sp, m, a, pair):
    for j in range(3):
        load_columns(sp, m.work[:, j * SEQ:(j + 1) * SEQ].rearrange("p (k n) -> p k n", k=NK),
                     a["na_w_qkv_2"][0], pair * P + j * D, P, m.sem["loaded_a"])


def load_group_weights(sp, m, a, g):
    w = m.work[:, 3 * SEQ:6 * SEQ].rearrange("p (k n) -> p k n", k=NK)
    for dst, column, n in ((slice(0, 4 * HD), g * 4 * HD, 4 * HD),
                           (slice(4 * HD, 5 * HD), g * HD + D, HD),
                           (slice(5 * HD, 6 * HD), g * HD + (D + KV_HEADS * HD), HD)):
        load_columns(sp, w[:, :, dst], a["gqa_w_qkv_2"][0], column, n, m.sem["loaded_a"])


def first_weights_stage(nc, m, a, load):
    with nc.Block() as block:
        @block.sync
        def _(sp):
            load(sp, m, a, 0)
            sp.wait_ge(m.sem["loaded_a"], 48)
    end_stage(nc, m)


def neighbourhood_pair(nc, m, a, pair):
    s = m.sem
    W = [m.work[:, n * SEQ:(n + 1) * SEQ] for n in range(12)]
    wt = [W[n].rearrange("p (k n) -> p k n", k=NK) for n in range(3)]
    q_pad, kT = (W[3], W[10]), W[4]
    v_tok = W[5].rearrange("p (t n) -> p t n", t=NT)
    full = [W[6 + n][:, 0:NA_RHO * GRID].rearrange("p (r k) -> p r k", k=GRID) for n in range(2)]
    inner = [W[8 + n][:, 0:9 * GRID].rearrange("p (r k) -> p r k", k=GRID) for n in range(2)]
    projected, masked = s["signal_0"], s["signal_1"]
    with nc.Block() as block:
        @block.sync
        def _(sp):
            for head in range(2):
                for row in range(2):
                    sp.dma_start(full[head][64 * row:64 * row + 64, :, :],
                                 m.bias_dram[:, bass.ds(pair * 30 + (head * 15 + 1 - row), NA_RHO), :]).then_inc(
                                     s["loaded_d"], 16)
            sp.wait_ge(s["loaded_d"], 64)

        @block.tensor
        def _(pe):
            for j in range(2):
                project_T(pe, m, wt[j], 2 * j).then_inc(projected, 1)
            for t in range(NT):
                for k in range(NK):
                    last = pe.matmul(banks(m, 4)[:, t * P:(t + 1) * P], m.xT[:, k, t * P:(t + 1) * P],
                                     wt[2][:, k, :], start=(k == 0), stop=(k == NK - 1))
            last.then_inc(projected, 1)

        @block.scalar
        def _(act):
            act.wait_ge(projected, 1)
            for head in range(2):
                rows = slice(64 * head, 64 * head + 64)
                act.mul(q_pad[head][rows, :], banks(m, 0)[rows, :], HD ** -0.5)
            act.wait_ge(projected, 2)
            act.copy(kT, banks(m, 2))
            act.wait_ge(projected, 3)
            act.copy(W[5], banks(m, 4))

        @block.vector
        def _(dve):
            for head in range(2):
                dve.memset(q_pad[head][64 * (1 - head):64 * (1 - head) + 64, :], 0.0)
            dve.wait_ge(s["loaded_d"], 64)
            for head in range(2):
                dve.tensor_tensor(full[head], full[head], each_chunk(m.const[:, K_COLS:K_COLS + GRID], NA_RHO),
                                  ALU.add).then_inc(masked, 1)
                dve.wait_ge(masked, head + 1)
                dve.tensor_tensor(inner[head], full[head][:, 2:11, :],
                                  spread(m.const[:, K_ROWS:K_ROWS + 9], GRID), ALU.add)
    end_stage(nc, m)
    steps, bias = [], []
    for head in range(2):
        rows = slice(64 * head, 64 * head + 64)
        for t in range(NT):
            first = min(max(2 * t - 4, 0), 8)
            n_rows = 9 if 2 <= t <= 5 else 8
            keys = kT[:, first * GRID:(first + n_rows) * GRID]
            values = [v_tok[0:min(P, n_rows * GRID - b * P), first // 2 + b, :]
                      for b in range((n_rows + 1) // 2)]
            steps.append((q_pad[head][:, t * P:(t + 1) * P], keys, values,
                          m.mixT[rows, pair, t * P:(t + 1) * P], rows, n_rows * GRID))
            tile = inner[head] if n_rows == 9 else full[head][:, first - 2 * t + 6:first - 2 * t + 14, :]
            bias.append(tile.rearrange("p r k -> p (r k)"))
    with nc.Block() as block:
        @block.sync
        def _(sp):
            load_neighbourhood_weights(sp, m, a, (pair + 1) % (D // P))
            sp.wait_ge(s["loaded_a"], 48)

        attention_steps(nc, m, block, steps, 1.0, bias)
    end_stage(nc, m)


KV_HEADS, GROUP = 4, 4
ROPE_HALF = 16


def rope_table():
    t = np.arange(SEQ, dtype=np.int32)
    pos = np.stack([t // GRID, t % GRID], axis=-1).astype(np.float32)
    inv_freq = np.float32(10000.0) ** (-np.arange(ROPE_HALF, dtype=np.float32) / ROPE_HALF)
    angle = (pos[:, :, None] * inv_freq).reshape(SEQ, 2 * ROPE_HALF)
    return np.concatenate([np.cos(angle), np.sin(angle)], axis=1).astype(np.float32)


def grouped_query_group(nc, m, a, g):
    s = m.sem
    W = [m.work[:, n * SEQ:(n + 1) * SEQ] for n in range(12)]
    WIDE = (GROUP + 2) * HD
    w = m.work[:, 3 * SEQ:6 * SEQ].rearrange("p (k n) -> p k n", k=NK)
    raw = m.work[:, 16 * SEQ:19 * SEQ].rearrange("p (t n) -> p t n", t=NT)
    n_norm = GROUP + 1
    square = m.work[:, 12 * SEQ:12 * SEQ + NT * n_norm * HD].rearrange("p (t n) -> p t n", t=NT)
    part_of = [slice(half * NT * n_norm // 2, (half + 1) * NT * n_norm // 2) for half in range(2)]
    q_pad, k2, v_tok = (W[6], W[7], W[0], W[1]), W[8], W[9].rearrange("p (t n) -> p t n", t=NT)
    gain_q, gain_k = W[10][:, 0:HD], W[10][:, HD:2 * HD]
    rope = W[10][:, 512:1024].rearrange("p (t n) -> p t n", t=NT)
    heads = raw[:, :, 0:n_norm * HD].rearrange("p t (h d) -> p t h d", d=HD)
    part = [x[:, 0:NT * n_norm * ROPE_HALF].rearrange("p (t h d) -> p t h d", t=NT, h=n_norm)
            for x in (W[6], W[7], W[8], W[11])]
    root = m.cols2[:, 0:NT * n_norm]
    projected, evicted, squared, summed, rooted, roped, turned = (s[f"signal_{n}"] for n in range(7))
    with nc.Block() as block:
        @block.sync
        def _(sp):
            sp.dma_start(gain_q, a["gqa_q_norm_2"][0].partition_broadcast(P)).then_inc(s["loaded_b"], 16)
            sp.dma_start(gain_k, a["gqa_k_norm_2"][0].partition_broadcast(P)).then_inc(s["loaded_b"], 16)
            sp.dma_start(rope, a["rope"].rearrange("(t p) n -> p t n", p=P)).then_inc(s["loaded_b"], 16)
            sp.wait_ge(s["loaded_b"], 48)

        @block.tensor
        def _(pe):
            for t in range(NT):
                for k in range(NK):
                    last = pe.matmul(m.ps[:, t, 0:WIDE], m.xT[:, k, t * P:(t + 1) * P], w[:, k, :],
                                     start=(k == 0), stop=(k == NK - 1))
                last.then_inc(projected, 1)
            pe.wait_ge(evicted, NT)
            for half in range(2):
                pe.wait_ge(roped, half + 1)
                for j in range(3):
                    for t in range(half * NT // 2, (half + 1) * NT // 2):
                        last = pe.transpose(banks(m, 2 * j)[:, t * P:(t + 1) * P], raw[:, t, j * P:(j + 1) * P],
                                            ident(m))
                    if half == 1:
                        last.then_inc(turned, 1)

        @block.scalar
        def _(act):
            st = Steps(act, s["act_step"])

            def inverse_root(half):
                act.wait_ge(summed, half + 1)
                st.settle(act.activation(root[:, part_of[half]], root[:, part_of[half]], ACT.Ln, bias=m.eps6[:],
                                         scale=1.0 / HD))
                act.activation(root[:, part_of[half]], root[:, part_of[half]], ACT.Exp, scale=-0.5).then_inc(rooted, 1)

            for t in range(NT):
                act.wait_ge(projected, t + 1)
                act.copy(raw[:, t, :], m.ps[:, t, 0:WIDE]).then_inc(evicted, 1)
                if t == NT // 2:
                    inverse_root(0)
                if t % (NT // 2) == NT // 2 - 1:
                    tiles = slice(t + 1 - NT // 2, t + 1)
                    act.wait_ge(evicted, t + 1)
                    act.activation(square[:, tiles, :], raw[:, tiles, 0:n_norm * HD], ACT.Square).then_inc(squared, 1)
            inverse_root(1)
            for j in range(2):
                act.wait_ge(turned, j + 1)
                for head in range(2):
                    rows = slice(64 * head, 64 * head + 64)
                    act.copy(q_pad[2 * j + head][rows, :], banks(m, 2 * j)[rows, :])
            act.wait_ge(turned, 3)
            act.copy(k2, banks(m, 4))

        @block.vector
        def _(dve):
            st = Steps(dve, s["dve_step"])
            dve.wait_ge(s["loaded_b"], 48)
            st.settle(dve.tensor_scalar(gain_q, gain_q, HD ** -0.5, None, ALU.mult))
            for half in range(2):
                tiles = slice(half * NT // 2, (half + 1) * NT // 2)
                n_tiles = NT // 2
                dve.wait_ge(squared, half + 1)
                dve.tensor_reduce(root[:, part_of[half]], square[:, tiles, :].rearrange("p t (h d) -> p (t h) d", d=HD),
                                  AX.X, ALU.add).then_inc(summed, 1)
                for twice in range(2):
                    dve.tensor_copy(v_tok[:, tiles, twice * HD:(twice + 1) * HD], raw[:, tiles, 5 * HD:6 * HD])
                dve.wait_ge(rooted, half + 1)
                spread_root = root[:, part_of[half]].rearrange("p (t h) -> p t h", t=n_tiles).unsqueeze(3).to_broadcast(
                    [P, n_tiles, n_norm, HD])
                st.settle(dve.tensor_tensor(heads[:, tiles], heads[:, tiles], spread_root, ALU.mult))
                for at, gain, n in ((slice(0, GROUP), gain_q, GROUP), (slice(GROUP, n_norm), gain_k, 1)):
                    last = dve.tensor_tensor(heads[:, tiles, at, :], heads[:, tiles, at, :],
                                             gain.unsqueeze(1).unsqueeze(1).to_broadcast([P, n_tiles, n, HD]), ALU.mult)
                st.settle(last)
                for axis in range(2):
                    x1 = heads[:, tiles, :, axis * 32:axis * 32 + 16]
                    x2 = heads[:, tiles, :, axis * 32 + 16:axis * 32 + 32]
                    cos, sin = (rope[:, tiles, f * 32 + axis * 16:f * 32 + axis * 16 + 16].unsqueeze(2).to_broadcast(
                        [P, n_tiles, n_norm, ROPE_HALF]) for f in range(2))
                    dve.tensor_tensor(part[0][:, tiles], x1, cos, ALU.mult)
                    dve.tensor_tensor(part[1][:, tiles], x2, sin, ALU.mult)
                    dve.tensor_tensor(part[2][:, tiles], x2, cos, ALU.mult)
                    st.settle(dve.tensor_tensor(part[3][:, tiles], x1, sin, ALU.mult))
                    dve.tensor_tensor(x1, part[0][:, tiles], part[1][:, tiles], ALU.subtract)
                    st.settle(dve.tensor_tensor(x2, part[2][:, tiles], part[3][:, tiles], ALU.add))
                dve.tensor_copy(raw[:, tiles, 5 * HD:6 * HD], raw[:, tiles, 4 * HD:5 * HD]).then_inc(roped, 1)
            for n in range(GROUP):
                other = 64 * (1 - n % 2)
                dve.memset(q_pad[n][other:other + 64, :], 0.0)
    end_stage(nc, m)
    steps = []
    for head in range(GROUP):
        rows = slice(64 * (head % 2), 64 * (head % 2) + 64)
        for t in range(NT):
            steps.append((q_pad[head][:, t * P:(t + 1) * P], k2, [v_tok[:, b, :] for b in range(NT)],
                          m.mixT[rows, g * 2 + head // 2, t * P:(t + 1) * P], rows, SEQ))
    with nc.Block() as block:
        @block.sync
        def _(sp):
            load_group_weights(sp, m, a, (g + 1) % KV_HEADS)
            sp.wait_ge(s["loaded_a"], 48)

        attention_steps(nc, m, block, steps, 1.0, None)
    end_stage(nc, m)


N_GROUPS, PER_GROUP, N_EXPERTS, D_EXPERT, TOP_K = 4, 8, 32, 512, 2
OVERFLOW = SEQ * TOP_K // P
N_BLOCKS = N_EXPERTS + OVERFLOW
MAX_MORE = NT - 1


def route_stage(nc, m, a, l):
    s = m.sem
    NL = N_GROUPS + N_EXPERTS
    base = 8 * SEQ
    at = [base]

    def take(*shape):
        n = int(np.prod(shape))
        view = m.work[:, at[0]:at[0] + n]
        at[0] += n
        if len(shape) == 2:
            view = view.rearrange("p (a b) -> p a b", b=shape[1])
        return view

    w, bias, logits = take(NK, NL), take(NL), take(NT, NL)
    padded, top_g, top_e, chosen, tmp8 = (take(NT, 8) for _ in range(5))
    index = take(NT, 8).bitcast(U32)
    g_id, e_loc, e_id, first, prob, e2, den = (take(NT, 2) for _ in range(7))
    onehot_g = take(NT, N_GROUPS)
    hot = [take(NT, N_EXPERTS) for _ in range(2)]
    both, rank, over_q, slot, tmp = (take(NT, N_EXPERTS) for _ in range(5))
    counts, more, ends, starts = (take(N_EXPERTS) for _ in range(4))
    compare = take(OVERFLOW, N_EXPERTS)
    ids = take(OVERFLOW)
    first_expert = expert_buffers(m)
    iota = m.const[:, K_IOTA:K_IOTA + N_EXPERTS]
    table_zero = take(N_BLOCKS).bitcast(I32)
    tokens = take(NT).bitcast(I32)
    summed, hot_ready, ranked, exp_in, exp_out, dest_ready, table_clear = (s[f"signal_{n}"] for n in range(7))
    with nc.Block() as block:
        @block.sync
        def _(sp):
            sp.dma_start(w[:, :, 0:N_GROUPS], a["moe_w_group_2"][l].rearrange("(k p) n -> p k n", p=P)).then_inc(
                s["loaded_a"], 16)
            sp.dma_start(w[:, :, N_GROUPS:NL], a["moe_w_expert_2"][l].rearrange("(k p) n -> p k n", p=P)).then_inc(
                s["loaded_a"], 16)
            sp.dma_start(bias[:, 0:N_GROUPS], a["moe_b_group_2"][l].partition_broadcast(P)).then_inc(s["loaded_b"], 16)
            sp.dma_start(bias[:, N_GROUPS:NL], a["moe_b_expert_2"][l].partition_broadcast(P)).then_inc(s["loaded_b"], 16)
            for dst, src in ((first_expert.gate[0], a["moe_w_gate_2"]), (first_expert.up[0], a["moe_w_up_2"])):
                sp.dma_start(dst, src[l, 0].rearrange("(k p) n -> p k n", p=P)).then_inc(s["loaded_d"], 16)
            sp.wait_ge(s["loaded_d"], 32)
            sp.wait_ge(s["loaded_b"], 32)
            sp.wait_ge(s["pool_step"], 1)
            sp.dma_start(m.slot_token.rearrange("(p b) o -> p (b o)", p=P), table_zero).then_inc(table_clear, 16)
            sp.wait_ge(table_clear, 16)
            sp.wait_ge(m.pool_dma[l]["scattered"], 16 * TOP_K * NT)
            sp.dma_start(m.slots[:], m.slot_token.rearrange("(p b) o -> p (b o)", p=P)).then_inc(s["loaded_c"], 16)
            sp.wait_ge(s["loaded_c"], 16)

        @block.tensor
        def _(pe):
            pe.wait_ge(s["loaded_a"], 32)
            for t in range(NT):
                for k in range(NK):
                    last = pe.matmul(m.ps[:, 0, t * NL:(t + 1) * NL], m.xT[:, k, t * P:(t + 1) * P], w[:, k, :],
                                     start=(k == 0), stop=(k == NK - 1))
            last.then_inc(summed, 1)
            pe.wait_ge(hot_ready, 1)
            for t in range(NT):
                out = m.ps[:, 1, t * N_EXPERTS:(t + 1) * N_EXPERTS]
                for b in range(t):
                    pe.matmul(out, ones(m), both[:, b, :], start=(b == 0), stop=False)
                pe.matmul(out, m.const[:, K_STRICT:K_STRICT + P], both[:, t, :], start=(t == 0), stop=True)
            for b in range(NT):
                last = pe.matmul(m.ps[:, 2, 0:N_EXPERTS], ones(m), both[:, b, :], start=(b == 0), stop=(b == NT - 1))
            last.then_inc(ranked, 1)

        @block.scalar
        def _(act):
            for n in range(2):
                act.wait_ge(exp_in, n + 1)
                dst = tmp8[:, :, 0:N_GROUPS] if n == 0 else e2[:, :, 0:1]
                act.activation(dst, dst, ACT.Exp).then_inc(exp_out, 1)

        @block.gpsimd
        def _(pool):
            pool.memset(table_zero, 0).then_inc(s["pool_step"], 1)
            pool.iota(tokens, pattern=[[P, NT]], base=0, channel_multiplier=1).then_inc(s["pool_step"], 1)
            pool.wait_ge(s["pool_step"], 2)
            pool.wait_ge(table_clear, 16)
            pool.wait_ge(dest_ready, 1)
            for t in range(NT):
                for c in range(TOP_K):
                    pool.indirect_dma_start(
                        m.slot_token, bass.IndirectOffsetOnAxis(m.dest[:, c, t:t + 1], 0),
                        tokens[:, t:t + 1], None).then_inc(m.pool_dma[l]["scattered"], 16)

        @block.vector
        def _(dve):
            st = Steps(dve, s["dve_step"])
            do = st.settle
            dve.wait_ge(s["loaded_b"], 32)
            do(dve.memset(padded, NEG))
            dve.wait_ge(summed, 1)
            do(dve.tensor_tensor(logits, m.ps[:, 0, 0:NT * NL].rearrange("p (t n) -> p t n", t=NT),
                                 each_chunk(bias), ALU.add))
            do(dve.tensor_copy(padded[:, :, 0:N_GROUPS], logits[:, :, 0:N_GROUPS]))
            for t in range(NT):
                do(dve.max(top_g[:, t, :], padded[:, t, :]))
                do(dve.max_index(index[:, t, :], top_g[:, t, :], padded[:, t, :]))
            dve.tensor_tensor(tmp8[:, :, 0:N_GROUPS], padded[:, :, 0:N_GROUPS],
                              top_g[:, :, 0:1].to_broadcast([P, NT, N_GROUPS]), ALU.subtract).then_inc(exp_in, 1)
            do(dve.tensor_copy(g_id[:, :, 0:1], index[:, :, 0:1]))
            do(dve.tensor_tensor(onehot_g, each_chunk(iota[:, 0:N_GROUPS]),
                                 g_id[:, :, 0:1].to_broadcast([P, NT, N_GROUPS]), ALU.is_equal))
            for g in range(N_GROUPS):
                part = logits[:, :, N_GROUPS + g * PER_GROUP:N_GROUPS + (g + 1) * PER_GROUP]
                mask = onehot_g[:, :, g:g + 1].to_broadcast([P, NT, PER_GROUP])
                if g == 0:
                    do(dve.tensor_tensor(chosen, part, mask, ALU.mult))
                else:
                    do(dve.tensor_tensor(top_e, part, mask, ALU.mult))
                    do(dve.tensor_tensor(chosen, chosen, top_e, ALU.add))
            for t in range(NT):
                do(dve.max(top_e[:, t, :], chosen[:, t, :]))
                do(dve.max_index(index[:, t, :], top_e[:, t, :], chosen[:, t, :]))
            do(dve.tensor_copy(e_loc, index[:, :, 0:2]))
            do(dve.scalar_tensor_tensor(e_id, g_id[:, :, 0:1].to_broadcast([P, NT, 2]), float(PER_GROUP), e_loc,
                                        ALU.mult, ALU.add))
            dve.tensor_tensor(e2[:, :, 0:1], top_e[:, :, 1:2], top_e[:, :, 0:1], ALU.subtract).then_inc(exp_in, 1)
            for c in range(TOP_K):
                last = dve.tensor_tensor(hot[c], each_chunk(iota), e_id[:, :, c:c + 1].to_broadcast(
                    [P, NT, N_EXPERTS]), ALU.is_equal)
            do(last)
            dve.tensor_tensor(both, hot[0], hot[1], ALU.add).then_inc(hot_ready, 1)
            dve.wait_ge(exp_out, 2)
            do(dve.tensor_reduce(prob[:, :, 0:1], tmp8[:, :, 0:N_GROUPS], AX.X, ALU.add))
            do(dve.tensor_scalar(den[:, :, 0:1], e2[:, :, 0:1], 1.0, None, ALU.add))
            do(dve.tensor_tensor(den[:, :, 0:1], den[:, :, 0:1], prob[:, :, 0:1], ALU.mult))
            do(dve.reciprocal(first[:, :, 0:1], den[:, :, 0:1]))
            dve.tensor_copy(m.gates[:, :, 0:1], first[:, :, 0:1])
            do(dve.tensor_tensor(m.gates[:, :, 1:2], first[:, :, 0:1], e2[:, :, 0:1], ALU.mult))
            dve.wait_ge(ranked, 1)
            do(dve.tensor_copy(counts, m.ps[:, 2, 0:N_EXPERTS]))
            do(dve.tensor_copy(rank, m.ps[:, 1, 0:NT * N_EXPERTS].rearrange("p (t n) -> p t n", t=NT)))
            do(dve.tensor_scalar(more, counts, float(P), None, ALU.is_gt))
            do(dve.tensor_scalar(over_q, rank, float(P), None, ALU.is_ge))
            for q in range(2, MAX_MORE + 1):
                do(dve.scalar_tensor_tensor(more, counts, float(P * q), more, ALU.is_gt, ALU.add))
                do(dve.scalar_tensor_tensor(over_q, rank, float(P * q), over_q, ALU.is_ge, ALU.add))
            do(dve.tensor_tensor_scan(ends, ones(m)[:, 0:N_EXPERTS], more, 0.0, ALU.mult, ALU.add))
            do(dve.tensor_tensor(starts, ends, more, ALU.subtract))
            do(dve.scalar_tensor_tensor(starts, starts, float(N_EXPERTS - 1), iota, ALU.add, ALU.subtract))
            do(dve.tensor_tensor(tmp, over_q, each_chunk(starts), ALU.add))
            do(dve.tensor_scalar(slot, over_q, 0.0, None, ALU.is_gt))
            do(dve.tensor_tensor(slot, slot, tmp, ALU.mult))
            do(dve.tensor_tensor(slot, slot, each_chunk(iota), ALU.add))
            do(dve.scalar_tensor_tensor(tmp, over_q, -float(P), rank, ALU.mult, ALU.add))
            do(dve.scalar_tensor_tensor(slot, tmp, float(N_BLOCKS), slot, ALU.mult, ALU.add))
            for c in range(TOP_K):
                do(dve.tensor_tensor(tmp, slot, hot[c], ALU.mult))
                do(dve.tensor_reduce(first[:, :, c:c + 1], tmp, AX.X, ALU.add))
                last = dve.tensor_copy(m.dest[:, c, :], first[:, :, c:c + 1].rearrange("p t o -> p (t o)"))
            do(last)
            do(dve.tensor_tensor(compare, ends.unsqueeze(1).to_broadcast([P, OVERFLOW, N_EXPERTS]),
                                 spread(m.const[:, K_IOTA:K_IOTA + OVERFLOW], N_EXPERTS), ALU.is_le))
            do(dve.tensor_reduce(ids, compare, AX.X, ALU.add))
            do(dve.tensor_scalar(ids, ids, float(N_EXPERTS - 1), None, ALU.min))
            dve.tensor_copy(m.overflow[:, 0:OVERFLOW], ids)
            do(dve.tensor_copy(m.overflow[:, OVERFLOW:OVERFLOW + 1], ends[:, N_EXPERTS - 1:N_EXPERTS]))
            dve.sem_inc(dest_ready, 1)
    end_stage(nc, m)


def expert_buffers(m):
    mix, xT, work = (t.rearrange("p a n -> p (a n)") for t in (m.mixT[:], m.xT[:], m.work[:].unsqueeze(1)))
    k8 = lambda v: v.rearrange("p (k n) -> p k n", n=D_EXPERT)
    k4 = lambda v: v.rearrange("p (k n) -> p k n", n=D)
    gate = [k8(work[:, 0:4096]), k8(mix[:, 0:4096])]
    up = [k8(work[:, 4096:8192]), k8(mix[:, 4096:8192])]
    down = [k4(work[:, 8192:12288]), k4(xT[:, 0:4096])]
    x = [xT[:, 4096:5120], xT[:, 5120:6144]]
    x_turned = [xT[:, 6144:7168], xT[:, 7168:8192]]
    act = [work[:, 12288 + n * 1024:12288 + n * 1024 + 512] for n in range(2)]
    act_turned = [work[:, 12800 + n * 1024:13312 + n * 1024] for n in range(2)]
    y = [work[:, 14336 + n * 1024:15360 + n * 1024] for n in range(2)]
    b = Places()
    b.gate, b.up, b.down, b.x, b.x_turned, b.act, b.act_turned, b.y = (
        gate, up, down, x, x_turned, act, act_turned, y)
    return b


def load_expert(sp, m, a, l, buffers, n, expert, semaphore):
    for dst, w, k in ((buffers.gate[n], a["moe_w_gate_2"], 8), (buffers.up[n], a["moe_w_up_2"], 8),
                      (buffers.down[n], a["moe_w_down_2"], 4)):
        sp.dma_start(dst, w[l, bass.ds(expert, 1)].rearrange("a (k p) n -> p (a k) n", p=P)).then_inc(semaphore, 16)


def gather_tokens(pool, m, buffers, n, column, copied, copied_count, gathered):
    pool.tensor_copy(m.index[:, n:n + 1], column).then_inc(copied, 1)
    pool.wait_ge(copied, copied_count)
    pool.indirect_dma_start(buffers.x[n], None, m.h_dram,
                            bass.IndirectOffsetOnAxis(m.index[:, n:n + 1], 0)).then_inc(gathered, 16)


def expert_engines(nc, m, block, b, n_blocks, loaded, gathered):
    s = m.sem
    x_turned, x_copied, up_ready, silued, multiplied, h_turned, h_copied, y_ready, y_copied = (
        s[f"signal_{n}"] for n in range(9))
    stored = (s["stored"], s["prefetched"])

    @block.tensor
    def _(pe):
        def turn_x(n):
            if gathered[n]:
                pe.wait_ge(*gathered[n])
            for k in range(NK):
                last = pe.transpose(banks(m, 0)[:, k * P:(k + 1) * P], b.x[n % 2][:, k * P:(k + 1) * P], ident(m))
            last.then_inc(x_turned, 1)

        def gate_up(n):
            if loaded[n]:
                pe.wait_ge(*loaded[n])
            pe.wait_ge(x_copied, 2 * (n + 1))
            if n:
                pe.wait_ge(multiplied, n)
            for w, bank in ((b.gate[n % 2], 2), (b.up[n % 2], 3)):
                for k in range(NK):
                    last = pe.matmul(m.ps[:, bank, :], b.x_turned[n % 2][:, k * P:(k + 1) * P], w[:, k, :],
                                     start=(k == 0), stop=(k == NK - 1))
                last.then_inc(up_ready, 1)

        def down(n):
            pe.wait_ge(multiplied, n + 1)
            for k in range(4):
                last = pe.transpose(m.ps[:, 4, k * P:(k + 1) * P], b.act[n % 2][:, k * P:(k + 1) * P], ident(m))
            last.then_inc(h_turned, 1)
            pe.wait_ge(h_copied, n + 1)
            if n:
                pe.wait_ge(y_copied, 2 * n)
            for half in range(2):
                for k in range(4):
                    last = pe.matmul(m.ps[:, 5 + half, :], b.act_turned[n % 2][:, k * P:(k + 1) * P],
                                     b.down[n % 2][:, k, half * HALF:(half + 1) * HALF],
                                     start=(k == 0), stop=(k == 3))
                last.then_inc(y_ready, 1)

        turn_x(0)
        gate_up(0)
        for n in range(n_blocks):
            if n + 1 < n_blocks:
                turn_x(n + 1)
            down(n)
            if n + 1 < n_blocks:
                gate_up(n + 1)

    @block.scalar
    def _(act):
        def copy_x(n):
            act.wait_ge(x_turned, n + 1)
            act.copy(b.x_turned[n % 2][:, 0:HALF], m.ps[:, 0, :]).then_inc(x_copied, 1)

        copy_x(0)
        for n in range(n_blocks):
            act.wait_ge(up_ready, 2 * n + 1)
            act.activation(b.act[n % 2], m.ps[:, 2, :], ACT.Silu).then_inc(silued, 1)
            if n + 1 < n_blocks:
                copy_x(n + 1)
            act.wait_ge(h_turned, n + 1)
            act.copy(b.act_turned[n % 2], m.ps[:, 4, :]).then_inc(h_copied, 1)
            act.wait_ge(y_ready, 2 * n + 2)
            if n >= 2:
                act.wait_ge(stored[n % 2], 16 * (n // 2))
            act.copy(b.y[n % 2][:, HALF:D], m.ps[:, 6, :]).then_inc(y_copied, 1)

    @block.vector
    def _(dve):
        def copy_x(n):
            dve.wait_ge(x_turned, n + 1)
            dve.tensor_copy(b.x_turned[n % 2][:, HALF:D], m.ps[:, 1, :]).then_inc(x_copied, 1)

        copy_x(0)
        for n in range(n_blocks):
            dve.wait_ge(up_ready, 2 * n + 2)
            dve.wait_ge(silued, n + 1)
            dve.tensor_tensor(b.act[n % 2], b.act[n % 2], m.ps[:, 3, :], ALU.mult).then_inc(multiplied, 1)
            if n + 1 < n_blocks:
                copy_x(n + 1)
            dve.wait_ge(y_ready, 2 * n + 1)
            if n >= 2:
                dve.wait_ge(stored[n % 2], 16 * (n // 2))
            dve.tensor_copy(b.y[n % 2][:, 0:HALF], m.ps[:, 5, :]).then_inc(y_copied, 1)


AT_ONCE = 8


def experts_stage(nc, m, a, l):
    s = m.sem
    b = expert_buffers(m)
    y_blocks = m.y_dram.rearrange("(p b) d -> p b d", p=P)
    x_turned, y_ready, y_copied, tokens_ready = s["signal_0"], s["signal_7"], s["signal_8"], s["signal_9"]
    gathered = (m.pool_dma[l]["gathered_a"], m.pool_dma[l]["gathered_b"])
    loads, stored = (s["loaded_a"], s["loaded_b"]), (s["stored"], s["prefetched"])
    with nc.Block() as block:
        @block.sync
        def _(sp):
            sp.dma_start(b.down[0], a["moe_w_down_2"][l, 0].rearrange("(k p) n -> p k n", p=P)).then_inc(
                s["loaded_a"], 16)
            sp.wait_ge(s["loaded_a"], 16)

        @block.gpsimd
        def _(pool):
            gather_tokens(pool, m, b, 0, m.slots[:, 0:1], s["pool_step"], 1, gathered[0])
            pool.wait_ge(gathered[0], 16)
    end_stage(nc, m)
    with nc.Fori(0, N_EXPERTS // AT_ONCE) as turn:
        first = turn * AT_ONCE

        def expert(n):
            return first + n if n < AT_ONCE else (first + n) % N_EXPERTS

        with nc.Block() as block:
            @block.sync
            def _(sp):
                for n in range(AT_ONCE):
                    if n:
                        sp.wait_ge(y_ready, 2 * n)
                    load_expert(sp, m, a, l, b, (n + 1) % 2, expert(n + 1), loads[(n + 1) % 2])
                    if n:
                        sp.wait_ge(y_copied, 2 * n)
                        sp.dma_start(y_blocks[:, bass.ds(expert(n - 1), 1), :],
                                     b.y[(n - 1) % 2].unsqueeze(1)).then_inc(stored[(n - 1) % 2], 16)
                sp.wait_ge(y_copied, 2 * AT_ONCE)
                sp.dma_start(y_blocks[:, bass.ds(expert(AT_ONCE - 1), 1), :],
                             b.y[(AT_ONCE - 1) % 2].unsqueeze(1)).then_inc(stored[(AT_ONCE - 1) % 2], 16)
                for n in range(2):
                    sp.wait_ge(loads[n], 48 * (AT_ONCE // 2))
                    sp.wait_ge(stored[n], 16 * (AT_ONCE // 2))

            @block.gpsimd
            def _(pool):
                for n in range(AT_ONCE):
                    if n:
                        pool.wait_ge(x_turned, n)
                    gather_tokens(pool, m, b, (n + 1) % 2, m.slots[:, bass.ds(expert(n + 1), 1)], s["pool_step"],
                                  n + 1, gathered[(n + 1) % 2])
                    earlier = turn * (AT_ONCE // 2)
                    pool.wait_ge(gathered[(n + 1) % 2], (earlier + (n // 2 + 1 + n % 2)) * 16)
                    pool.sem_inc(tokens_ready, 1)

            expert_engines(nc, m, block, b, AT_ONCE,
                           [None] + [(loads[n % 2], 48 * ((n + 1) // 2)) for n in range(1, AT_ONCE)],
                           [None] + [(tokens_ready, n) for n in range(1, AT_ONCE)])
        end_stage(nc, m)
    overflow_blocks = nc.values_load(m.overflow[0:1, OVERFLOW:OVERFLOW + 1], min_val=0, max_val=OVERFLOW)
    with nc.Fori(0, OVERFLOW) as o:
        with nc.If(overflow_blocks > o):
            with nc.Block() as block:
                @block.sync
                def _(sp):
                    expert = sp.value_load(m.overflow[0:1, bass.ds(o, 1)], min_val=0, max_val=N_EXPERTS - 1)
                    load_expert(sp, m, a, l, b, 0, expert, s["loaded_a"])
                    sp.wait_ge(y_copied, 2)
                    sp.dma_start(y_blocks[:, bass.ds(o + N_EXPERTS, 1), :], b.y[0].unsqueeze(1)).then_inc(s["stored"], 16)
                    sp.wait_ge(s["loaded_a"], 48)
                    sp.wait_ge(s["stored"], 16)

                @block.gpsimd
                def _(pool):
                    gather_tokens(pool, m, b, 0, m.slots[:, bass.ds(o + N_EXPERTS, 1)], s["pool_step"], 1,
                                  m.pool_dma[l]["gathered_more"])
                    pool.wait_ge(m.pool_dma[l]["gathered_more"], (o + 1) * 16)
                    pool.sem_inc(tokens_ready, 1)

                expert_engines(nc, m, block, b, 1, [(s["loaded_a"], 48)], [(tokens_ready, 1)])
            end_stage(nc, m)


def combine_stage(nc, m, l):
    s = m.sem
    y = [[m.work[:, (13 + 2 * n + c) * SEQ:(14 + 2 * n + c) * SEQ] for c in range(2)] for n in range(2)]
    weighted = s["signal_0"]
    done = [m.pool_dma[l]["combined_a"], m.pool_dma[l]["combined_b"]]
    with nc.Block() as block:
        @block.gpsimd
        def _(pool):
            for t in range(NT):
                if t >= 2:
                    pool.wait_ge(weighted, t - 1)
                for c in range(TOP_K):
                    pool.indirect_dma_start(y[t % 2][c], None, m.y_dram, bass.IndirectOffsetOnAxis(
                        m.dest[:, c, t:t + 1], 0)).then_inc(done[t % 2], 16)

        @block.vector
        def _(dve):
            st = Steps(dve, s["dve_step"])
            for t in range(NT):
                dve.wait_ge(done[t % 2], 32 * (t // 2 + 1))
                st.settle(dve.tensor_scalar(m.mixT[:, t, :], y[t % 2][0], m.gates[:, t, 0:1], None, ALU.mult))
                dve.scalar_tensor_tensor(m.mixT[:, t, :], y[t % 2][1], m.gates[:, t, 1:2], m.mixT[:, t, :],
                                         ALU.mult, ALU.add).then_inc(weighted, 1)
    end_stage(nc, m)


def program(nc, a, out):
    m = make_memory(nc)
    more_memory(nc, m)
    load_inputs_stage(nc, m, a["x"], a["constants"])
    constants_stage(nc, m)
    modulation_stage(nc, m, a)
    for l in range(DEPTH):
        transpose_stage(nc, m, m.x_tok, m.xT)
        hybrid_small_stage(nc, m, l, a)
        first_delta_weights_stage(nc, m, a, l)
        with nc.Fori(0, DN_HEADS) as h:
            delta_head(nc, m, l, a, h)
        with nc.Fori(0, GLA_HEADS // 2) as pair:
            gla_pair(nc, m, l, a, pair)
        out_stage(nc, m, a["w_out"][l], a["ln_g"][l], a["ln_b"][l], m.eps6,
                  background=(lambda sp: relative_bias(sp, m, a)) if l == 0 else (lambda sp: clear_overflow(sp, m)))
    second_block(nc, m, a)
    with nc.Block() as block:
        @block.sync
        def _(sp):
            sp.dma_start(out[0].rearrange("(t p) d -> p t d", p=P), m.x_tok[:]).then_inc(m.sem["stored"], 16)
            sp.wait_ge(m.sem["stored"], 16)


def second_block(nc, m, a, layers=range(DEPTH)):
    for l in layers:
        mod = [m.mods[l, n * D:(n + 1) * D] for n in range(6)]
        h = modulate_stage(nc, m, mod[0], mod[1])
        transpose_stage(nc, m, h, m.xT)
        first_weights_stage(nc, m, a, load_neighbourhood_weights if l % 2 == 0 else load_group_weights)
        if l % 2 == 0:
            with nc.Fori(0, D // P) as pair:
                neighbourhood_pair(nc, m, a, pair)
        else:
            with nc.Fori(0, KV_HEADS) as g:
                grouped_query_group(nc, m, a, g)
        w_o = a["na_w_o_2"][0] if l % 2 == 0 else a["gqa_w_o_2"][0]
        out_stage(nc, m, w_o, a["ln_g_2"][l, 0], a["ln_b_2"][l, 0], m.eps5, mod[2])
        h = modulate_stage(nc, m, mod[3], mod[4], m.h_dram)
        transpose_stage(nc, m, h, m.xT)
        route_stage(nc, m, a, l)
        experts_stage(nc, m, a, l)
        combine_stage(nc, m, l)
        out_stage(nc, m, None, a["ln_g_2"][l, 1], a["ln_b_2"][l, 1], m.eps5, mod[5])


INPUTS = ["x", "w_in", "conv_w", "dn_a_log", "dn_dt_bias", "gla_gate_w2", "gla_gate_b", "dn_norm_g", "gla_norm_g",
          "w_out", "ln_g", "ln_b", "c_2", "ada_w_2", "ada_b_2", "ln_g_2", "ln_b_2", "na_w_qkv_2", "na_rpb_2",
          "na_w_o_2", "gqa_w_qkv_2", "gqa_q_norm_2", "gqa_k_norm_2", "gqa_w_o_2", "moe_w_group_2", "moe_b_group_2",
          "moe_w_expert_2", "moe_b_expert_2", "moe_w_gate_2", "moe_w_up_2", "moe_w_down_2"]


def kernel(**inputs):
    import concourse.bacc as bacc
    from concourse.bass_utils import run_bass_kernel_spmd

    nc = bacc.Bacc("TRN2", target_bir_lowering=False, num_devices=1)
    arrays = {name: np.ascontiguousarray(inputs[name]) for name in INPUTS}
    arrays["constants"] = shape_constants()
    arrays["rope"] = rope_table()
    a = {name: nc.dram_tensor(name, v.shape, mybir.dt.from_np(v.dtype), kind="ExternalInput").ap()
         for name, v in arrays.items()}
    out = nc.dram_tensor("out", (1, SEQ, D), F32, kind="ExternalOutput").ap()
    program(nc, a, out)
    result = run_bass_kernel_spmd(nc, [arrays], core_ids=[0])
    return result.results[0]["out"]
```
